# Optimizing a Trainium2 kernel written in Bass

```python
import math
import jax, jax.numpy as jnp
from jax import lax
import numpy as np

D_MODEL = 1024
BATCH = 1
SEQ = 512
DEPTH = 2

N_META = 16
POOL_WIDTH = D_MODEL // 2
POOL_WINDOWS = (2, 4, 8, 16)
POOL_GROUPS = len(POOL_WINDOWS)
POOL_GROUP_DIM = POOL_WIDTH // POOL_GROUPS
N_HEADS = 8
QK_NOPE_DIM = 64
QK_ROPE_DIM = 32
QK_HEAD_DIM = QK_NOPE_DIM + QK_ROPE_DIM
V_HEAD_DIM = 64
MLA_WIDTH = N_HEADS * V_HEAD_DIM
KV_LORA_RANK = 256
Q_LORA_RANK = 768
ROPE_THETA = 10000.0
NORM_EPS = 1e-6
Q_BLOCK = 128
MASK_VALUE = -1e30

IN_SPLITS = (POOL_WIDTH, POOL_WIDTH, Q_LORA_RANK, KV_LORA_RANK, QK_ROPE_DIM, MLA_WIDTH, D_MODEL, D_MODEL)
D_IN = sum(IN_SPLITS)
IN_SPLIT_POINTS = tuple(int(v) for v in np.cumsum(IN_SPLITS)[:-1])


def rmsnorm(x, gain):
    xf = x.astype(jnp.float32)
    inv = lax.rsqrt(jnp.mean(xf * xf, axis=-1, keepdims=True) + NORM_EPS)
    return (xf * inv * gain.astype(jnp.float32)).astype(x.dtype)

def apply_rope(x, pos):
    half = x.shape[-1] // 2
    inv_freq = ROPE_THETA ** (-jnp.arange(half, dtype=jnp.float32) / half)
    ang = pos.astype(jnp.float32)[..., None] * inv_freq
    cos = jnp.cos(ang)[:, :, None, :]
    sin = jnp.sin(ang)[:, :, None, :]
    xf = x.astype(jnp.float32)
    x1, x2 = xf[..., :half], xf[..., half:]
    return jnp.concatenate([x1 * cos - x2 * sin, x2 * cos + x1 * sin], axis=-1).astype(x.dtype)

def pool_mix(u, w_group, scale):
    B, L, _ = u.shape
    ug = u.reshape(B, L, POOL_GROUPS, POOL_GROUP_DIM).astype(jnp.float32)
    csum = jnp.cumsum(ug, axis=1)
    t1 = jnp.arange(1, L + 1, dtype=jnp.float32)
    means = []
    for g, w in enumerate(POOL_WINDOWS):
        s = csum[:, :, g]
        lag = jnp.pad(s, ((0, 0), (w, 0), (0, 0)))[:, :L]
        cnt = jnp.minimum(t1, float(w))[None, :, None]
        means.append((s - lag) / cnt)
    mixed = (jnp.stack(means, axis=2) - ug).astype(u.dtype)
    y = jnp.einsum('blgc,gcd->blgd', mixed, w_group)
    return y.reshape(B, L, POOL_WIDTH) * scale

def causal_block_attention(q, k, v):
    B, L = q.shape[0], q.shape[1]
    pad_front = (-N_META) % Q_BLOCK
    pad_back = (-(L + pad_front)) % Q_BLOCK
    padw = ((0, 0), (pad_front, pad_back), (0, 0), (0, 0))
    q, k, v = jnp.pad(q, padw), jnp.pad(k, padw), jnp.pad(v, padw)
    n_blocks = q.shape[1] // Q_BLOCK
    scale = 1.0 / math.sqrt(QK_HEAD_DIM)
    outs = []
    for i in range(n_blocks):
        q0 = i * Q_BLOCK
        kend = q0 + Q_BLOCK
        s = jnp.einsum('bqhd,bkhd->bhqk', q[:, q0:kend], k[:, :kend]).astype(jnp.float32) * scale
        qi = jnp.arange(q0, kend)[:, None]
        ki = jnp.arange(kend)[None, :]
        valid = (ki <= qi) & (ki >= pad_front)
        s = jnp.where(valid, s, MASK_VALUE)
        p = jax.nn.softmax(s, axis=-1).astype(v.dtype)
        outs.append(jnp.einsum('bhqk,bkhd->bqhd', p, v[:, :kend]))
    o = jnp.concatenate(outs, axis=1)
    return o[:, pad_front:pad_front + L]

def mla(c_q_raw, c_kv_raw, k_rope_raw, pos, g_qa, g_kva, w_q_b, w_kv_b, g_qn, g_kn):
    B, L, _ = c_q_raw.shape
    c_q = rmsnorm(c_q_raw, g_qa)
    c_kv = rmsnorm(c_kv_raw, g_kva)
    q = (c_q @ w_q_b).reshape(B, L, N_HEADS, QK_HEAD_DIM)
    kv = (c_kv @ w_kv_b).reshape(B, L, N_HEADS, QK_NOPE_DIM + V_HEAD_DIM)
    k_nope, v = kv[..., :QK_NOPE_DIM], kv[..., QK_NOPE_DIM:]
    k_pe = jnp.broadcast_to(k_rope_raw[:, :, None, :], (B, L, N_HEADS, QK_ROPE_DIM))
    k = jnp.concatenate([k_nope, k_pe], axis=-1)
    q = rmsnorm(q, g_qn)
    k = rmsnorm(k, g_kn)
    q = jnp.concatenate([q[..., :QK_NOPE_DIM], apply_rope(q[..., QK_NOPE_DIM:], pos)], axis=-1)
    k = jnp.concatenate([k[..., :QK_NOPE_DIM], apply_rope(k[..., QK_NOPE_DIM:], pos)], axis=-1)
    o = causal_block_attention(q, k, v)
    return o.reshape(B, L, MLA_WIDTH)

def first_inputs(seed: int = 0) -> dict:
    key = jax.random.key(seed)
    ks = jax.random.split(key, 18)
    f32 = jnp.float32

    def nrm(k, shape, scale):
        return jax.random.normal(k, shape, f32) * scale

    def gain(k, shape):
        return 1.0 + 0.02 * jax.random.normal(k, shape, f32)

    x = jax.random.normal(ks[0], (BATCH, SEQ, D_MODEL), f32)
    offset = jax.random.randint(ks[1], (BATCH, 1), 0, 4096, dtype=jnp.int32)
    positions = offset + jnp.arange(SEQ, dtype=jnp.int32)[None, :]
    return {
        "x": x,
        "positions": positions,
        "meta_tokens": nrm(ks[2], (N_META, D_MODEL), 1.0),
        "norm_gain": gain(ks[3], (DEPTH, D_MODEL)),
        "w_in": nrm(ks[4], (DEPTH, D_MODEL, D_IN), D_MODEL ** -0.5),
        "pool_w_group": nrm(ks[5], (DEPTH, POOL_GROUPS, POOL_GROUP_DIM, POOL_GROUP_DIM), POOL_GROUP_DIM ** -0.5),
        "pool_scale": gain(ks[6], (DEPTH, POOL_WIDTH)),
        "pool_w_up": nrm(ks[7], (DEPTH, POOL_WIDTH, D_MODEL), POOL_WIDTH ** -0.5),
        "q_a_norm_gain": gain(ks[8], (DEPTH, Q_LORA_RANK)),
        "kv_a_norm_gain": gain(ks[9], (DEPTH, KV_LORA_RANK)),
        "w_q_b": nrm(ks[10], (DEPTH, Q_LORA_RANK, N_HEADS * QK_HEAD_DIM), Q_LORA_RANK ** -0.5),
        "w_kv_b": nrm(ks[11], (DEPTH, KV_LORA_RANK, N_HEADS * (QK_NOPE_DIM + V_HEAD_DIM)), KV_LORA_RANK ** -0.5),
        "q_norm_gain": gain(ks[12], (DEPTH, QK_HEAD_DIM)),
        "k_norm_gain": gain(ks[13], (DEPTH, QK_HEAD_DIM)),
        "mla_w_up": nrm(ks[14], (DEPTH, MLA_WIDTH, D_MODEL), MLA_WIDTH ** -0.5),
        "w_out": nrm(ks[15], (DEPTH, D_MODEL, D_MODEL), (D_MODEL * 2 * DEPTH) ** -0.5),
    }

def first_block(x, positions, meta_tokens, norm_gain, w_in, pool_w_group, pool_scale, pool_w_up,
              q_a_norm_gain, kv_a_norm_gain, w_q_b, w_kv_b, q_norm_gain, k_norm_gain, mla_w_up, w_out):
    B = x.shape[0]
    meta = jnp.broadcast_to(meta_tokens[None].astype(x.dtype), (B, N_META, D_MODEL))
    h_res = jnp.concatenate([meta, x], axis=1)
    meta_pos = jnp.broadcast_to(jnp.arange(N_META, dtype=jnp.int32)[None], (B, N_META))
    pos = jnp.concatenate([meta_pos, positions + N_META], axis=1)

    for l in range(DEPTH):
        h = rmsnorm(h_res, norm_gain[l])
        proj = h @ w_in[l]
        u_pool, z_pool, c_q, c_kv, k_rope, z_mla, g_pool, g_mla = jnp.split(proj, IN_SPLIT_POINTS, axis=-1)
        y_pool = (pool_mix(u_pool, pool_w_group[l], pool_scale[l]) * jax.nn.silu(z_pool)) @ pool_w_up[l]
        o_mla = mla(c_q, c_kv, k_rope, pos, q_a_norm_gain[l], kv_a_norm_gain[l], w_q_b[l], w_kv_b[l],
                    q_norm_gain[l], k_norm_gain[l])
        y_mla = (o_mla * jax.nn.silu(z_mla)) @ mla_w_up[l]
        merged = jax.nn.sigmoid(g_pool) * y_pool + jax.nn.sigmoid(g_mla) * y_mla
        h_res = h_res + merged @ w_out[l]

    return h_res[:, N_META:]


DEPTH_2 = 1

N_ATTN_HEADS = 8
SUB_HEAD_DIM = 64
V_HEAD_DIM_2 = 2 * SUB_HEAD_DIM
ATTN_WIDTH = N_ATTN_HEADS * V_HEAD_DIM_2
LAMBDA_BASE = 0.8
LAMBDA_AMP = 0.6
LAMBDA_RATE = 0.3

LRU_WIDTH = 1024
LRU_BLOCKS = 8
LRU_BLOCK_DIM = LRU_WIDTH // LRU_BLOCKS
CONV_WIDTH = 4
CONV_PAD_LEFT = (CONV_WIDTH - 1) // 2
CONV_PAD_RIGHT = CONV_WIDTH - 1 - CONV_PAD_LEFT
LRU_C = 8.0
N_DIRECTIONS = 2

N_GATED_BRANCHES = 2
PROJ_WIDTH = 3 * ATTN_WIDTH + 2 * LRU_WIDTH + N_GATED_BRANCHES * D_MODEL
SPLIT_POINTS = (ATTN_WIDTH, 2 * ATTN_WIDTH, 3 * ATTN_WIDTH,
                3 * ATTN_WIDTH + LRU_WIDTH, 3 * ATTN_WIDTH + 2 * LRU_WIDTH)

N_GROUPS = 4
EXPERTS_PER_GROUP = 4
N_EXPERTS = N_GROUPS * EXPERTS_PER_GROUP
TOP_K_IN_GROUP = 2
EXPERT_HIDDEN = 512
TOKEN_BLOCK = 128

RMS_EPS = 1e-6


def rms_norm(x, gain):
    xf = x.astype(jnp.float32)
    y = xf * lax.rsqrt(jnp.mean(xf * xf, axis=-1, keepdims=True) + RMS_EPS)
    return (y * gain.astype(jnp.float32)).astype(x.dtype)

def lambda_init_fn(layer_idx):
    return LAMBDA_BASE - LAMBDA_AMP * math.exp(-LAMBDA_RATE * layer_idx)

def rope_tables(seq, dim):
    pos = jnp.arange(seq, dtype=jnp.float32)
    inv_freq = ROPE_THETA ** (-jnp.arange(0, dim, 2, dtype=jnp.float32) / dim)
    ang = pos[:, None] * inv_freq[None, :]
    return jnp.cos(ang), jnp.sin(ang)

def apply_rope_2(x, cos, sin):
    xf = x.astype(jnp.float32)
    x1, x2 = jnp.split(xf, 2, axis=-1)
    c = cos[None, :, None, None, :]
    s = sin[None, :, None, None, :]
    return jnp.concatenate([x1 * c - x2 * s, x1 * s + x2 * c], axis=-1).astype(x.dtype)

def diff_attention(q, k, v, lam):
    B, S, H, _, dh = q.shape
    scale = dh ** -0.5
    n_blk = S // Q_BLOCK
    qb = q.reshape(B, n_blk, Q_BLOCK, H, 2, dh).transpose(1, 0, 2, 3, 4, 5)

    def one_block(q_blk):
        s = jnp.einsum('bqhcd,bkhcd->bhcqk', q_blk, k,
                       preferred_element_type=jnp.float32) * scale
        p = jax.nn.softmax(s, axis=-1)
        p_diff = p[:, :, 0] - lam * p[:, :, 1]
        return jnp.einsum('bhqk,bkhd->bqhd', p_diff.astype(v.dtype), v)

    out = lax.map(one_block, qb)
    return out.transpose(1, 0, 2, 3, 4).reshape(B, S, H, v.shape[-1])

def centred_depthwise_conv(x, w, b):
    y = lax.conv_general_dilated(
        x, w[:, None, :], window_strides=(1,),
        padding=[(CONV_PAD_LEFT, CONV_PAD_RIGHT)],
        dimension_numbers=('NWC', 'WIO', 'NWC'),
        feature_group_count=x.shape[-1])
    return y + b

def block_diag_linear(x, w, b):
    B, S, C = x.shape
    xb = x.reshape(B, S, LRU_BLOCKS, LRU_BLOCK_DIM)
    y = jnp.einsum('bsnd,nde->bsne', xb, w)
    return y.reshape(B, S, C) + b

def rg_lru(x, w_a, b_a, w_i, b_i, lam_param, reverse):
    r = jax.nn.sigmoid(block_diag_linear(x, w_a, b_a).astype(jnp.float32))
    i = jax.nn.sigmoid(block_diag_linear(x, w_i, b_i).astype(jnp.float32))
    log_a = -LRU_C * r * jax.nn.softplus(-lam_param.astype(jnp.float32))
    a = jnp.exp(log_a)
    mult = jnp.sqrt(-jnp.expm1(2.0 * log_a))
    u = mult * (i * x.astype(jnp.float32))

    def combine(c1, c2):
        a1, b1 = c1
        a2, b2 = c2
        return a1 * a2, a2 * b1 + b2

    _, h = lax.associative_scan(combine, (a, u), axis=1, reverse=reverse)
    return h.astype(x.dtype)

def hierarchical_moe(h, w_group, b_group, w_er, b_er, w_gate, w_up, w_down):
    B, S, D = h.shape
    N = B * S
    xt = h.reshape(N, D)
    g_logits = (xt @ w_group + b_group).astype(jnp.float32)
    g_prob = jax.nn.softmax(g_logits, axis=-1)
    g_sel = jnp.argmax(g_logits, axis=-1)
    g_w = jnp.take_along_axis(g_prob, g_sel[:, None], axis=-1)
    e_logits = (xt @ w_er + b_er).astype(jnp.float32).reshape(N, N_GROUPS, EXPERTS_PER_GROUP)
    e_sel_logits = jnp.take_along_axis(e_logits, g_sel[:, None, None], axis=1)[:, 0]
    top_val, top_idx = lax.top_k(e_sel_logits, TOP_K_IN_GROUP)
    top_w = jax.nn.softmax(top_val, axis=-1) * g_w
    expert_id = g_sel[:, None] * EXPERTS_PER_GROUP + top_idx
    combine_w = jnp.sum(jax.nn.one_hot(expert_id, N_EXPERTS, dtype=jnp.float32)
                        * top_w[..., None], axis=1)

    n_blk = S // TOKEN_BLOCK
    xb = h.reshape(B, n_blk, TOKEN_BLOCK, D).transpose(1, 0, 2, 3).reshape(n_blk, B * TOKEN_BLOCK, D)
    cb = combine_w.reshape(B, n_blk, TOKEN_BLOCK, N_EXPERTS).transpose(1, 0, 2, 3)
    cb = cb.reshape(n_blk, B * TOKEN_BLOCK, N_EXPERTS).astype(h.dtype)

    def expert_block(args):
        xs, cs = args
        a = jnp.einsum('nd,edf->nef', xs, w_gate)
        u = jnp.einsum('nd,edf->nef', xs, w_up)
        hid = jax.nn.silu(a) * u * cs[:, :, None]
        return jnp.einsum('nef,efd->nd', hid, w_down)

    y = lax.map(expert_block, (xb, cb))
    y = y.reshape(n_blk, B, TOKEN_BLOCK, D).transpose(1, 0, 2, 3)
    return y.reshape(B, S, D)

def second_inputs(seed: int = 0) -> dict:
    key = jax.random.key(seed)
    ks = jax.random.split(key, 32)
    f32 = jnp.float32
    nrm = lambda k, shape, scale: jax.random.normal(k, shape, f32) * scale
    gain = lambda k, shape: jnp.ones(shape, f32) + 0.02 * jax.random.normal(k, shape, f32)

    a_c = jax.random.uniform(ks[16], (DEPTH_2, N_DIRECTIONS, LRU_WIDTH), f32, 0.9, 0.999)
    a_base = a_c ** (1.0 / LRU_C)
    lru_lambda = jnp.log(a_base) - jnp.log1p(-a_base)

    return {
        "x": jax.random.normal(ks[0], (BATCH, SEQ, D_MODEL), f32),
        "norm1_gain": gain(ks[1], (DEPTH_2, D_MODEL)),
        "w_in": nrm(ks[2], (DEPTH_2, D_MODEL, PROJ_WIDTH), D_MODEL ** -0.5),
        "b_gates": nrm(ks[3], (DEPTH_2, N_GATED_BRANCHES * D_MODEL), 0.02),
        "q_norm_gain": gain(ks[4], (DEPTH_2, SUB_HEAD_DIM)),
        "k_norm_gain": gain(ks[5], (DEPTH_2, SUB_HEAD_DIM)),
        "lambda_q1": nrm(ks[6], (DEPTH_2, SUB_HEAD_DIM), 0.1),
        "lambda_k1": nrm(ks[7], (DEPTH_2, SUB_HEAD_DIM), 0.1),
        "lambda_q2": nrm(ks[8], (DEPTH_2, SUB_HEAD_DIM), 0.1),
        "lambda_k2": nrm(ks[9], (DEPTH_2, SUB_HEAD_DIM), 0.1),
        "attn_subln_gain": gain(ks[10], (DEPTH_2, V_HEAD_DIM_2)),
        "w_attn_o": nrm(ks[11], (DEPTH_2, ATTN_WIDTH, D_MODEL), ATTN_WIDTH ** -0.5),
        "conv_w": nrm(ks[12], (DEPTH_2, CONV_WIDTH, LRU_WIDTH), CONV_WIDTH ** -0.5),
        "conv_b": nrm(ks[13], (DEPTH_2, LRU_WIDTH), 0.02),
        "lru_wa": nrm(ks[14], (DEPTH_2, N_DIRECTIONS, LRU_BLOCKS, LRU_BLOCK_DIM, LRU_BLOCK_DIM), LRU_BLOCK_DIM ** -0.5),
        "lru_ba": nrm(ks[15], (DEPTH_2, N_DIRECTIONS, LRU_WIDTH), 0.02),
        "lru_wi": nrm(ks[17], (DEPTH_2, N_DIRECTIONS, LRU_BLOCKS, LRU_BLOCK_DIM, LRU_BLOCK_DIM), LRU_BLOCK_DIM ** -0.5),
        "lru_bi": nrm(ks[18], (DEPTH_2, N_DIRECTIONS, LRU_WIDTH), 0.02),
        "lru_lambda": lru_lambda,
        "w_lru_o": nrm(ks[19], (DEPTH_2, LRU_WIDTH, D_MODEL), LRU_WIDTH ** -0.5),
        "w_out": nrm(ks[20], (DEPTH_2, D_MODEL, D_MODEL), D_MODEL ** -0.5),
        "norm2_gain": gain(ks[21], (DEPTH_2, D_MODEL)),
        "w_group_router": nrm(ks[22], (DEPTH_2, D_MODEL, N_GROUPS), D_MODEL ** -0.5),
        "b_group_router": nrm(ks[23], (DEPTH_2, N_GROUPS), 0.01),
        "w_expert_router": nrm(ks[24], (DEPTH_2, D_MODEL, N_EXPERTS), D_MODEL ** -0.5),
        "b_expert_router": nrm(ks[25], (DEPTH_2, N_EXPERTS), 0.01),
        "w_expert_gate": nrm(ks[26], (DEPTH_2, N_EXPERTS, D_MODEL, EXPERT_HIDDEN), D_MODEL ** -0.5),
        "w_expert_up": nrm(ks[27], (DEPTH_2, N_EXPERTS, D_MODEL, EXPERT_HIDDEN), D_MODEL ** -0.5),
        "w_expert_down": nrm(ks[28], (DEPTH_2, N_EXPERTS, EXPERT_HIDDEN, D_MODEL), EXPERT_HIDDEN ** -0.5),
    }

def second_block(x, norm1_gain, w_in, b_gates, q_norm_gain, k_norm_gain,
              lambda_q1, lambda_k1, lambda_q2, lambda_k2, attn_subln_gain, w_attn_o,
              conv_w, conv_b, lru_wa, lru_ba, lru_wi, lru_bi, lru_lambda, w_lru_o,
              w_out, norm2_gain, w_group_router, b_group_router,
              w_expert_router, b_expert_router, w_expert_gate, w_expert_up, w_expert_down):
    B, S, D = x.shape
    cos, sin = rope_tables(S, SUB_HEAD_DIM)
    for l in range(DEPTH_2):
        lam_init = lambda_init_fn(l)
        h = rms_norm(x, norm1_gain[l])
        proj = jnp.einsum('bsd,dc->bsc', h, w_in[l])
        q, k, v, lru_x, lru_g, gate_pre = jnp.split(proj, SPLIT_POINTS, axis=-1)

        q = q.reshape(B, S, N_ATTN_HEADS, 2, SUB_HEAD_DIM)
        k = k.reshape(B, S, N_ATTN_HEADS, 2, SUB_HEAD_DIM)
        v = v.reshape(B, S, N_ATTN_HEADS, V_HEAD_DIM_2)
        q = apply_rope_2(rms_norm(q, q_norm_gain[l]), cos, sin)
        k = apply_rope_2(rms_norm(k, k_norm_gain[l]), cos, sin)
        lam = (jnp.exp(jnp.sum(lambda_q1[l].astype(jnp.float32) * lambda_k1[l].astype(jnp.float32)))
               - jnp.exp(jnp.sum(lambda_q2[l].astype(jnp.float32) * lambda_k2[l].astype(jnp.float32)))
               + lam_init)
        o = diff_attention(q, k, v, lam)
        o = rms_norm(o, attn_subln_gain[l]) * (1.0 - lam_init)
        attn_d = jnp.einsum('bsc,cd->bsd', o.reshape(B, S, ATTN_WIDTH), w_attn_o[l])

        xr = centred_depthwise_conv(lru_x, conv_w[l], conv_b[l])
        h_fwd = rg_lru(xr, lru_wa[l, 0], lru_ba[l, 0], lru_wi[l, 0], lru_bi[l, 0], lru_lambda[l, 0], False)
        h_bwd = rg_lru(xr, lru_wa[l, 1], lru_ba[l, 1], lru_wi[l, 1], lru_bi[l, 1], lru_lambda[l, 1], True)
        y_lru = (h_fwd + h_bwd) * jax.nn.gelu(lru_g)
        lru_d = jnp.einsum('bsc,cd->bsd', y_lru, w_lru_o[l])

        g_attn, g_lru = jnp.split(jax.nn.sigmoid(gate_pre + b_gates[l]), N_GATED_BRANCHES, axis=-1)
        merged = g_attn * attn_d + g_lru * lru_d
        x = x + jnp.einsum('bsd,de->bse', merged, w_out[l])

        h2 = rms_norm(x, norm2_gain[l])
        x = x + hierarchical_moe(h2, w_group_router[l], b_group_router[l],
                                 w_expert_router[l], b_expert_router[l],
                                 w_expert_gate[l], w_expert_up[l], w_expert_down[l])
    return x


def setup_inputs(seed=0):
    out = dict(first_inputs(seed))
    for name, value in second_inputs(seed + 1).items():
        if name != "x":
            out[name + "_2"] = value
    return out


def reference(
    x, positions, meta_tokens, norm_gain, w_in, pool_w_group, pool_scale, pool_w_up,
    q_a_norm_gain, kv_a_norm_gain, w_q_b, w_kv_b, q_norm_gain, k_norm_gain, mla_w_up, w_out,
    norm1_gain_2, w_in_2, b_gates_2, q_norm_gain_2, k_norm_gain_2, lambda_q1_2, lambda_k1_2,
    lambda_q2_2, lambda_k2_2, attn_subln_gain_2, w_attn_o_2, conv_w_2, conv_b_2, lru_wa_2,
    lru_ba_2, lru_wi_2, lru_bi_2, lru_lambda_2, w_lru_o_2, w_out_2, norm2_gain_2,
    w_group_router_2, b_group_router_2, w_expert_router_2, b_expert_router_2, w_expert_gate_2,
    w_expert_up_2, w_expert_down_2,
):
    x = first_block(
        x, positions, meta_tokens, norm_gain, w_in, pool_w_group, pool_scale, pool_w_up,
        q_a_norm_gain, kv_a_norm_gain, w_q_b, w_kv_b, q_norm_gain, k_norm_gain, mla_w_up, w_out,
    )
    return second_block(
        x, norm1_gain_2, w_in_2, b_gates_2, q_norm_gain_2, k_norm_gain_2, lambda_q1_2,
        lambda_k1_2, lambda_q2_2, lambda_k2_2, attn_subln_gain_2, w_attn_o_2, conv_w_2,
        conv_b_2, lru_wa_2, lru_ba_2, lru_wi_2, lru_bi_2, lru_lambda_2, w_lru_o_2, w_out_2,
        norm2_gain_2, w_group_router_2, b_group_router_2, w_expert_router_2, b_expert_router_2,
        w_expert_gate_2, w_expert_up_2, w_expert_down_2,
    )


_drawn_inputs = setup_inputs


def setup_inputs(seed=0):
    import zlib

    import numpy as np

    out = dict(_drawn_inputs(seed))
    spreads = {}
    factors = {'norm_gain': 3.384,
     'pool_scale': 7.432,
     'q_a_norm_gain': 8.0,
     'kv_a_norm_gain': 8.0,
     'q_norm_gain': 8.0,
     'k_norm_gain': 8.0,
     'b_gates_2': 47.126,
     'q_norm_gain_2': 24.272,
     'k_norm_gain_2': 12.934,
     'attn_subln_gain_2': 109.695,
     'lru_ba_2': 200.0,
     'lru_bi_2': 200.0,
     'norm2_gain_2': 9.779,
     'b_group_router_2': 34.634,
     'b_expert_router_2': 44.8,
     'norm1_gain_2': 3.254,
     'lambda_q1_2': 6.163,
     'lambda_k1_2': 5.797,
     'lambda_k2_2': 5.626,
     'conv_w_2': 27.728,
     'conv_b_2': 64.0,
     'lru_wa_2': 45.512,
     'lru_wi_2': 43.408,
     'lru_lambda_2': 41.824,
     'w_lru_o_2': 8.0}
    for name, (base, spread) in spreads.items():
        noise = np.random.default_rng([zlib.crc32(name.encode()), seed]).standard_normal(out[name].shape)
        drawn = base * np.exp(spread * noise) if base else spread * noise
        out[name] = __import__('jax').numpy.asarray(drawn.astype(out[name].dtype))
    for name, factor in factors.items():
        out[name] = (out[name] * factor).astype(out[name].dtype)
    return out
```

```python
import math
from contextlib import ExitStack

import numpy as np

import concourse.bass as bass
from concourse import mybir
from concourse.alu_op_type import AluOpType as ALU

F32 = mybir.dt.float32
I32 = mybir.dt.int32
U32 = mybir.dt.uint32
ACT = mybir.ActivationFunctionType
AX = mybir.AxisListType

P = 128
D = 1024
DC = D // P
SEQ = 512
META = 16
T = META + SEQ
HALF = T // 2
LAYERS = 2
HEADS = 8
NOPE, ROPE, VD = 64, 32, 64
QK = NOPE + ROPE
QR, KVR = 768, 256
QC, KC = QR // P, KVR // P
POOLW = 512
PG = POOLW // P
EPS = 1e-6
SCALE1 = 1.0 / math.sqrt(QK)
TILES = [(0, META)] + [(META + P * i, P) for i in range(SEQ // P)]
NT = len(TILES)
PAD = 16
LV = 22

C_U, C_Z, C_Q, C_ROPE, C_ZM, C_GP, C_GM = 0, 512, 1024, 2048, 2080, 2592, 3616

R_L, R_A, R_B, R_R, R_S, R_X, R_M, R_W, R_P, R_Q, R_WT, R_END = (
    0, 80, 400, 720, 800, 824, 904, 968, 1032, 1112, 1176, 1184)
R_V = 1200

SLOTS = 3
SLOT_F = 4096
ACCS = 4

K_IDENT, K_MASK, K_ROT2, K_ROT1, K_FREQ, K_META, K_CNT = 0, 128, 256, 384, 416, 417, 433
K_BD = K_CNT + PG * PAD
K_TIE = K_BD + P
K_LT = K_TIE + 16
K_IOTA = K_LT + P
K_TOKEN = K_IOTA + P
K_FIRST = K_TOKEN + 4
K_ONES = K_FIRST + 16
OVER = 7
K_NTH = K_ONES + 48
K_OE = K_NTH + OVER
K_OT = K_OE + 48
K_END = K_OT + 48

S = SEQ
QT = S // P
SUB = 64
SCALE2 = SUB ** -0.5
LAM_INIT = 0.8 - 0.6 * math.exp(-0.3 * 0)
G2 = 14
DIRS = 2
TAPS = 4
GROUPS, EPG = 4, 4
EXPERTS = GROUPS * EPG
HID = 512
V_N1, V_N2, V_BG, V_SUB, V_CW, V_CB, V_BA, V_BI, V_LM, V_QN, V_KN, V_END = (
    0, 8, 16, 32, 33, 65, 73, 89, 105, 121, 122, 123)


def constants():
    t = np.zeros((P, K_END), np.float32)
    t[:, K_IDENT:K_IDENT + P] = np.eye(P)
    t[:, K_MASK:K_MASK + P] = np.where(np.arange(P)[None, :] > np.arange(P)[:, None], -1e30, 0.0)
    for sub in range(2):
        for m in range(64):
            k = m + 32 if m < 32 else m - 32
            t[64 * sub + k, K_ROT2 + 64 * sub + m] = -1.0 if m < 32 else 1.0
    for m in range(ROPE):
        k = m + 16 if m < 16 else m - 16
        t[NOPE + k, K_ROT1 + m] = -1.0 if m < 16 else 1.0
    freq = (10000.0 ** (-(np.arange(16, dtype=np.float32) / np.float32(16)).astype(np.float64))).astype(np.float32)
    t[NOPE:QK, K_FREQ] = np.tile(freq, 2)
    t[:, K_META:K_META + META] = np.arange(META)
    for g in range(PG):
        t[:, K_CNT + g * PAD:K_CNT + (g + 1) * PAD] = 1.0 / np.minimum(np.arange(1, PAD + 1), 2 ** (g + 1))
    for sub in range(2):
        t[64 * sub:64 * sub + 64, K_BD + 64 * sub:K_BD + 64 * sub + 64] = 1.0
    for i in range(4):
        t[:, K_TIE + 4 * i:K_TIE + 4 * i + i] = 1.0
    t[:, K_IOTA:K_IOTA + P] = np.arange(P)
    t[:, K_TOKEN:K_TOKEN + 4] = np.arange(P)[:, None] + P * np.arange(4)
    t[:, K_FIRST:K_FIRST + 16] = P * np.arange(16) + 1
    t[:, K_ONES:K_ONES + 48] = 1.0
    t[:, K_NTH:K_NTH + OVER] = np.arange(1, OVER + 1)
    t[:, K_OE:K_OE + 48] = np.tile(np.arange(16), 3)
    t[:, K_OT:K_OT + 48] = np.repeat(128 * np.arange(1, 4), 16)
    t[:, K_LT:K_LT + P] = np.arange(P)[:, None] < np.arange(P)[None, :]
    return t


def rotary_table():
    inv = (10000.0 ** (-(np.arange(0, SUB, 2, dtype=np.float32) / np.float32(SUB)).astype(np.float64)))
    ang = (np.arange(S, dtype=np.float32)[:, None] * inv.astype(np.float32)[None, :]).astype(np.float32)
    ang = np.tile(ang.T.astype(np.float64), (P // 32, 1))
    return np.stack([np.cos(ang), np.sin(ang)], axis=1).astype(np.float32)


class Counts:

    def __init__(self, known=None):
        self.known = known
        self.value, self.marks, self.start, self.per, self.trips = {}, {}, {}, {}, {}
        self.slots = {}
        self.inside = None

    def mark(self, sem, label=None, by=1):
        self.value[sem.name] = self.value.get(sem.name, 0) + by
        if label is not None:
            assert (sem.name, label) not in self.marks, label
            self.marks[sem.name, label] = (self.inside and self.inside[0], self.value[sem.name])

    def enter(self, loop, index, trips):
        self.inside = (loop, index)
        self.trips[loop] = trips
        self.begun = dict(self.value)

    def leave(self):
        loop = self.inside[0]
        for name, v in self.value.items():
            start = self.begun.get(name, 0)
            if v > start:
                self.start[loop, name], self.per[loop, name] = start, v - start
                self.value[name] = start + (v - start) * self.trips[loop]
        self.inside = None

    def _value(self, name, loop, v, back):
        if loop is None:
            return v
        per = self.known.per[loop, name]
        if self.inside and self.inside[0] == loop:
            return self.inside[1] * per + (v - back * per)
        return v + (self.known.trips[loop] - 1) * per

    def at(self, sem, label, back=0):
        if self.known is None:
            return 1
        loop, v = self.known.marks[sem.name, label]
        return self._value(sem.name, loop, v, back)

    def now(self, sem):
        if self.known is None:
            return 1
        return self._value(sem.name, self.inside and self.inside[0], self.value[sem.name], 0)


def program(nc, a, out, known=None, debug=None):
    n = Counts(known)
    mark, at, now = n.mark, n.at, n.now
    with ExitStack() as ctx:
        def sb(name, shape, dt=F32):
            return ctx.enter_context(nc.sbuf_tensor(name, shape, dt))

        def sem(name):
            return ctx.enter_context(nc.semaphore(name))

        ring = sb("ring", [P, SLOTS, SLOT_F])
        hres = sb("hres", [P, DC, T])
        h = sb("h", [P, DC, T])
        upad = sb("upad", [P, PG, PAD + T])
        zp = sb("zp", [P, PG, T])
        latent = sb("latent", [P, QC + KC, T])
        krope = sb("krope", [P, 2, T])
        qk = sb("qk", [P, 2 * HEADS, T])
        v = sb("v", [P, NT, HEADS * VD])
        work = sb("work", [P, DC, T])
        gate = sb("gate", [P, 2, T])
        o = sb("o", [P, PG, T])
        trig = sb("trig", [P, 2, T])
        const = sb("const", [P, K_END])
        ones = sb("ones", [P, P])
        vecs = sb("vecs", [P, LAYERS * LV])
        lv = sb("lv", [P, LV])
        small = sb("small", [P, 16])
        vec2 = sb("vec2", [P, V_END])
        half_bias = sb("half_bias", [P, V_LM - V_BG])
        lamt = sb("lamt", [P, 4 * SUB])
        decay = sb("decay", [P, 6, 16])
        router = sb("router", [P, DC, GROUPS + EXPERTS])
        router_bias = sb("router_bias", [P, GROUPS + EXPERTS])
        logits = sb("logits", [P, QT, GROUPS + EXPERTS])
        rt = sb("rt", [P, 1, 8])
        rows_of = sb("rows_of", [P, EXPERTS + 1], U32)
        back_rows = sb("back_rows", [P, 8], U32)
        over_i = sb("over_i", [P, 1 + OVER], I32)
        over_t = sb("over_t", [P, OVER])
        h_rows = nc.dram_tensor("h_rows", (S, D), F32, kind="Internal").ap()
        y_rows = nc.dram_tensor("y_rows", ((EXPERTS + OVER) * P, D), F32, kind="Internal").ap()

        qT, kT = qk[:, 0:HEADS, :], qk[:, HEADS:, :]
        cq, ckv = latent[:, 0:QC, :], latent[:, QC:, :]
        flat = latent[:, :, :].rearrange("p c t -> p (c t)")
        probs = [flat[:, i * T:(i + 1) * T] for i in range(3)]
        probsT = [flat[:, 3 * T + i * NT * P:3 * T + (i + 1) * NT * P].rearrange("p (j q) -> p j q", j=NT)
                  for i in range(2)]
        cosT, sinT = trig[NOPE:QK, 0, :], trig[NOPE:QK, 1, :]
        win = [kT[:, i, :] for i in range(2)]
        winA = qk[:, HEADS:HEADS + 2, :].rearrange("p c t -> p (c t)")[:, 0:PAD + T]
        winB = qk[:, HEADS + 2:HEADS + 4, :].rearrange("p c t -> p (c t)")[:, 0:PAD + T]
        qkf = qk[:, :, :].rearrange("p c t -> p (c t)")
        xin = qkf[:, 0:4 * D].rearrange("p (i d) -> p i d", i=4)
        metain = qkf[:, 4 * D:5 * D]
        vrows = qkf[:, 5 * D:5 * D + P]
        vrows2 = qkf[:, 5 * D + P:5 * D + 2 * P]
        ident, mask = const[:, K_IDENT:K_IDENT + P], const[:, K_MASK:K_MASK + P]
        rot1 = const[NOPE:QK, K_ROT1:K_ROT1 + ROPE]

        xr = hres[:, :, META:T]
        h2 = h[:, :, 0:S]
        q2, k2 = qk[:, 0:DC, 0:S], qk[:, DC:, 0:S]
        workf = work[:, :, :].rearrange("p c t -> p (c t)")
        v2 = workf[:, 0:QT * D].rearrange("p (j n) -> p j n", j=QT)
        merged = work[:, :, 0:S]
        lru_x = latent
        gelu = [zp[:, c, 0:S] if c < PG else o[:, c - PG, 0:S] for c in range(DC)]
        tmp = [v[:, i, :] for i in range(NT)]
        probs2 = [[gate[:, c, 0:S] for c in range(2)], [krope[:, c, 0:S] for c in range(2)]]
        padf = upad[:, :, :].rearrange("p c t -> p (c t)")
        probsT2 = [padf[:, i * S:(i + 1) * S].rearrange("p (j q) -> p j q", j=QT) for i in range(4)]
        cos2, sin2 = trig[:, 0, 0:S], trig[:, 1, 0:S]
        x_tok = workf[:, 0:QT * D].rearrange("p (i d) -> p i d", i=QT)
        h_tok = qkf[:, 0:QT * D].rearrange("p (i d) -> p i d", i=QT)
        returned = qkf[:, 0:8 * D].rearrange("p (i d) -> p i d", i=8)
        x_gath = flat[:, 0:D]
        x_exp = flat[:, D:2 * D].rearrange("p (k s) -> p k s", k=DC)
        hid = flat[:, 2 * D:2 * D + HID]
        hid_t = flat[:, 2 * D + HID:3 * D].rearrange("p (k s) -> p k s", k=HID // P)
        y_out = flat[:, 3 * D:4 * D]
        zpf = zp[:, :, :].rearrange("p c t -> p (c t)")
        picks = [zpf[:, i * 512:(i + 1) * 512].rearrange("p (i s) -> p i s", i=QT) for i in range(2)]
        R = o[:, :, :].rearrange("p c t -> p (c t)")
        rot2 = const[:, K_ROT2:K_ROT2 + P]
        blocks = const[:, K_BD:K_BD + P]

        acc = ctx.enter_context(nc.psum_tensor("acc", [P, ACCS, 2, 512], F32))

        psum_filled = sem("psum_filled")
        act_evacuated = sem("act_evacuated")
        dve_evacuated = sem("dve_evacuated")
        act_made = sem("act_made")
        dve_made = sem("dve_made")
        pool_made = sem("pool_made")
        dve_step = sem("dve_step")
        pool_step = sem("pool_step")
        w_loaded = [sem(f"w_loaded{i}") for i in range(SLOTS)]
        w_free = [sem(f"w_free{i}") for i in range(SLOTS)]
        const_loaded = sem("const_loaded")
        x_loaded = sem("x_loaded")
        vec_loaded = sem("vec_loaded")
        stored = sem("stored")
        y_zeroed = sem("y_zeroed")
        summed = sem("summed")
        turned_x = sem("turned_x")
        column = sb("column", [P, 1], U32)
        picked = sem("picked")
        combined = sem("combined")
        h_stored = sem("h_stored")
        x_gathered = sem("x_gathered")
        y_stored = sem("y_stored")
        all_stored = sem("all_stored")
        rows_back = [sem(f"rows_back{i}") for i in range(QT)]

        held = sem("held")

        def rows(w, c0, c1):
            return w[:, c0:c1].rearrange("(k p) n -> p k n", p=P)

        def layer_granules(layer):
            w = a["w_in"][layer]
            return [
                ("cq0", rows(w, C_Q, C_Q + 512)), ("cq1", rows(w, C_Q + 512, C_Q + 1024)),
                ("u", rows(w, C_U, C_U + 512)), ("rope", rows(w, C_ROPE, C_ROPE + ROPE)),
                ("kvb", rows(a["w_kv_b"][layer], 0, HEADS * (NOPE + VD))),
                ("qb0", rows(a["w_q_b"][layer], 0, 4 * QK)), ("qb1", rows(a["w_q_b"][layer], 4 * QK, 8 * QK)),
                ("z", rows(w, C_Z, C_Z + 512)),
                ("pg", a["pool_w_group"][layer].rearrange("g c d -> c g d")),
                ("pup", rows(a["pool_w_up"][layer], 0, D)),
                ("gp0", rows(w, C_GP, C_GP + 512)), ("gp1", rows(w, C_GP + 512, C_GP + 1024)),
                ("zm", rows(w, C_ZM, C_ZM + 512)),
                ("mup", rows(a["mla_w_up"][layer], 0, D)),
                ("gm0", rows(w, C_GM, C_GM + 512)), ("gm1", rows(w, C_GM + 512, C_GM + 1024)),
                ("wo0", rows(a["w_out"][layer], 0, 512)), ("wo1", rows(a["w_out"][layer], 512, 1024)),
            ]

        shapes1 = {name: (i % SLOTS, ap.shape[1], ap.shape[2])
                   for i, (name, ap) in enumerate(layer_granules(0))}
        assert len(shapes1) % SLOTS == 0
        LAST1 = list(shapes1)

        def weight(name):
            slot, k, m = shapes1[name]
            return ring[:, slot, 0:k * m].rearrange("p (k m) -> p k m", k=k)

        GRANULES2 = (["q0", "q1", "k0", "k1", "v0", "v1", "lx0", "lx1", "lg0", "lg1", "lru",
                      "ga0", "ao0", "ga1", "ao1", "gl0", "lo0", "gl1", "lo1", "xo0", "xo1"])
        COLS2 = {x: 512 * i for i, x in enumerate(
            ["q0", "q1", "k0", "k1", "v0", "v1", "lx0", "lx1", "lg0", "lg1", "ga0", "ga1", "gl0", "gl1"])}
        PLACE2 = [0, 1, 2, 0, 1, 2, 0, 1, 2, 0, 1, 2, 0, 2, 0, 1, 2, 0, 1, 2, 0]
        for name, place in zip(GRANULES2, PLACE2):
            shapes1[name] = (place, 32, P) if name == "lru" else (place, DC, 512)
        order1 = list(shapes1)
        for over in "", "+":
            shapes1["gate" + over], shapes1["up" + over] = (0, DC, HID), (1, DC, HID)
            shapes1["down" + over] = (2, HID // P, D)

        background = ([("z", i) for i in range(PG)] + [("pg", i) for i in range(PG)]
                      + [x for m in range(DC) for x in (("gp", m), ("yp", m))])
        items = [(hd, i) for hd in range(HEADS) for i in range(NT)]
        STEPS = len(items) + 3

        def background_at(step):
            lo, hi = (step * len(background)) // STEPS, ((step + 1) * len(background)) // STEPS
            return background[lo:hi]

        def gate_uses():
            order = []
            for x in background:
                if x[0] in ("z", "gp"):
                    order.append(x)
            order += [("zm", c) for c in range(PG)] + [("gm", m) for m in range(DC)]
            return {x: i for i, x in enumerate(order)}, order

        gate_no, gate_order = gate_uses()

        def gate_reader(x):
            return {"z": ("z", x[1]), "gp": ("yp", x[1]), "zm": ("og", x[1]), "gm": ("mg", x[1])}[x[0]]

        items2 = [(hd, i) for hd in range(HEADS) for i in range(QT)]
        STEPS2 = len(items2) + 2

        def background2_at(step):
            return range((step * DC) // STEPS2, ((step + 1) * DC) // STEPS2)

        lru_units = [(d, c) for c0 in range(0, DC, 2) for d in range(DIRS) for c in (c0, c0 + 1)]

        def unit_tiles(u):
            tiles = [k2[:, i, :] for i in range(DC)] + [padf[:, i * S:(i + 1) * S] for i in range(4)]
            return tiles[3 * (u % 4):3 * (u % 4) + 3]

        block = ctx.enter_context(nc.Block())

        @block.sync
        def _(sp):
            sp.dma_start(const[:, :], a["const"]).then_inc(const_loaded, 16)
            for i in range(4):
                sp.dma_start(xin[:, i, :], a["x"][0, i * P:(i + 1) * P, :]).then_inc(x_loaded, 16)
            sp.dma_start(metain[0:META, :], a["meta_tokens"]).then_inc(x_loaded, 16)
            sp.wait_ge(pool_made, at(pool_made, "vrows"))
            for l in range(LAYERS):
                r = LV * l
                for name, r0, k, m in (("norm_gain", 0, DC, P), ("q_a_norm_gain", 8, QC, P),
                                       ("kv_a_norm_gain", 14, KC, P), ("pool_scale", 16, PG, P),
                                       ("q_norm_gain", 20, 1, QK), ("k_norm_gain", 21, 1, QK)):
                    sp.dma_start(vrows[r + r0:r + r0 + k, 0:m],
                                 a[name][l].rearrange("(k m) -> k m", k=k)).then_inc(vec_loaded, 16)
                    mark(vec_loaded, None, 16)
            for name, r0, k in (("norm1_gain_2", V_N1, DC), ("norm2_gain_2", V_N2, DC), ("b_gates_2", V_BG, 16),
                                ("attn_subln_gain_2", V_SUB, 1), ("conv_w_2", V_CW, TAPS * DC),
                                ("conv_b_2", V_CB, DC), ("lru_ba_2", V_BA, 16), ("lru_bi_2", V_BI, 16),
                                ("lru_lambda_2", V_LM, 16)):
                src = a[name][0]
                src = src.rearrange("j (c m) -> (j c) m", m=P) if len(src.shape) == 2 else \
                    src.rearrange("(k m) -> k m", k=k)
                sp.dma_start(vrows2[r0:r0 + k, :], src).then_inc(vec_loaded, 16)
                mark(vec_loaded, None, 16)
            for name, r0 in (("q_norm_gain_2", V_QN), ("k_norm_gain_2", V_KN)):
                for sub in range(2):
                    sp.dma_start(vrows2[r0:r0 + 1, SUB * sub:SUB * sub + SUB], a[name]).then_inc(vec_loaded, 16)
                    mark(vec_loaded, None, 16)
            for i, name in enumerate(("lambda_q1_2", "lambda_k1_2", "lambda_q2_2", "lambda_k2_2")):
                sp.dma_start(lamt[:, i * SUB:(i + 1) * SUB], a[name].to_broadcast([P, SUB])).then_inc(vec_loaded, 16)
                mark(vec_loaded, None, 16)
            with nc.allow_non_contiguous_dma(reason="narrow router weights"):
                sp.dma_start(router[:, :, 0:GROUPS], a["w_group_router_2"][0].rearrange("(k p) n -> p k n", p=P))\
                    .then_inc(vec_loaded, 16)
                sp.dma_start(router[:, :, GROUPS:], a["w_expert_router_2"][0].rearrange("(k p) n -> p k n", p=P))\
                    .then_inc(vec_loaded, 16)
            sp.dma_start(router_bias[:, 0:GROUPS], a["b_group_router_2"].to_broadcast([P, GROUPS]))\
                .then_inc(vec_loaded, 16)
            sp.dma_start(router_bias[:, GROUPS:], a["b_expert_router_2"].to_broadcast([P, EXPERTS]))\
                .then_inc(vec_loaded, 16)
            mark(vec_loaded, None, 64)
            sp.dma_start(krope[NOPE:QK, 0, META:T].bitcast(I32),
                         
                         a["positions"].to_broadcast([ROPE, SEQ])).then_inc(vec_loaded, 16)
            mark(vec_loaded, "positions", 16)

            with sp.Fori(0, LAYERS) as layer:
                n.enter("layer", layer, LAYERS)
                for i, (name, src) in enumerate(layer_granules(layer)):
                    slot = i % SLOTS
                    last = LAST1[i - SLOTS] if i < SLOTS else order1[i - SLOTS]
                    sp.wait_ge(w_free[slot], at(w_free[slot], ("used", last), back=i < SLOTS))
                    sp.sem_inc(held, 1)
                    sp.dma_start(weight(name), src).then_inc(w_loaded[slot], 16)
                    mark(w_loaded[slot], name, 16)
                n.leave()
            w2 = {x: rows(a["w_in_2"][0], c, c + 512) for x, c in COLS2.items()}
            for x, name in (("ao", "w_attn_o_2"), ("lo", "w_lru_o_2"), ("xo", "w_out_2")):
                for i in range(2):
                    w2[f"{x}{i}"] = rows(a[name][0], 512 * i, 512 * i + 512)
            in_slot = {shapes1[x][0]: x for x in LAST1}
            for name in GRANULES2:
                slot = shapes1[name][0]
                last, in_slot[slot] = in_slot[slot], name
                sp.wait_ge(w_free[slot], at(w_free[slot], ("used", last)))
                if name == "lru":
                    for kind, x in enumerate(("lru_wa_2", "lru_wi_2")):
                        for d in range(DIRS):
                            at_ = 16 * kind + 8 * d
                            sp.dma_start(weight(name)[:, at_:at_ + 8, :],
                                         a[x][0, d].rearrange("b d e -> d b e")).then_inc(w_loaded[slot], 16)
                    mark(w_loaded[slot], name, 64)
                else:
                    sp.dma_start(weight(name), w2[name]).then_inc(w_loaded[slot], 16)
                    mark(w_loaded[slot], name, 16)
                if name == "q0":
                    sp.wait_ge(dve_made, at(dve_made, ("qr", HEADS - 1)))
                    sp.dma_start(trig[:, :, 0:S], a["rotary"]).then_inc(const_loaded, 16)
                    mark(const_loaded, "rotary", 32)
            for i in range(QT):
                sp.wait_ge(act_evacuated, at(act_evacuated, ("h_tok", i)))
                sp.dma_start(h_rows[i * P:(i + 1) * P, :], h_tok[:, i, :]).then_inc(h_stored, 16)

            def expert_weights(expert, over):
                for x in "gate", "up", "down":
                    name = x + over
                    slot = shapes1[name][0]
                    sp.wait_ge(w_free[slot], at(w_free[slot], ("used", name), back=1))
                    sp.sem_inc(held, 1)
                    sp.dma_start(weight(name), a[f"w_expert_{x}_2"][0, expert].rearrange("(k p) n -> p k n", p=P))\
                        .then_inc(w_loaded[slot], 16)
                    mark(w_loaded[slot], name, 16)

            with sp.Fori(0, EXPERTS) as e:
                n.enter("experts", e, EXPERTS)
                expert_weights(e, "")
                n.leave()
            sp.wait_ge(dve_made, at(dve_made, "over"))
            tiles = sp.value_load(over_i[0:1, 0:1], min_val=0, max_val=OVER)
            with sp.If(tiles > 0):
                with sp.Fori(0, tiles) as k:
                    n.enter("over", k, 1)
                    expert_weights(sp.value_load(over_i[0:1, bass.ds(k + 1, 1)], min_val=0, max_val=EXPERTS - 1), "+")
                    n.leave()
            for i in range(QT):
                sp.wait_ge(combined, i + 1)
                sp.dma_start(out[0, i * P:(i + 1) * P, :], x_tok[:, i, :]).then_inc(stored, 16)
            sp.wait_ge(stored, 16 * QT)
            if debug is not None:
                sp.wait_ge(dve_evacuated, at(dve_evacuated, ("out2", DC - 1)))
                sp.dma_start(debug, hres[:, :, :]).then_inc(stored, 16)
                sp.wait_ge(stored, 16 * QT + 16)

        @block.tensor
        def _(pe):
            jobs = []

            def accumulator(label, reader):
                slot = len(jobs) % ACCS
                if len(jobs) >= ACCS:
                    before, by = jobs[-ACCS]
                    pe.wait_ge(by, at(by, before))
                    pe.sem_inc(held, 1)
                jobs.append((label, reader))
                n.slots[label] = slot
                return acc[:, slot, :, :]

            def done(ins, label):
                ins.then_inc(psum_filled, 1)
                mark(psum_filled, label)

            def drained():
                last = {by.name: (before, by) for before, by in jobs[-ACCS:]}
                for before, by in last.values():
                    pe.wait_ge(by, at(by, before))
                jobs.clear()

            def loaded(name):
                slot = shapes1[name][0]
                pe.wait_ge(w_loaded[slot], at(w_loaded[slot], name))

            def used(ins, name):
                slot = shapes1[name][0]
                ins.then_inc(w_free[slot], 1)
                mark(w_free[slot], ("used", name))

            def free(name):
                slot = shapes1[name][0]
                pe.drain().then_inc(w_free[slot], 1)
                mark(w_free[slot], ("used", name))

            def product(label, reader, lhs, rhs, rows_=P, at_row=0, before=None):
                dst = accumulator(label, reader)
                for k, w in enumerate(lhs):
                    if before:
                        before(k)
                    for half in range(2):
                        ins = nc.tensor.matmul(dst[at_row:at_row + rows_, half, 0:HALF], w,
                                               rhs(k)[:, half * HALF:(half + 1) * HALF],
                                               start=(k == 0), stop=(k == len(lhs) - 1),
                                               skip_group_check=True)
                done(ins, label)

            for slot in range(SLOTS):
                pe.sem_inc(w_free[slot], LAYERS * 3)
                mark(w_free[slot], None, LAYERS * 3)

            pe.wait_ge(const_loaded, 16)
            pe.wait_ge(vec_loaded, at(vec_loaded, "positions"))
            pe.wait_ge(pool_made, at(pool_made, "vrows"))
            dst = accumulator("vecs", dve_evacuated)
            done(nc.tensor.transpose(dst[:, 0, 0:LAYERS * LV], vrows[0:LAYERS * LV, :],
                                     ident[0:LAYERS * LV, 0:LAYERS * LV]), "vecs")
            dst = accumulator("vec2", dve_evacuated)
            done(nc.tensor.transpose(dst[:, 0, 0:V_END], vrows2[0:V_END, :], ident[0:V_END, 0:V_END]), "vec2")
            pe.wait_ge(x_loaded, 80)
            for c in range(DC):
                dst = accumulator(("x", c), dve_evacuated)
                for i in range(4):
                    nc.tensor.transpose(dst[:, 0, i * P:(i + 1) * P], xin[:, i, c * P:(c + 1) * P], ident)
                done(nc.tensor.transpose(dst[:, 1, 0:META], metain[0:META, c * P:(c + 1) * P],
                                         ident[0:META, 0:META]), ("x", c))
            drained()
            pe.wait_ge(pool_made, at(pool_made, "ones"))

            with pe.Fori(0, LAYERS) as layer:
                n.enter("layer", layer, LAYERS)
                chunk = lambda x: (lambda k: x[:, k, :])

                product("ss_h", act_evacuated, [ones[:, :]] * DC, chunk(work),
                        before=lambda k: pe.wait_ge(act_made, at(act_made, ("sq", k))))

                def h_ready(k):
                    pe.wait_ge(dve_made, at(dve_made, ("h", k)))

                for name, c0, kinds in (("cq0", 0, 4), ("cq1", 4, 4)):
                    loaded(name)
                    for j in range(kinds):
                        c = c0 + j
                        product(("c", c), act_evacuated,
                                [weight(name)[:, k, j * P:(j + 1) * P] for k in range(DC)], chunk(h),
                                before=h_ready if c == 0 else None)
                    free(name)
                loaded("u")
                for j in range(PG):
                    product(("u", j), dve_evacuated,
                            [weight("u")[:, k, j * P:(j + 1) * P] for k in range(DC)], chunk(h))
                free("u")
                pe.wait_ge(act_evacuated, at(act_evacuated, ("c", QC + KC - 1)))
                product("ss_cq", act_evacuated, [ones[:, :]] * QC, chunk(work))
                product("ss_ckv", act_evacuated, [ones[:, :]] * KC, lambda k: work[:, QC + k, :])
                loaded("rope")
                product("rope", dve_evacuated, [weight("rope")[:, k, :] for k in range(DC)], chunk(h),
                        rows_=ROPE, at_row=NOPE)
                free("rope")
                pe.wait_ge(dve_evacuated, at(dve_evacuated, "rope"))
                product("rotk", dve_evacuated, [rot1], lambda k: krope[NOPE:QK, 0, :],
                        rows_=ROPE, at_row=NOPE)
                loaded("kvb")
                wkv = weight("kvb").rearrange("p k (h c) -> p k h c", h=HEADS)
                pe.wait_ge(dve_made, at(dve_made, ("cn", QC + KC - 1)))
                for i, (t0, nt) in enumerate(TILES):
                    dst = accumulator(("v", i), act_evacuated)
                    for k in range(KC):
                        ins = nc.tensor.matmul(dst[0:nt, 0, :], ckv[:, k, t0:t0 + nt], wkv[:, k, :, NOPE:],
                                               start=(k == 0), stop=(k == KC - 1))
                    done(ins, ("v", i))
                def k_head(hd):
                    product(("k", hd), act_evacuated, [wkv[:, k, hd, 0:NOPE] for k in range(KC)],
                            chunk(ckv), rows_=NOPE)

                def kss(hd):
                    pe.wait_ge(act_evacuated, at(act_evacuated, ("k", hd)))
                    if hd == 0:
                        pe.wait_ge(act_made, at(act_made, "sq_rope"))
                    product(("kss", hd), act_evacuated, [ones[0:QK, 0:QK]],
                            lambda k: work[0:QK, 2 + hd % 2, :], rows_=QK)

                def q_head(hd):
                    w = weight(f"qb{hd // 4}")
                    m = (hd % 4) * QK
                    product(("q", hd), act_evacuated, [w[:, k, m:m + QK] for k in range(QC)],
                            chunk(cq), rows_=QK)

                def qss(hd):
                    pe.wait_ge(act_evacuated, at(act_evacuated, ("q", hd)))
                    product(("qss", hd), act_evacuated, [ones[0:QK, 0:QK]],
                            lambda k: work[0:QK, 4 + hd % 2, :], rows_=QK)

                def rotq(hd):
                    pe.wait_ge(dve_made, at(dve_made, ("qn", hd)))
                    product(("rotq", hd), dve_evacuated, [rot1], lambda k: qT[NOPE:QK, hd, :],
                            rows_=ROPE, at_row=NOPE)

                for hd in range(HEADS + 2):
                    if hd < HEADS:
                        if hd % 4 == 0:
                            loaded(f"qb{hd // 4}")
                        k_head(hd)
                        if hd == HEADS - 1:
                            free("kvb")
                        q_head(hd)
                        if hd % 4 == 3:
                            free(f"qb{hd // 4}")
                    if 1 <= hd <= HEADS:
                        kss(hd - 1)
                        qss(hd - 1)
                    if hd >= 2:
                        rotq(hd - 2)

                def scores(s):
                    hd, i = items[s]
                    t0, nt = TILES[i]
                    if i == 0:
                        pe.wait_ge(dve_made, at(dve_made, ("qr", hd)))
                    dst = accumulator(("s", s), act_evacuated).rearrange("p a b -> p (a b)")
                    for c0 in range(0, t0 + nt, 512):
                        c1 = min(c0 + 512, t0 + nt)
                        ins = nc.tensor.matmul(dst[0:nt, c0:c1], qT[0:QK, hd, t0:t0 + nt],
                                               kT[0:QK, hd, c0:c1], start=True, stop=True)
                    done(ins, ("s", s))

                def turn(s):
                    hd, i = items[s]
                    nt = TILES[i][1]
                    pe.wait_ge(dve_made, at(dve_made, ("p", s)))
                    dst = accumulator(("t", s), act_evacuated).rearrange("p a (b q) -> p (a b) q", q=P)
                    for j in range(i + 1):
                        k0, nk = TILES[j]
                        ins = nc.tensor.transpose(dst[0:nk, j, 0:nt], probs[s % 3][0:nt, k0:k0 + nk],
                                                  ident[0:nt, 0:nt])
                    done(ins, ("t", s))

                def values(s):
                    hd, i = items[s]
                    nt = TILES[i][1]
                    pe.wait_ge(act_evacuated, at(act_evacuated, ("t", s)))
                    dst = accumulator(("o", s), act_evacuated)
                    r = VD * (hd % 2)
                    for j in range(i + 1):
                        nk = TILES[j][1]
                        ins = nc.tensor.matmul(dst[r:r + VD, 0, 0:nt], v[0:nk, j, hd * VD:(hd + 1) * VD],
                                               probsT[s % 2][0:nk, j, 0:nt], start=(j == 0), stop=(j == i),
                                               skip_group_check=True)
                    done(ins, ("o", s))

                def back(x):
                    kind, m = x
                    if kind == "z":
                        if m == 0:
                            loaded("z")
                        product(x, dve_evacuated, [weight("z")[:, k, m * P:(m + 1) * P] for k in range(DC)],
                                chunk(h))
                        if m == PG - 1:
                            free("z")
                    elif kind == "pg":
                        if m == 0:
                            loaded("pg")
                        pe.wait_ge(dve_made, at(dve_made, ("mixed", m)))
                        product(x, dve_evacuated, [weight("pg")[:, m, :]], lambda k: upad[:, m, PAD:])
                        if m == PG - 1:
                            free("pg")
                    elif kind == "gp":
                        g = f"gp{m // 4}"
                        if m % 4 == 0:
                            loaded(g)
                        product(x, act_evacuated,
                                [weight(g)[:, k, (m % 4) * P:(m % 4 + 1) * P] for k in range(DC)], chunk(h))
                        if m == 3:
                            free(g)
                    else:
                        if m == 0:
                            loaded("pup")
                            pe.wait_ge(dve_evacuated, at(dve_evacuated, ("pg", PG - 1)))
                        product(x, dve_evacuated, [weight("pup")[:, k, m * P:(m + 1) * P] for k in range(PG)],
                                chunk(zp))
                        if m == DC - 1:
                            free("pup")
                            free("gp1")

                for s in range(STEPS):
                    if s < len(items):
                        scores(s)
                    for x in background_at(s):
                        back(x)
                    if 2 <= s < len(items) + 2:
                        turn(s - 2)
                    if s >= 3:
                        values(s - 3)

                loaded("zm")
                for c in range(PG):
                    product(("zm", c), dve_evacuated,
                            [weight("zm")[:, k, c * P:(c + 1) * P] for k in range(DC)], chunk(h))
                free("zm")
                loaded("mup")
                for m in range(DC):
                    g = f"gm{m // 4}"
                    if m % 4 == 0:
                        loaded(g)
                    product(("gm", m), act_evacuated,
                            [weight(g)[:, k, (m % 4) * P:(m % 4 + 1) * P] for k in range(DC)], chunk(h))
                    if m == 3:
                        free(g)
                    if m == 0:
                        pe.wait_ge(dve_made, at(dve_made, ("og", PG - 1)))
                    product(("ym", m), dve_evacuated,
                            [weight("mup")[:, k, m * P:(m + 1) * P] for k in range(PG)], chunk(o))
                free("mup")
                free("gm1")
                for m in range(DC):
                    g = f"wo{m // 4}"
                    if m % 4 == 0:
                        loaded(g)
                    product(("out", m), dve_evacuated,
                            [weight(g)[:, k, (m % 4) * P:(m % 4 + 1) * P] for k in range(DC)], chunk(work),
                            before=(lambda k: pe.wait_ge(dve_made, at(dve_made, ("mg", k)))) if m == 0 else None)
                    if m % 4 == 3:
                        free(g)
                drained()
                n.leave()

            def product2(label, reader, lhs, rhs, before=None):
                dst = accumulator(label, reader)
                for k, w in enumerate(lhs):
                    if before:
                        before(k)
                    ins = nc.tensor.matmul(dst[:, 0, :], w, rhs(k), start=(k == 0), stop=(k == len(lhs) - 1))
                done(ins, label)

            def projection(label, reader, name, j, rhs, before=None):
                if j == 0:
                    loaded(name)
                product2(label, reader, [weight(name)[:, k, j * P:(j + 1) * P] for k in range(DC)], rhs, before)
                if j == 3:
                    free(name)

            on_h2, on = (lambda k: h2[:, k, :]), (lambda x: (lambda k: x))
            product2("ss_1", act_evacuated, [ones[:, :]] * DC, lambda k: merged[:, k, :],
                     before=lambda k: pe.wait_ge(act_made, at(act_made, ("sq1", k))))

            def qk_sum(c):
                pe.wait_ge(act_evacuated, at(act_evacuated, ("qk", c)))
                product2(("qkss", c), act_evacuated, [blocks], on(tmp[c % 2]))

            def qk_turn(c):
                pe.wait_ge(dve_made, at(dve_made, ("qkn", c)))
                product2(("qkrot", c), dve_evacuated, [rot2], on(qk[:, c, 0:S]))

            for c in range(2 * DC + 2):
                if c < 2 * DC:
                    name = ("q0", "q1", "k0", "k1")[c // 4]
                    projection(("qk", c), act_evacuated, name, c % 4, on_h2,
                               before=(lambda k: pe.wait_ge(dve_made, at(dve_made, ("h1", k)))) if c == 0 else None)
                if 1 <= c <= 2 * DC:
                    qk_sum(c - 1)
                if c >= 2:
                    qk_turn(c - 2)
            for g in range(2):
                name = f"v{g}"
                loaded(name)
                for j in range(QT):
                    dst = accumulator(("v2", g, j), act_evacuated)
                    for k in range(DC):
                        ins = nc.tensor.matmul(dst[:, 0, :], h2[:, k, j * P:(j + 1) * P], weight(name)[:, k, :],
                                               start=(k == 0), stop=(k == DC - 1))
                    done(ins, ("v2", g, j))
                free(name)

            def scores2(s):
                hd, i = items2[s]
                if s == 0:
                    pe.wait_ge(dve_made, at(dve_made, ("qkr", 2 * DC - 1)))
                dst = accumulator(("s2", s), act_evacuated)
                for c in range(2):
                    r = slice(SUB * c, SUB * c + SUB)
                    ins = nc.tensor.matmul(dst[:, c, :], q2[r, hd, i * P:(i + 1) * P], k2[r, hd, :],
                                           start=True, stop=True)
                done(ins, ("s2", s))

            def turn2(s):
                pe.wait_ge(dve_made, at(dve_made, ("p2", s)))
                dst = accumulator(("t2", s), act_evacuated)
                for j in range(QT):
                    ins = nc.tensor.transpose(dst[:, 0, j * P:(j + 1) * P], probs2[s % 2][0][:, j * P:(j + 1) * P],
                                              ident)
                done(ins, ("t2", s))

            def values2(s):
                hd, i = items2[s]
                pe.wait_ge(act_evacuated, at(act_evacuated, ("t2", s)))
                dst = accumulator(("o2", s), act_evacuated)
                for j in range(QT):
                    ins = nc.tensor.matmul(dst[:, 0, 0:P], v2[:, j, hd * P:(hd + 1) * P], probsT2[s % 4][:, j, :],
                                           start=(j == 0), stop=(j == QT - 1))
                done(ins, ("o2", s))

            for s in range(STEPS2):
                if s < len(items2):
                    scores2(s)
                for c in background2_at(s):
                    projection(("lx", c), act_evacuated, f"lx{c // 4}", c % 4, on_h2)
                if 1 <= s <= len(items2):
                    turn2(s - 1)
                if s >= 2:
                    values2(s - 2)
            for c in range(DC):
                projection(("lg", c), act_evacuated, f"lg{c // 4}", c % 4, on_h2)
            for c in range(DC):
                pe.wait_ge(act_made, at(act_made, ("sqo", c)))
                product2(("oss", c), act_evacuated, [ones[:, :]], on(tmp[c % 2]))

            def lru(u):
                d, c = lru_units[u]
                if d == 0:
                    pe.wait_ge(pool_made, at(pool_made, ("conv", c)))
                dst = accumulator(("lru", u), act_evacuated)
                for kind in range(2):
                    ins = nc.tensor.matmul(dst[:, kind, :], weight("lru")[:, 16 * kind + 8 * d + c, :],
                                           lru_x[:, c, 0:S], start=True, stop=True)
                done(ins, ("lru", u))

            loaded("lru")
            for m in range(DC):
                projection(("ga", m), act_evacuated, f"ga{m // 4}", m % 4, on_h2)
                projection(("ya", m), dve_evacuated, f"ao{m // 4}", m % 4, lambda k: q2[:, k, :],
                           before=(lambda k: pe.wait_ge(dve_made, at(dve_made, ("on", k)))) if m == 0 else None)
                lru(2 * m)
                lru(2 * m + 1)
            free("lru")
            for m in range(DC):
                projection(("gl", m), act_evacuated, f"gl{m // 4}", m % 4, on_h2)
                projection(("yl", m), dve_evacuated, f"lo{m // 4}", m % 4, lambda k: gelu[k],
                           before=(lambda k: pe.wait_ge(dve_made, at(dve_made, ("lru_y", k)))) if m == 0 else None)
            for m in range(DC):
                projection(("out2", m), dve_evacuated, f"xo{m // 4}", m % 4, lambda k: merged[:, k, :],
                           before=(lambda k: pe.wait_ge(dve_made, at(dve_made, ("mg2", k)))) if m == 0 else None)
            product2("ss_2", act_evacuated, [ones[:, :]] * DC, lambda k: merged[:, k, :],
                     before=lambda k: pe.wait_ge(act_made, at(act_made, ("sq2", k))))
            for i in range(QT):
                dst = accumulator(("x_tok", i), act_evacuated).rearrange("p a b -> p (a b)")
                for c in range(DC):
                    ins = nc.tensor.transpose(dst[:, c * P:(c + 1) * P], xr[:, c, i * P:(i + 1) * P], ident)
                done(ins, ("x_tok", i))
            dst = accumulator("logits", dve_evacuated)
            for i in range(QT):
                for k in range(DC):
                    if i == 0:
                        pe.wait_ge(dve_made, at(dve_made, ("h3", k)))
                    ins = nc.tensor.matmul(dst[:, 0, 20 * i:20 * i + 20], h2[:, k, i * P:(i + 1) * P],
                                           router[:, k, :], start=(k == 0), stop=(k == DC - 1))
            done(ins, "logits")
            for i in range(QT):
                dst = accumulator(("h_tok", i), act_evacuated).rearrange("p a b -> p (a b)")
                for c in range(DC):
                    ins = nc.tensor.transpose(dst[:, c * P:(c + 1) * P], h2[:, c, i * P:(i + 1) * P], ident)
                done(ins, ("h_tok", i))
            pe.wait_ge(dve_made, at(dve_made, "chosen"))
            dst = accumulator("places", dve_evacuated)
            chosen = R[:, R_M:R_M + 64]
            for i in range(QT):
                for j in range(i + 1):
                    lhs = const[:, K_LT:K_LT + P] if j == i else ones[:, :]
                    nc.tensor.matmul(dst[:, 0, 16 * i:16 * i + 16], lhs, chosen[:, 16 * j:16 * j + 16],
                                     start=(j == 0), stop=(j == i))
            for j in range(QT):
                ins = nc.tensor.matmul(dst[:, 0, 64:80], ones[:, :], chosen[:, 16 * j:16 * j + 16],
                                       start=(j == 0), stop=(j == QT - 1))
            done(ins, "places")
            dst = accumulator("rows_of", dve_evacuated)
            for e in range(EXPERTS):
                pe.wait_ge(dve_made, at(dve_made, ("pick", e)))
                for i in range(QT):
                    ins = nc.tensor.matmul(dst[:, 0, e:e + 1], picks[e % 2][:, i, :],
                                           const[:, K_TOKEN + i:K_TOKEN + i + 1], start=(i == 0), stop=(i == QT - 1))
                ins.then_inc(picked, 1)
                mark(picked, ("pick", e))
            pe.wait_ge(picked, at(picked, ("pick", EXPERTS - 1)))
            done(pe.drain(), "rows_of")
            drained()

            BANK = {"g": acc[:, 0, 0, :], "u": acc[:, 0, 1, :], "ht": acc[:, 3, 0, :], "pick": acc[:, 3, 1, :]}
            TWO = {"xt": acc[:, 1, :, :], "y": acc[:, 2, :, :]}

            def turn_tokens(label, arrived):
                pe.wait_ge(x_gathered, arrived)
                for c in range(DC):
                    ins = nc.tensor.transpose(TWO["xt"].rearrange("p a b -> p (a b)")[:, c * P:(c + 1) * P],
                                              x_gath[:, c * P:(c + 1) * P], ident)
                done(ins, label)

            def hidden(over):
                for x, by in ("g", act_evacuated), ("u", dve_evacuated):
                    name = {"g": "gate", "u": "up"}[x] + over
                    pe.wait_ge(by, at(by, (x, over), back=1))
                    loaded(name)
                    for k in range(DC):
                        ins = nc.tensor.matmul(BANK[x], x_exp[:, k, :], weight(name)[:, k, :], start=(k == 0),
                                               stop=(k == DC - 1))
                    done(ins, (x, over))
                    free(name)

            def down(over):
                pe.wait_ge(dve_evacuated, at(dve_evacuated, ("u", over)))
                for k in range(HID // P):
                    ins = nc.tensor.transpose(BANK["ht"][:, k * P:(k + 1) * P], hid[:, k * P:(k + 1) * P], ident)
                done(ins, ("ht", over))
                pe.wait_ge(dve_evacuated, at(dve_evacuated, ("ht", over)))
                pe.wait_ge(act_evacuated, at(act_evacuated, ("y", over), back=1))
                loaded("down" + over)
                for half in range(2):
                    for k in range(HID // P):
                        ins = nc.tensor.matmul(TWO["y"][:, half, :], hid_t[:, k, :],
                                               weight("down" + over)[:, k, half * 512:(half + 1) * 512],
                                               start=(k == 0), stop=(k == HID // P - 1))
                done(ins, ("y", over))
                free("down" + over)

            turn_tokens("xt0", at(x_gathered, "x0"))
            pe.wait_ge(act_evacuated, at(act_evacuated, "xt0"))
            with pe.Fori(0, EXPERTS) as e:
                n.enter("experts", e, EXPERTS)
                pe.wait_ge(act_evacuated, at(act_evacuated, ("xt", ""), back=1))
                hidden("")
                turn_tokens(("xt", ""), at(x_gathered, ("x", "")))
                down("")
                n.leave()
            pe.wait_ge(dve_made, at(dve_made, "over"))
            pe.wait_ge(act_evacuated, at(act_evacuated, ("y", "")))
            tiles = pe.value_load(over_i[0:1, 0:1], min_val=0, max_val=OVER)
            with pe.If(tiles > 0):
                with pe.Fori(0, tiles) as k:
                    n.enter("over", k, 1)
                    pe.wait_ge(dve_made, at(dve_made, ("pick", "+")))
                    pe.sem_inc(held, 1)
                    for i in range(QT):
                        ins = nc.tensor.matmul(BANK["pick"][:, 0:1], picks[0][:, i, :],
                                               const[:, K_TOKEN + i:K_TOKEN + i + 1], start=(i == 0), stop=(i == QT - 1))
                    done(ins, ("pick", "+"))
                    turn_tokens(("xt", "+"), at(x_gathered, ("x", "+")))
                    pe.wait_ge(act_evacuated, at(act_evacuated, ("xt", "+")))
                    hidden("+")
                    down("+")
                    n.leave()

        @block.scalar
        def _(act):
            def result(label):
                act.wait_ge(psum_filled, at(psum_filled, label))
                slot = known.slots[label] if known else 0
                return acc[:, slot, :, 0:HALF]

            def flat2(x):
                return x.rearrange("p (a t) -> p a t", a=2)

            act.wait_ge(dve_made, at(dve_made, "angles"))
            nc.scalar.activation(sinT, krope[NOPE:QK, 0, :], ACT.Sin).then_inc(act_made, 1)
            mark(act_made)
            nc.scalar.activation(cosT, krope[NOPE:QK, 1, :], ACT.Sin, scale=-1.0,
                                 bias=small[NOPE:QK, 0:1]).then_inc(act_made, 1)
            mark(act_made, "trig")

            with act.Fori(0, LAYERS) as layer:
                n.enter("layer", layer, LAYERS)
                for c in range(DC):
                    act.wait_ge(dve_evacuated, at(dve_evacuated, ("x", DC - 1)) if known is None else
                                known.marks["dve_evacuated", ("x", DC - 1)][1]
                                + layer * known.per["layer", "dve_evacuated"])
                    nc.scalar.activation(work[:, c, :], hres[:, c, :], ACT.Square).then_inc(act_made, 1)
                    mark(act_made, ("sq", c))

                def root(label, dst, width, rows_=P):
                    src = result(label)
                    nc.scalar.activation(flat2(dst), src[0:rows_], ACT.Sqrt, scale=1.0 / width,
                                         bias=small[0:rows_, 1:2]).then_inc(act_evacuated, 1)
                    mark(act_evacuated, label)

                root("ss_h", work[:, 0, :], D)
                for c in range(QC + KC):
                    src = result(("c", c))
                    if c == 0:
                        act.wait_ge(dve_made, at(dve_made, ("h", DC - 1)))
                    nc.scalar.activation(flat2(work[:, c, :]), src, ACT.Square)
                    nc.scalar.activation(flat2(latent[:, c, :]), src, ACT.Copy).then_inc(act_evacuated, 1)
                    mark(act_evacuated, ("c", c))
                root("ss_cq", work[:, 0, :], QR)
                root("ss_ckv", work[:, 1, :], KVR)
                src = result("rope")
                for i in range(2):
                    ins = nc.scalar.activation(flat2(work[NOPE:QK, 2 + i, :]), src[NOPE:QK], ACT.Square)
                ins.then_inc(act_made, 1)
                mark(act_made, "sq_rope")
                for i, (t0, nt) in enumerate(TILES):
                    result(("v", i))
                    slot = known.slots["v", i] if known else 0
                    nc.scalar.activation(v[0:nt, i, :], acc[0:nt, slot, 0, :], ACT.Copy).then_inc(act_evacuated, 1)
                    mark(act_evacuated, ("v", i))

                def head(kind, hd, rows_, dst, sq):
                    src = result((kind, hd))
                    if hd >= 2:
                        act.wait_ge(psum_filled, at(psum_filled, (kind + "ss", hd - 2)))
                    nc.scalar.activation(flat2(sq), src[0:rows_], ACT.Square)
                    nc.scalar.activation(flat2(dst), src[0:rows_], ACT.Copy).then_inc(act_evacuated, 1)
                    mark(act_evacuated, (kind, hd))

                def head_root(kind, hd, tile):
                    if hd >= 1:
                        act.wait_ge(dve_made, at(dve_made, (kind + "n", hd - 1)))
                    elif kind == "k":
                        act.wait_ge(dve_made, at(dve_made, ("cn", QC + KC - 1)))
                    root((kind + "ss", hd), work[0:QK, tile, :], QK, QK)

                for hd in range(HEADS + 1):
                    if hd < HEADS:
                        if hd == 0:
                            act.wait_ge(pool_made, at(pool_made, ("krep", 0)))
                        head("k", hd, NOPE, kT[0:NOPE, hd, :], work[0:NOPE, 2 + hd % 2, :])
                        head("q", hd, QK, qT[0:QK, hd, :], work[0:QK, 4 + hd % 2, :])
                    if hd >= 1:
                        head_root("k", hd - 1, 0)
                        head_root("q", hd - 1, 1)

                def gate_free(x):
                    i = gate_no[x]
                    if i >= 2:
                        y = gate_reader(gate_order[i - 2])
                        s_ = dve_evacuated if y[0] in ("z", "yp") else dve_made
                        act.wait_ge(s_, at(s_, y))
                    return gate[:, i % 2, :]

                def back(x):
                    if x[0] in ("z", "gp"):
                        src = result(x)
                        dst = gate_free(x)
                        ins = nc.scalar.activation(flat2(dst), src, ACT.Tanh, scale=0.5)
                        if x[0] == "z":
                            ins.then_inc(act_made, 1)
                            mark(act_made, ("tanh",) + x)
                        else:
                            ins.then_inc(act_evacuated, 1)
                            mark(act_evacuated, x)

                for s in range(STEPS):
                    if s < len(items):
                        hd, i = items[s]
                        t0, nt = TILES[i]
                        result(("s", s))
                        slot = known.slots["s", s] if known else 0
                        act.wait_ge(dve_made, at(dve_made, ("max", s)))
                        if s >= 3:
                            act.wait_ge(psum_filled, at(psum_filled, ("t", s - 3)))
                        nc.scalar.activation(
                            probs[s % 3][0:nt, 0:t0 + nt],
                            acc[0:nt, slot, :, :].rearrange("p a b -> p (a b)")[:, 0:t0 + nt],
                            ACT.Exp, scale=SCALE1, bias=small[0:nt, 2 + s % 3:3 + s % 3],
                            accum_out=small[0:nt, 5 + s % 3:6 + s % 3]).then_inc(act_evacuated, 1)
                        mark(act_evacuated, ("s", s))
                    for x in background_at(s):
                        back(x)
                    if 2 <= s < len(items) + 2:
                        hd, i = items[s - 2]
                        nt = TILES[i][1]
                        result(("t", s - 2))
                        slot = known.slots["t", s - 2] if known else 0
                        src = acc[:, slot, :, :].rearrange("p a (b q) -> p (a b) q", q=P)
                        if s >= 4:
                            act.wait_ge(psum_filled, at(psum_filled, ("o", s - 4)))
                        ins = nc.scalar.activation(probsT[s % 2][0:META, 0, 0:nt], src[0:META, 0, 0:nt], ACT.Copy)
                        if i:
                            ins = nc.scalar.activation(probsT[s % 2][:, 1:i + 1, 0:nt], src[:, 1:i + 1, 0:nt], ACT.Copy)
                        ins.then_inc(act_evacuated, 1)
                        mark(act_evacuated, ("t", s - 2))
                    if s >= 3:
                        hd, i = items[s - 3]
                        t0, nt = TILES[i]
                        result(("o", s - 3))
                        slot = known.slots["o", s - 3] if known else 0
                        r = VD * (hd % 2)
                        nc.scalar.activation(o[r:r + VD, hd // 2, t0:t0 + nt], acc[r:r + VD, slot, 0, 0:nt],
                                             ACT.Copy).then_inc(act_evacuated, 1)
                        mark(act_evacuated, ("o", s - 3))

                for c in range(PG):
                    src = result(("zm", c))
                    nc.scalar.activation(flat2(gate_free(("zm", c))), src, ACT.Tanh, scale=0.5).then_inc(act_made, 1)
                    mark(act_made, ("tanh", "zm", c))
                for m in range(DC):
                    src = result(("gm", m))
                    nc.scalar.activation(flat2(gate_free(("gm", m))), src, ACT.Tanh, scale=0.5)\
                        .then_inc(act_evacuated, 1)
                    mark(act_evacuated, ("gm", m))
                n.leave()

            def result2(label):
                act.wait_ge(psum_filled, at(psum_filled, label))
                return acc[:, known.slots[label] if known else 0, 0, :]

            def evacuated(ins, label):
                ins.then_inc(act_evacuated, 1)
                mark(act_evacuated, label)

            def made(ins, label):
                ins.then_inc(act_made, 1)
                mark(act_made, label)

            def root2(label, dst, width):
                evacuated(nc.scalar.activation(dst, result2(label), ACT.Sqrt, scale=1.0 / width,
                                               bias=small[:, 1:2]), label)

            act.wait_ge(dve_evacuated, at(dve_evacuated, ("out", DC - 1)))
            for c in range(DC):
                made(nc.scalar.activation(merged[:, c, :], xr[:, c, :], ACT.Square), ("sq1", c))
            root2("ss_1", tmp[2], D)
            for c in range(2 * DC + 1):
                if c < 2 * DC:
                    src = result2(("qk", c))
                    if c >= 2:
                        act.wait_ge(psum_filled, at(psum_filled, ("qkss", c - 2)))
                    nc.scalar.activation(tmp[c % 2], src, ACT.Square)
                    evacuated(nc.scalar.activation(qk[:, c, 0:S], src, ACT.Copy), ("qk", c))
                if c >= 1:
                    i = c - 1
                    if i < 2:
                        act.wait_ge(dve_made, at(dve_made, ("h1", DC - 1)))
                    else:
                        act.wait_ge(dve_made, at(dve_made, ("qkn", i - 2)))
                    root2(("qkss", i), tmp[2 + i % 2], SUB)
            for g in range(2):
                for j in range(QT):
                    if g == j == 0:
                        act.wait_ge(psum_filled, at(psum_filled, "ss_1"))
                    evacuated(nc.scalar.activation(v2[:, j, g * S:(g + 1) * S], result2(("v2", g, j)), ACT.Copy),
                              ("v2", g, j))
            act.wait_ge(dve_made, at(dve_made, "lam_sums"))
            made(nc.scalar.activation(small[:, 10:12], small[:, 8:10], ACT.Exp), "lam_exp")
            for s in range(STEPS2):
                if s < len(items2):
                    act.wait_ge(psum_filled, at(psum_filled, ("s2", s)))
                    act.wait_ge(dve_made, at(dve_made, ("max2", s)))
                    if s >= 2:
                        act.wait_ge(psum_filled, at(psum_filled, ("t2", s - 2)))
                    slot = known.slots["s2", s] if known else 0
                    for c in range(2):
                        b = 2 * (s % 2) + c
                        ins = nc.scalar.activation(probs2[s % 2][c], acc[:, slot, c, :], ACT.Exp, scale=SCALE2,
                                                   bias=rt[:, 0, b:b + 1], accum_out=rt[:, 0, 4 + b:5 + b])
                    evacuated(ins, ("s2", s))
                for c in background2_at(s):
                    evacuated(nc.scalar.activation(lru_x[:, c, 1:1 + S], result2(("lx", c)), ACT.Copy), ("lx", c))
                if 1 <= s <= len(items2):
                    src = result2(("t2", s - 1)).rearrange("p (j q) -> p j q", j=QT)
                    if s >= 5:
                        act.wait_ge(psum_filled, at(psum_filled, ("o2", s - 5)))
                    evacuated(nc.scalar.activation(probsT2[(s - 1) % 4], src, ACT.Copy), ("t2", s - 1))
                if s >= 2:
                    hd, i = items2[s - 2]
                    evacuated(nc.scalar.activation(q2[:, hd, i * P:(i + 1) * P], result2(("o2", s - 2))[:, 0:P],
                                                   ACT.Copy), ("o2", s - 2))
            act.wait_ge(dve_made, at(dve_made, "neg_abs"))
            made(nc.scalar.activation(decay[:, 1, :], decay[:, 1, :], ACT.Exp), "lam_e")
            for c in range(DC):
                evacuated(nc.scalar.activation(gelu[c], result2(("lg", c)), ACT.Gelu_apprx_tanh), ("lg", c))
            for c in range(DC + 1):
                if c < DC:
                    if c >= 2:
                        act.wait_ge(psum_filled, at(psum_filled, ("oss", c - 2)))
                    act.wait_ge(act_evacuated, at(act_evacuated, ("lg", DC - 1)))
                    made(nc.scalar.activation(tmp[c % 2], q2[:, c, :], ACT.Square), ("sqo", c))
                if c >= 1:
                    if c >= 3:
                        act.wait_ge(dve_made, at(dve_made, ("on", c - 3)))
                    elif c == 1:
                        act.wait_ge(pool_made, at(pool_made, ("conv", DC - 1)))
                    root2(("oss", c - 1), tmp[2 + (c - 1) % 2], P)

            def lru_gates(u):
                d, c = lru_units[u]
                act.wait_ge(psum_filled, at(psum_filled, ("lru", u)))
                slot = known.slots["lru", u] if known else 0
                if u:
                    act.wait_ge(dve_made, at(dve_made, ("lru_in", u - 1)))
                else:
                    act.wait_ge(dve_made, at(dve_made, ("on", DC - 1)))
                b = V_BA - V_BG + 8 * d + c
                nc.scalar.activation(tmp[0], acc[:, slot, 0, :], ACT.Tanh, scale=0.5, bias=half_bias[:, b:b + 1])
                b += V_BI - V_BA
                evacuated(nc.scalar.activation(tmp[1], acc[:, slot, 1, :], ACT.Tanh, scale=0.5,
                                               bias=half_bias[:, b:b + 1]), ("lru", u))
                act.wait_ge(dve_made, at(dve_made, ("lru_z", u)))
                if u >= 4:
                    act.wait_ge(dve_made, at(dve_made, ("scan", u - 4)))
                made(nc.scalar.activation(unit_tiles(u)[0], tmp[2], ACT.Exp, scale=-1.0), ("lru_a", u))
                made(nc.scalar.activation(tmp[3], tmp[2], ACT.Tanh), ("lru_t", u))

            def gate2(label, col, i):
                src = result2(label)
                if i >= 2:
                    before = ("mg2" if label[0] == "gl" or i >= 2 and False else "x", 0)
                if i == 1 or i == 0:
                    act.wait_ge(psum_filled, at(psum_filled, ("t2", len(items2) - 1)))
                if label[0] == "ga" and i >= 2:
                    act.wait_ge(dve_evacuated, at(dve_evacuated, ("ya", i - 2)))
                elif label[0] == "gl":
                    j = i - DC
                    if j < 2:
                        act.wait_ge(dve_evacuated, at(dve_evacuated, ("ya", DC - 2 + j)))
                    else:
                        act.wait_ge(dve_made, at(dve_made, ("mg2", j - 2)))
                evacuated(nc.scalar.activation(gate[:, i % 2, 0:S], src, ACT.Tanh, scale=0.5,
                                               bias=half_bias[:, col:col + 1]), label)

            for m in range(DC):
                gate2(("ga", m), m, m)
                lru_gates(2 * m)
                lru_gates(2 * m + 1)
                if m % 2 == 1:
                    for u in range(4 * (m // 2), 4 * (m // 2) + 4):
                        act.wait_ge(dve_made, at(dve_made, ("lru_f", u)))
                        made(nc.scalar.activation(unit_tiles(u)[2], unit_tiles(u)[2], ACT.Sqrt, scale=0.5),
                             ("lru_m", u))
            for m in range(DC):
                gate2(("gl", m), DC + m, DC + m)
            act.wait_ge(dve_evacuated, at(dve_evacuated, ("out2", DC - 1)))
            for c in range(DC):
                made(nc.scalar.activation(merged[:, c, :], xr[:, c, :], ACT.Square), ("sq2", c))
            root2("ss_2", tmp[2], D)

            def both(label):
                act.wait_ge(psum_filled, at(psum_filled, label))
                return acc[:, known.slots[label] if known else 0, :, :].rearrange("p a b -> p (a b)")

            for i in range(QT):
                evacuated(nc.scalar.activation(x_tok[:, i, :], both(("x_tok", i)), ACT.Copy), ("x_tok", i))
            act.wait_ge(dve_made, at(dve_made, "shifted"))
            made(nc.scalar.activation(R[:, R_X:R_X + 80], R[:, R_X:R_X + 80], ACT.Exp), "shares")
            for i in range(QT):
                evacuated(nc.scalar.activation(h_tok[:, i, :], both(("h_tok", i)), ACT.Copy), ("h_tok", i))

            def turned(label):
                act.wait_ge(psum_filled, at(psum_filled, label))
                evacuated(nc.scalar.activation(x_exp, acc[:, 1, :, :].rearrange("p a (k s) -> p (a k) s", s=P),
                                               ACT.Copy), label)

            def gated(over):
                act.wait_ge(psum_filled, at(psum_filled, ("g", over)))
                act.wait_ge(dve_evacuated, at(dve_evacuated, ("ht", over), back=1))
                evacuated(nc.scalar.activation(hid, acc[:, 0, 0, :], ACT.Silu), ("g", over))

            def results(over, row):
                act.wait_ge(psum_filled, at(psum_filled, ("y", over)))
                act.wait_ge(y_stored, at(y_stored, ("y", over), back=1))
                evacuated(nc.scalar.activation(y_out, acc[:, 2, :, :].rearrange("p a b -> p (a b)"), ACT.Copy),
                          ("y", over))
                act.wait_ge(act_evacuated, at(act_evacuated, ("y", over)))
                act.sem_inc(held, 1)
                act.dma_start(y_rows[bass.ds(row, P), :], y_out).then_inc(y_stored, 16)
                mark(y_stored, ("y", over), 16)

            act.sem_inc(y_stored, 1)
            mark(y_stored)
            turned("xt0")
            act.wait_ge(act_evacuated, at(act_evacuated, "xt0"))
            act.sem_inc(turned_x, 1)
            with act.Fori(0, EXPERTS) as e:
                n.enter("experts", e, EXPERTS)
                gated("")
                turned(("xt", ""))
                act.wait_ge(act_evacuated, at(act_evacuated, ("xt", "")))
                act.sem_inc(turned_x, 1)
                results("", e * P)
                n.leave()
            act.wait_ge(y_zeroed, 16 * OVER)
            act.wait_ge(dve_made, at(dve_made, "over"))
            tiles = act.value_load(over_i[0:1, 0:1], min_val=0, max_val=OVER)
            with act.If(tiles > 0):
                with act.Fori(0, tiles) as k:
                    n.enter("over", k, 1)
                    turned(("xt", "+"))
                    gated("+")
                    results("+", k * P + EXPERTS * P)
                    n.leave()
            act.wait_ge(y_stored, tiles * 16 + (1 + 16 * EXPERTS))
            act.sem_inc(all_stored, 1)

        @block.vector
        def _(dve):
            def result(label):
                dve.wait_ge(psum_filled, at(psum_filled, label))
                slot = known.slots[label] if known else 0
                return acc[:, slot, :, 0:HALF]

            def flat2(x):
                return x.rearrange("p (a t) -> p a t", a=2)

            def chain(ins):
                ins.then_inc(dve_step, 1)
                mark(dve_step)
                dve.wait_ge(dve_step, now(dve_step))

            def made(ins, label):
                ins.then_inc(dve_made, 1)
                mark(dve_made, label)

            def evacuated(ins, label):
                ins.then_inc(dve_evacuated, 1)
                mark(dve_evacuated, label)

            stt, ts = nc.vector.scalar_tensor_tensor, nc.vector.tensor_scalar
            nc.vector.memset(small[:, 0:1], math.pi / 2)
            nc.vector.memset(small[:, 1:2], EPS)
            nc.vector.memset(upad[:, :, 0:PAD], 0.0)
            dve.wait_ge(const_loaded, 16)
            dve.wait_ge(vec_loaded, at(vec_loaded, "positions"))
            ang, turns = trig[NOPE:QK, 0, :], trig[NOPE:QK, 1, :]
            nc.vector.tensor_copy(ang[:, 0:META], const[NOPE:QK, K_META:K_META + META])
            chain(nc.vector.tensor_copy(ang[:, META:T], krope[NOPE:QK, 0, META:T].bitcast(I32)))
            chain(ts(ang[:, META:T], ang[:, META:T], float(META), None, ALU.add))
            chain(ts(ang, ang, const[NOPE:QK, K_FREQ:K_FREQ + 1], None, ALU.mult))
            big = 1.5 * 2 ** 23
            chain(ts(turns, ang, 1.0 / (2 * math.pi), big, ALU.mult, ALU.add))
            chain(ts(turns, turns, -big, None, ALU.add))
            rest, parts = 2 * math.pi, []
            for bits in (8, 12, 24):
                e = 2.0 ** (bits - 1 - math.floor(math.log2(abs(rest))))
                parts.append(math.trunc(rest * e) / e if bits < 24 else rest)
                rest -= parts[-1]
            for part in parts:
                chain(stt(out=ang, in0=turns, scalar=-part, in1=ang, op0=ALU.mult, op1=ALU.add))
            chain(ts(krope[NOPE:QK, 0, :], ang, 3.1415925, -3.1415925, ALU.min, ALU.max))
            dve.wait_ge(dve_step, now(dve_step))
            made(stt(out=krope[NOPE:QK, 1, :], in0=krope[NOPE:QK, 0, :], scalar=-1.0,
                     in1=krope[NOPE:QK, 0, :], op0=ALU.mult, op1=ALU.max), "angles")

            result("vecs")
            slot = known.slots["vecs"] if known else 0
            evacuated(nc.vector.tensor_copy(vecs[:, :], acc[:, slot, 0, 0:LAYERS * LV]), "vecs")
            result("vec2")
            slot = known.slots["vec2"] if known else 0
            evacuated(nc.vector.tensor_copy(vec2[:, :], acc[:, slot, 0, 0:V_END]), "vec2")
            dve.wait_ge(dve_evacuated, at(dve_evacuated, "vec2"))
            made(ts(half_bias[:, :], vec2[:, V_BG:V_LM], 0.5, None, ALU.mult), "half_bias")
            for c in range(DC):
                result(("x", c))
                slot = known.slots["x", c] if known else 0
                nc.vector.tensor_copy(hres[:, c, 0:META], acc[:, slot, 1, 0:META])
                evacuated(nc.vector.tensor_copy(hres[:, c, META:T], acc[:, slot, 0, :]), ("x", c))

            dve.wait_ge(dve_evacuated, at(dve_evacuated, ("x", DC - 1)))
            with dve.Fori(0, LAYERS) as layer:
                n.enter("layer", layer, LAYERS)
                chain(nc.vector.tensor_copy(lv[:, :], vecs[:, bass.ds(layer * LV, LV)]))
                chain(nc.vector.tensor_copy(small[:, 8:9], lv[:, 21:22]))
                chain(nc.vector.memset(small[NOPE:QK, 8:9], 1.0))

                def inverse(label, tile, rows_=P):
                    dve.wait_ge(act_evacuated, at(act_evacuated, label))
                    chain(nc.vector.reciprocal(work[0:rows_, tile, :], work[0:rows_, tile, :]))

                inverse("ss_h", 0)
                for c in range(DC):
                    made(stt(out=h[:, c, :], in0=hres[:, c, :], scalar=lv[:, c:c + 1], in1=work[:, 0, :],
                             op0=ALU.mult, op1=ALU.mult), ("h", c))
                for g in range(PG):
                    src = result(("u", g))
                    evacuated(nc.vector.tensor_copy(flat2(upad[:, g, PAD:]), src), ("u", g))
                for label, tile, c0, c1 in (("ss_cq", 0, 0, QC), ("ss_ckv", 1, QC, QC + KC)):
                    inverse(label, tile)
                    for c in range(c0, c1):
                        made(stt(out=latent[:, c, :], in0=latent[:, c, :], scalar=lv[:, 8 + c:9 + c],
                                 in1=work[:, tile, :], op0=ALU.mult, op1=ALU.mult), ("cn", c))
                src = result("rope")
                dve.wait_ge(act_made, at(act_made, "sq_rope"))
                dve.wait_ge(act_made, at(act_made, "trig"))
                evacuated(ts(flat2(krope[NOPE:QK, 0, :]), src[NOPE:QK], lv[NOPE:QK, 21:22], None, ALU.mult), "rope")
                src = result("rotk")
                evacuated(nc.vector.tensor_tensor(flat2(krope[NOPE:QK, 1, :]), src[NOPE:QK], flat2(sinT), ALU.mult),
                          "rotk")
                chain(nc.vector.tensor_tensor(krope[NOPE:QK, 0, :], krope[NOPE:QK, 0, :], cosT, ALU.mult))
                dve.wait_ge(dve_evacuated, at(dve_evacuated, "rotk"))
                made(nc.vector.tensor_tensor(krope[NOPE:QK, 0, :], krope[NOPE:QK, 0, :], krope[NOPE:QK, 1, :],
                                             ALU.add), "kR")
                for g in range(PG):
                    w = 2 ** (g + 1)
                    dve.wait_ge(pool_made, at(pool_made, ("window", g)))
                    win_ = winA if g % 2 == 0 else winB
                    first = const[:, K_CNT + g * PAD:K_CNT + (g + 1) * PAD]
                    chain(nc.vector.tensor_tensor(win_[:, PAD:2 * PAD], win_[:, PAD:2 * PAD], first, ALU.mult))
                    nc.vector.tensor_tensor(upad[:, g, PAD:2 * PAD], win_[:, PAD:2 * PAD],
                                            upad[:, g, PAD:2 * PAD], ALU.subtract)
                    made(stt(out=upad[:, g, 2 * PAD:], in0=win_[:, 2 * PAD:], scalar=1.0 / w,
                             in1=upad[:, g, 2 * PAD:], op0=ALU.mult, op1=ALU.subtract), ("mixed", g))

                def k_norm(hd):
                    inverse(("kss", hd), 0, QK)
                    dve.wait_ge(pool_made, at(pool_made, ("krep", hd)))
                    made(stt(out=kT[0:QK, hd, :], in0=kT[0:QK, hd, :], scalar=small[0:QK, 8:9],
                             in1=work[0:QK, 0, :], op0=ALU.mult, op1=ALU.mult), ("kn", hd))

                def q_norm(hd):
                    inverse(("qss", hd), 1, QK)
                    made(stt(out=qT[0:QK, hd, :], in0=qT[0:QK, hd, :], scalar=lv[0:QK, 20:21],
                             in1=work[0:QK, 1, :], op0=ALU.mult, op1=ALU.mult), ("qn", hd))

                def q_rope(hd):
                    src = result(("rotq", hd))
                    turned = work[NOPE:QK, 6, :]
                    if hd:
                        dve.wait_ge(dve_made, at(dve_made, ("qr", hd - 1)))
                    evacuated(nc.vector.tensor_tensor(flat2(turned), src[NOPE:QK], flat2(sinT), ALU.mult),
                              ("rotq", hd))
                    chain(nc.vector.tensor_tensor(qT[NOPE:QK, hd, :], qT[NOPE:QK, hd, :], cosT, ALU.mult))
                    dve.wait_ge(dve_evacuated, at(dve_evacuated, ("rotq", hd)))
                    made(nc.vector.tensor_tensor(qT[NOPE:QK, hd, :], qT[NOPE:QK, hd, :], turned, ALU.add),
                         ("qr", hd))

                for hd in range(HEADS + 1):
                    if hd < HEADS:
                        k_norm(hd)
                        q_norm(hd)
                    if hd >= 1:
                        q_rope(hd - 1)

                def back(x):
                    kind, m = x
                    src = result(x) if kind != "gp" else None
                    if kind == "z":
                        dve.wait_ge(act_made, at(act_made, ("tanh",) + x))
                        evacuated(stt(out=flat2(zp[:, m, :]), in0=flat2(gate[:, gate_no[x] % 2, :]), scalar=1.0,
                                      in1=src, op0=ALU.add, op1=ALU.mult), x)
                    elif kind == "pg":
                        dve.wait_ge(dve_evacuated, at(dve_evacuated, ("z", m)))
                        evacuated(stt(out=flat2(zp[:, m, :]), in0=src, scalar=lv[:, 16 + m:17 + m],
                                      in1=flat2(zp[:, m, :]), op0=ALU.mult, op1=ALU.mult), x)
                    elif kind == "yp":
                        dve.wait_ge(act_evacuated, at(act_evacuated, ("gp", m)))
                        if m == 0:
                            dve.wait_ge(dve_made, at(dve_made, ("qr", HEADS - 1)))
                        g = gate[:, gate_no["gp", m] % 2, :]
                        evacuated(stt(out=flat2(work[:, m, :]), in0=flat2(g), scalar=1.0, in1=src,
                                      op0=ALU.add, op1=ALU.mult), x)

                def normalise(s):
                    hd, i = items[s]
                    t0, nt = TILES[i]
                    r = small[0:nt, 5 + s % 3:6 + s % 3]
                    dve.wait_ge(act_evacuated, at(act_evacuated, ("s", s)))
                    chain(nc.vector.reciprocal(r, r))
                    made(ts(probs[s % 3][0:nt, 0:t0 + nt], probs[s % 3][0:nt, 0:t0 + nt], r, None, ALU.mult),
                         ("p", s))

                for s in range(STEPS):
                    if s < len(items):
                        hd, i = items[s]
                        t0, nt = TILES[i]
                        result(("s", s))
                        slot = known.slots["s", s] if known else 0
                        src = acc[0:nt, slot, :, :].rearrange("p a b -> p (a b)")
                        top = small[0:nt, 2 + s % 3:3 + s % 3]
                        chain(nc.vector.tensor_tensor(src[:, t0:t0 + nt], src[:, t0:t0 + nt], mask[0:nt, 0:nt],
                                                      ALU.add))
                        chain(nc.vector.tensor_reduce(top, src[:, 0:t0 + nt], AX.X, ALU.max))
                        made(ts(top, top, -SCALE1, None, ALU.mult), ("max", s))
                    if 1 <= s <= len(items):
                        normalise(s - 1)
                    for x in background_at(s):
                        back(x)

                for c in range(PG):
                    src = result(("zm", c))
                    dve.wait_ge(act_made, at(act_made, ("tanh", "zm", c)))
                    g = gate[:, gate_no["zm", c] % 2, :]
                    evacuated(stt(out=flat2(g), in0=flat2(g), scalar=1.0, in1=src, op0=ALU.add, op1=ALU.mult),
                              ("zm", c))
                    dve.wait_ge(dve_evacuated, at(dve_evacuated, ("zm", c)))
                    if c == 0:
                        dve.wait_ge(act_evacuated, at(act_evacuated, ("o", len(items) - 1)))
                    made(nc.vector.tensor_tensor(o[:, c, :], o[:, c, :], g, ALU.mult), ("og", c))
                for m in range(DC):
                    src = result(("ym", m))
                    dve.wait_ge(act_evacuated, at(act_evacuated, ("gm", m)))
                    g = gate[:, gate_no["gm", m] % 2, :]
                    evacuated(stt(out=flat2(g), in0=flat2(g), scalar=1.0, in1=src, op0=ALU.add, op1=ALU.mult),
                              ("ym", m))
                    dve.wait_ge(dve_evacuated, at(dve_evacuated, ("ym", m)))
                    made(nc.vector.tensor_tensor(work[:, m, :], work[:, m, :], g, ALU.add), ("mg", m))
                for m in range(DC):
                    src = result(("out", m))
                    evacuated(stt(out=flat2(hres[:, m, :]), in0=src, scalar=0.25, in1=flat2(hres[:, m, :]),
                                  op0=ALU.mult, op1=ALU.add), ("out", m))
                dve.wait_ge(dve_evacuated, at(dve_evacuated, ("out", DC - 1)))
                n.leave()

            def result2(label):
                dve.wait_ge(psum_filled, at(psum_filled, label))
                return acc[:, known.slots[label] if known else 0, 0, :]

            tt = nc.vector.tensor_tensor

            def inverse2(label, tile):
                dve.wait_ge(act_evacuated, at(act_evacuated, label))
                chain(nc.vector.reciprocal(tmp[tile], tmp[tile]))

            inverse2("ss_1", 2)
            for c in range(DC):
                made(stt(out=h2[:, c, :], in0=xr[:, c, :], scalar=vec2[:, V_N1 + c:V_N1 + c + 1], in1=tmp[2],
                         op0=ALU.mult, op1=ALU.mult), ("h1", c))
            dve.wait_ge(const_loaded, at(const_loaded, "rotary"))

            def qk_turned(c):
                src = result2(("qkrot", c))
                x = qk[:, c, 0:S]
                if c:
                    dve.wait_ge(dve_made, at(dve_made, ("qkr", c - 1)))
                evacuated(tt(tmp[4], src, sin2, ALU.mult), ("qkrot", c))
                chain(tt(x, x, cos2, ALU.mult))
                dve.wait_ge(dve_evacuated, at(dve_evacuated, ("qkrot", c)))
                made(tt(x, x, tmp[4], ALU.add), ("qkr", c))

            for c in range(2 * DC + 1):
                if c < 2 * DC:
                    x = qk[:, c, 0:S]
                    g = V_QN if c < DC else V_KN
                    inverse2(("qkss", c), 2 + c % 2)
                    made(stt(out=x, in0=x, scalar=vec2[:, g:g + 1], in1=tmp[2 + c % 2], op0=ALU.mult,
                             op1=ALU.mult), ("qkn", c))
                if c >= 1:
                    qk_turned(c - 1)
            for i in range(2):
                x, y = lamt[:, 2 * i * SUB:(2 * i + 1) * SUB], lamt[:, (2 * i + 1) * SUB:(2 * i + 2) * SUB]
                chain(tt(x, x, y, ALU.mult))
                ins = nc.vector.tensor_reduce(small[:, 8 + i:9 + i], x, AX.X, ALU.add)
            made(ins, "lam_sums")
            dve.wait_ge(act_made, at(act_made, "lam_exp"))
            chain(tt(small[:, 12:13], small[:, 11:12], small[:, 10:11], ALU.subtract))
            chain(ts(small[:, 12:13], small[:, 12:13], -LAM_INIT, None, ALU.add))
            nc.vector.memset(lru_x[:, :, 0:1], 0.0)
            made(nc.vector.memset(lru_x[:, :, 1 + S:3 + S], 0.0), "lru_pad")

            def weigh(s):
                dve.wait_ge(act_evacuated, at(act_evacuated, ("s2", s)))
                b = 4 + 2 * (s % 2)
                chain(nc.vector.reciprocal(rt[:, 0, b:b + 2], rt[:, 0, b:b + 2]))
                chain(ts(rt[:, 0, b + 1:b + 2], rt[:, 0, b + 1:b + 2], small[:, 12:13], None, ALU.mult))
                p0, p1 = probs2[s % 2]
                chain(ts(p1, p1, rt[:, 0, b + 1:b + 2], None, ALU.mult))
                made(stt(out=p0, in0=p0, scalar=rt[:, 0, b:b + 1], in1=p1, op0=ALU.mult, op1=ALU.add), ("p2", s))

            for s in range(STEPS2):
                if s < len(items2):
                    dve.wait_ge(psum_filled, at(psum_filled, ("s2", s)))
                    slot = known.slots["s2", s] if known else 0
                    b = 2 * (s % 2)
                    chain(nc.vector.tensor_reduce(rt[:, 0, b:b + 2], acc[:, slot, :, :], AX.X, ALU.max))
                    made(ts(rt[:, 0, b:b + 2], rt[:, 0, b:b + 2], -SCALE2, None, ALU.mult), ("max2", s))
                if 1 <= s <= len(items2):
                    weigh(s - 1)

            lam = vec2[:, V_LM:V_LM + 16]
            d_ = [decay[:, i, :] for i in range(6)]
            chain(ts(d_[0], lam, -1.0, None, ALU.mult))
            made(tt(d_[1], d_[0], lam, ALU.min), "neg_abs")
            dve.wait_ge(act_made, at(act_made, "lam_e"))
            chain(ts(d_[2], d_[1], 2.0, None, ALU.add))
            chain(nc.vector.reciprocal(d_[2], d_[2]))
            chain(tt(d_[2], d_[2], d_[1], ALU.mult))
            chain(tt(d_[3], d_[2], d_[2], ALU.mult))
            chain(ts(d_[4], d_[3], 1.0 / 17, 1.0 / 15, ALU.mult, ALU.add))
            for i in range(13, 0, -2):
                chain(tt(d_[4], d_[4], d_[3], ALU.mult))
                chain(ts(d_[4], d_[4], 1.0 / i, None, ALU.add))
            chain(tt(d_[4], d_[4], d_[2], ALU.mult))
            chain(ts(d_[0], d_[0], 0.0, 4.0, ALU.max, ALU.mult))
            chain(stt(out=d_[5], in0=d_[4], scalar=8.0, in1=d_[0], op0=ALU.mult, op1=ALU.add))

            for c in range(DC):
                if c >= 2:
                    dve.wait_ge(pool_made, at(pool_made, ("conv", c - 2)))
                elif c == 0:
                    dve.wait_ge(act_evacuated, at(act_evacuated, ("lx", DC - 1)))
                y = tmp[2 + c % 2]
                for j in range(TAPS):
                    x, w = lru_x[:, c, j:j + S], vec2[:, V_CW + 8 * j + c:V_CW + 8 * j + c + 1]
                    if j == 0:
                        chain(ts(y, x, w, vec2[:, V_CB + c:V_CB + c + 1], ALU.mult, ALU.add))
                    elif j < TAPS - 1:
                        chain(stt(out=y, in0=x, scalar=w, in1=y, op0=ALU.mult, op1=ALU.add))
                    else:
                        made(stt(out=y, in0=x, scalar=w, in1=y, op0=ALU.mult, op1=ALU.add), ("conv", c))
            for c in range(DC):
                inverse2(("oss", c), 2 + c % 2)
                if c == 0:
                    chain(ts(small[:, 13:14], vec2[:, V_SUB:V_SUB + 1], 1.0 - LAM_INIT, None, ALU.mult))
                made(stt(out=q2[:, c, :], in0=q2[:, c, :], scalar=small[:, 13:14], in1=tmp[2 + c % 2],
                         op0=ALU.mult, op1=ALU.mult), ("on", c))

            def lru_unit(u):
                d, c = lru_units[u]
                dve.wait_ge(act_evacuated, at(act_evacuated, ("lru", u)))
                if u:
                    dve.wait_ge(act_made, at(act_made, ("lru_t", u - 1)))
                made(ts(tmp[2], tmp[0], 1.0, decay[:, 5, 8 * d + c:8 * d + c + 1], ALU.add, ALU.mult), ("lru_z", u))
                made(stt(out=unit_tiles(u)[1], in0=tmp[1], scalar=1.0, in1=lru_x[:, c, 0:S], op0=ALU.add,
                         op1=ALU.mult), ("lru_in", u))
                dve.wait_ge(act_made, at(act_made, ("lru_t", u)))
                f = unit_tiles(u)[2]
                chain(ts(f, tmp[3], 1.0, None, ALU.add))
                chain(nc.vector.reciprocal(f, f))
                made(tt(f, f, tmp[3], ALU.mult), ("lru_f", u))

            def lru_scan(u):
                d, c = lru_units[u]
                a_, x_, m_ = unit_tiles(u)
                dve.wait_ge(act_made, at(act_made, ("lru_m", u)))
                chain(tt(x_, x_, m_, ALU.mult))
                back_ = slice(None, None, -1 if d else 1)
                made(nc.vector.tensor_tensor_scan(m_[:, back_], a_[:, back_], x_[:, back_], 0.0, ALU.mult,
                                                  ALU.add), ("scan", u))
                if d:
                    f_ = unit_tiles(u - 2)[2]
                    dve.wait_ge(dve_made, at(dve_made, ("scan", u)))
                    chain(tt(m_, m_, f_, ALU.add))
                    made(tt(gelu[c], gelu[c], m_, ALU.mult), ("lru_y", c))

            def weighed(label, gate_label, i, dst):
                src = result2(label)
                dve.wait_ge(act_evacuated, at(act_evacuated, gate_label))
                evacuated(stt(out=dst, in0=gate[:, i % 2, 0:S], scalar=1.0, in1=src, op0=ALU.add, op1=ALU.mult),
                          label)

            for m in range(DC):
                if m == 0:
                    dve.wait_ge(act_evacuated, at(act_evacuated, ("o2", len(items2) - 1)))
                weighed(("ya", m), ("ga", m), m, merged[:, m, :])
                lru_unit(2 * m)
                lru_unit(2 * m + 1)
                if m % 2 == 1:
                    for u in range(4 * (m // 2), 4 * (m // 2) + 4):
                        lru_scan(u)
            for m in range(DC):
                weighed(("yl", m), ("gl", m), m, gate[:, m % 2, 0:S])
                dve.wait_ge(dve_evacuated, at(dve_evacuated, ("yl", m)))
                made(tt(merged[:, m, :], merged[:, m, :], gate[:, m % 2, 0:S], ALU.add), ("mg2", m))
            for m in range(DC):
                evacuated(stt(out=xr[:, m, :], in0=result2(("out2", m)), scalar=0.5, in1=xr[:, m, :],
                              op0=ALU.mult, op1=ALU.add), ("out2", m))
            inverse2("ss_2", 2)
            for c in range(DC):
                made(stt(out=h2[:, c, :], in0=xr[:, c, :], scalar=vec2[:, V_N2 + c:V_N2 + c + 1], in1=tmp[2],
                         op0=ALU.mult, op1=ALU.mult), ("h3", c))

            def r(at_, *dims):
                x = R[:, at_:at_ + math.prod(dims)]
                return x if len(dims) == 1 else x.rearrange("p (a b) -> p a b", a=dims[0])

            def spread(x, count):
                return x.unsqueeze(2).to_broadcast([P, x.shape[1], count])

            src = result2("logits")[:, 0:80].rearrange("p (i n) -> p i n", i=QT)
            evacuated(tt(logits[:, :, :], src, router_bias[:, :].unsqueeze(1).to_broadcast([P, QT, 20]), ALU.add),
                      "logits")
            dve.wait_ge(dve_evacuated, at(dve_evacuated, "logits"))
            nc.vector.tensor_copy(r(R_L, QT, 4), logits[:, :, 0:GROUPS])
            chain(nc.vector.tensor_copy(r(R_L + 16, QT, 16), logits[:, :, GROUPS:]))
            four = r(R_L, 20, 4)
            shape = [P, 20, 4, 4]
            other, own = four.unsqueeze(2).to_broadcast(shape), four.unsqueeze(3).to_broadcast(shape)
            tie = const[:, K_TIE:K_TIE + 16].rearrange("p (x j) -> p x j", x=4).unsqueeze(1).to_broadcast(shape)
            pa, pb_ = (R[:, x:x + 320].rearrange("p (m x j) -> p m x j", m=20, x=4) for x in (R_A, R_B))
            chain(tt(pb_, other, own, ALU.is_equal))
            chain(tt(pb_, pb_, tie, ALU.mult))
            chain(tt(pa, other, own, ALU.is_gt))
            chain(tt(pa, pa, pb_, ALU.add))
            chain(nc.vector.tensor_reduce(R[:, R_R:R_R + 80], R[:, R_A:R_A + 320].rearrange("p (m j) -> p m j", j=4),
                                          AX.X, ALU.add))
            chain(nc.vector.tensor_reduce(R[:, R_S:R_S + 20], four, AX.X, ALU.max))
            made(tt(r(R_X, 20, 4), four, spread(R[:, R_S:R_S + 20], 4), ALU.subtract), "shifted")
            chain(ts(R[:, R_R:R_R + 16], R[:, R_R:R_R + 16], 0.5, None, ALU.is_lt))
            chain(ts(R[:, R_R + 16:R_R + 80], R[:, R_R + 16:R_R + 80], 1.5, None, ALU.is_lt))
            made(tt(r(R_M, 16, 4), r(R_R + 16, 16, 4), spread(R[:, R_R:R_R + 16], 4), ALU.mult), "chosen")
            dve.wait_ge(act_made, at(act_made, "shares"))
            chain(tt(R[:, R_X + 16:R_X + 80], R[:, R_X + 16:R_X + 80], R[:, R_R + 16:R_R + 80], ALU.mult))
            chain(nc.vector.tensor_reduce(R[:, R_S:R_S + 20], r(R_X, 20, 4), AX.X, ALU.add))
            chain(nc.vector.reciprocal(R[:, R_S:R_S + 20], R[:, R_S:R_S + 20]))
            chain(tt(r(R_S + 4, 4, 4), r(R_S + 4, 4, 4), spread(R[:, R_S:R_S + 4], 4), ALU.mult))
            chain(tt(r(R_W, 16, 4), r(R_X + 16, 16, 4), spread(R[:, R_S + 4:R_S + 20], 4), ALU.mult))
            chain(tt(R[:, R_W:R_W + 64], R[:, R_W:R_W + 64], R[:, R_M:R_M + 64], ALU.mult))
            src = result2("places")
            evacuated(nc.vector.tensor_copy(R[:, R_P:R_P + 80], src[:, 0:80]), "places")
            dve.wait_ge(dve_evacuated, at(dve_evacuated, "places"))
            chain(stt(out=R[:, R_Q:R_Q + 64], in0=R[:, R_P:R_P + 64], scalar=1.0, in1=R[:, R_M:R_M + 64],
                      op0=ALU.add, op1=ALU.mult))
            chain(ts(R[:, R_Q:R_Q + 64], R[:, R_Q:R_Q + 64], -1.0, None, ALU.add))
            places = r(R_Q, QT, 16)

            def pick(dst, place):
                iota = const[:, K_IOTA:K_IOTA + P].unsqueeze(1).to_broadcast([P, QT, P])
                return tt(dst, iota, place.to_broadcast([P, QT, P]), ALU.is_equal)

            dve.wait_ge(psum_filled, at(psum_filled, ("out2", 0)))
            for e in range(EXPERTS):
                if e >= 2:
                    dve.wait_ge(picked, at(picked, ("pick", e - 2)))
                made(pick(picks[e % 2], places[:, :, e:e + 1]), ("pick", e))
            nc.vector.memset(R[:, R_A:R_A + 17], 0.0)
            evacuated(nc.vector.tensor_copy(R[:, R_B:R_B + 16], result2("rows_of")[:, 0:16]), "rows_of")
            dve.wait_ge(dve_evacuated, at(dve_evacuated, "rows_of"))
            chain(nc.vector.tensor_copy(rows_of[:, 0:EXPERTS], R[:, R_B:R_B + 16]))
            made(nc.vector.tensor_copy(rows_of[:, EXPERTS:], R[:, R_A:R_A + 1]), "rows_of")
            dve.wait_ge(dve_made, at(dve_made, "rows_of"))
            counts = R[:, R_P + 64:R_P + 80].unsqueeze(1).to_broadcast([P, 3, 16])
            edges = const[:, K_OT:K_OT + 48].rearrange("p (t e) -> p t e", t=3)
            chain(tt(r(R_A, 3, 16), counts, edges, ALU.is_gt))
            flags = R[:, R_A:R_A + 48]
            chain(nc.vector.tensor_tensor_scan(R[:, R_A + 48:R_A + 96], const[:, K_ONES:K_ONES + 48], flags, 0.0,
                                               ALU.mult, ALU.add))
            shape = [P, OVER, 48]
            lst, lst2 = r(R_V, OVER, 48), r(R_V + OVER * 48, OVER, 48)
            chain(tt(lst, R[:, R_A + 48:R_A + 96].unsqueeze(1).to_broadcast(shape),
                     spread(const[:, K_NTH:K_NTH + OVER], 48), ALU.is_equal))
            chain(tt(lst, lst, flags.unsqueeze(1).to_broadcast(shape), ALU.mult))
            chain(tt(lst2, lst, const[:, K_OT:K_OT + 48].unsqueeze(1).to_broadcast(shape), ALU.mult))
            chain(nc.vector.tensor_reduce(over_t[:, :], lst2, AX.X, ALU.add))
            chain(tt(lst, lst, const[:, K_OE:K_OE + 48].unsqueeze(1).to_broadcast(shape), ALU.mult))
            chain(nc.vector.tensor_reduce(R[:, R_B + 1:R_B + 1 + OVER], lst, AX.X, ALU.add))
            chain(nc.vector.tensor_copy(R[:, R_B:R_B + 1], R[:, R_A + 95:R_A + 96]))
            made(nc.vector.tensor_copy(over_i[:, :], R[:, R_B:R_B + 1 + OVER]), "over")

            first = const[:, K_FIRST:K_FIRST + 16].unsqueeze(1).to_broadcast([P, QT, 16])
            chain(tt(r(R_V, QT, 16), r(R_P, QT, 16), first, ALU.add))
            base = R[:, R_A + 48:R_A + 96]
            step = R[:, R_A + 96:R_A + 144]
            chain(ts(base, base, float(P), float((EXPERTS - 1) * P + 1), ALU.mult, ALU.add))
            chain(tt(base, base, const[:, K_OT:K_OT + 48], ALU.subtract))
            chain(tt(step[:, 16:48], base[:, 16:48], base[:, 0:32], ALU.subtract))
            chain(tt(step[:, 0:16], base[:, 0:16], const[:, K_FIRST:K_FIRST + 16], ALU.subtract))
            for t in range(3):
                beyond = r(R_A + 144, QT, 16)
                chain(ts(beyond, r(R_P, QT, 16), float(P * (t + 1)), None, ALU.is_ge))
                chain(tt(beyond, beyond, step[:, 16 * t:16 * t + 16].unsqueeze(1).to_broadcast([P, QT, 16]),
                         ALU.mult))
                chain(tt(r(R_V, QT, 16), r(R_V, QT, 16), beyond, ALU.add))
            chain(tt(R[:, R_V:R_V + 64], R[:, R_V:R_V + 64], R[:, R_M:R_M + 64], ALU.mult))
            chain(nc.vector.tensor_reduce(R[:, R_S:R_S + 4], r(R_V, QT, 16), AX.X, ALU.max))
            chain(nc.vector.tensor_reduce(R[:, R_S + 4:R_S + 8], r(R_V, QT, 16), AX.X, ALU.add))
            chain(tt(r(R_A, QT, 16), r(R_V, QT, 16), spread(R[:, R_S:R_S + 4], 16), ALU.is_equal))
            chain(tt(R[:, R_A:R_A + 64], R[:, R_A:R_A + 64], R[:, R_W:R_W + 64], ALU.mult))
            chain(nc.vector.tensor_reduce(R[:, R_WT:R_WT + 4], r(R_A, QT, 16), AX.X, ALU.add))
            chain(tt(R[:, R_A:R_A + 64], R[:, R_W:R_W + 64], R[:, R_A:R_A + 64], ALU.subtract))
            chain(nc.vector.tensor_reduce(R[:, R_WT + 4:R_WT + 8], r(R_A, QT, 16), AX.X, ALU.add))
            chain(tt(R[:, R_S + 4:R_S + 8], R[:, R_S + 4:R_S + 8], R[:, R_S:R_S + 4], ALU.subtract))
            chain(ts(R[:, R_S:R_S + 8], R[:, R_S:R_S + 8], -1.0, None, ALU.add))
            made(nc.vector.tensor_copy(back_rows[:, :], R[:, R_S:R_S + 8]), "back_rows")
            def hidden(over):
                dve.wait_ge(psum_filled, at(psum_filled, ("u", over)))
                dve.wait_ge(act_evacuated, at(act_evacuated, ("g", over)))
                evacuated(tt(hid, hid, acc[:, 0, 1, :], ALU.mult), ("u", over))
                dve.wait_ge(psum_filled, at(psum_filled, ("ht", over)))
                evacuated(nc.vector.tensor_copy(hid_t, acc[:, 3, 0, :].rearrange("p (k s) -> p k s", s=P)),
                          ("ht", over))

            with dve.Fori(0, EXPERTS) as e:
                n.enter("experts", e, EXPERTS)
                hidden("")
                n.leave()
            dve.wait_ge(dve_made, at(dve_made, "over"))
            tiles = dve.value_load(over_i[0:1, 0:1], min_val=0, max_val=OVER)
            with dve.If(tiles > 0):
                with dve.Fori(0, tiles) as k:
                    n.enter("over", k, 1)
                    expert = dve.value_load(over_i[0:1, bass.ds(k + 1, 1)], min_val=0, max_val=EXPERTS - 1)
                    mine = R[:, R_A:R_A + 4]
                    chain(nc.vector.tensor_copy(mine.unsqueeze(2), places[:, :, bass.ds(expert, 1)]))
                    chain(ts(mine, mine, over_t[:, bass.ds(k, 1)], None, ALU.subtract))
                    made(pick(picks[0], mine.unsqueeze(2)), ("pick", "+"))
                    dve.wait_ge(psum_filled, at(psum_filled, ("pick", "+")))
                    made(nc.vector.tensor_copy(rows_of[:, 0:1], acc[:, 3, 1, 0:1]), ("rows_of", "+"))
                    hidden("+")
                    n.leave()
            for i in range(QT):
                dve.wait_ge(rows_back[i], 32)
                for j in range(2):
                    ins = stt(out=x_tok[:, i, :], in0=returned[:, 2 * i + j, :],
                              scalar=R[:, R_WT + 4 * j + i:R_WT + 4 * j + i + 1], in1=x_tok[:, i, :],
                              op0=ALU.mult, op1=ALU.add)
                    if j == 0:
                        ins.then_inc(summed, 1)
                        dve.wait_ge(summed, i + 1)
                ins.then_inc(combined, 1)

        @block.gpsimd
        def _(pool):
            nc.gpsimd.memset(vrows2, 0.0).then_inc(pool_step, 1)
            mark(pool_step)
            nc.gpsimd.memset(vrows, 0.0).then_inc(pool_made, 1)
            mark(pool_made, "vrows")
            nc.gpsimd.memset(ones[:, :], 1.0).then_inc(pool_made, 1)
            mark(pool_made, "ones")

            def chain(ins):
                ins.then_inc(pool_step, 1)
                mark(pool_step)
                pool.wait_ge(pool_step, now(pool_step))

            with pool.Fori(0, LAYERS) as layer:
                n.enter("layer", layer, LAYERS)
                for g in range(PG):
                    pool.wait_ge(dve_evacuated, at(dve_evacuated, ("u", g)))
                    if g >= 2:
                        pool.wait_ge(dve_made, at(dve_made, ("mixed", g - 1)))
                    src = upad[:, g, :]
                    bufs = [winA, winB] if g % 2 == 0 else [winB, winA]
                    lo = 0
                    order = [bufs[(g - j) % 2] for j in range(g + 1)]
                    for j, dst in enumerate(order):
                        sh = 2 ** j
                        lo += sh
                        if g == 1 and j == 0:
                            pool.wait_ge(dve_made, at(dve_made, ("mixed", 0)))
                        ins = nc.gpsimd.tensor_tensor(dst[:, lo:], src[:, lo:], src[:, lo - sh:PAD + T - sh], ALU.add)
                        src = dst
                        if j < g:
                            chain(ins)
                    ins.then_inc(pool_made, 1)
                    mark(pool_made, ("window", g))
                pool.wait_ge(dve_made, at(dve_made, ("mixed", PG - 1)))
                pool.sem_inc(held, 1)
                for hd in range(HEADS):
                    nc.gpsimd.tensor_copy(kT[NOPE:QK, hd, :], krope[NOPE:QK, 0, :]).then_inc(pool_made, 1)
                    mark(pool_made, ("krep", hd))
                n.leave()
            for c in range(DC):
                pool.wait_ge(dve_made, at(dve_made, ("conv", c)))
                nc.gpsimd.tensor_copy(lru_x[:, c, 0:S], tmp[2 + c % 2]).then_inc(pool_made, 1)
                mark(pool_made, ("conv", c))
            def gather(label, column):
                nc.gpsimd.indirect_dma_start(x_gath, None, h_rows,
                                             bass.IndirectOffsetOnAxis(column, 0)).then_inc(x_gathered, 16)
                mark(x_gathered, label, 16)

            pool.wait_ge(dve_made, at(dve_made, ("lru_y", DC - 1)))
            chain(nc.gpsimd.memset(padf[:, 0:D], 0.0))
            for k in range(OVER):
                pool.dma_start(y_rows[(EXPERTS + k) * P:(EXPERTS + k + 1) * P, :], padf[:, 0:D])\
                    .then_inc(y_zeroed, 16)
            pool.wait_ge(h_stored, 16 * QT)
            pool.wait_ge(dve_made, at(dve_made, "rows_of"))
            gather("x0", rows_of[:, 0:1])
            with pool.Fori(0, EXPERTS) as e:
                n.enter("experts", e, EXPERTS)
                pool.wait_ge(turned_x, e + 1)
                pool.sem_inc(held, 1)
                nc.gpsimd.tensor_copy(column[:, :], rows_of[:, bass.ds(e + 1, 1)]).then_inc(pool_step, 1)
                mark(pool_step)
                pool.wait_ge(pool_step, now(pool_step))
                pool.sem_inc(held, 1)
                gather(("x", ""), column[:, :])
                n.leave()
            pool.wait_ge(dve_made, at(dve_made, "over"))
            tiles = pool.value_load(over_i[0:1, 0:1], min_val=0, max_val=OVER)
            with pool.If(tiles > 0):
                with pool.Fori(0, tiles) as k:
                    n.enter("over", k, 1)
                    pool.wait_ge(dve_made, at(dve_made, ("rows_of", "+")))
                    pool.sem_inc(held, 1)
                    gather(("x", "+"), rows_of[:, 0:1])
                    n.leave()
            pool.wait_ge(dve_made, at(dve_made, "back_rows"))
            pool.wait_ge(all_stored, 1)
            for i in range(QT):
                for j in range(2):
                    nc.gpsimd.indirect_dma_start(returned[:, 2 * i + j, :], None, y_rows,
                                                 bass.IndirectOffsetOnAxis(back_rows[:, 4 * j + i:4 * j + i + 1], 0))\
                        .then_inc(rows_back[i], 16)
    return n


_IN = ("x", "positions", "meta_tokens", "norm_gain", "w_in", "pool_w_group", "pool_scale", "pool_w_up",
       "q_a_norm_gain", "kv_a_norm_gain", "w_q_b", "w_kv_b", "q_norm_gain", "k_norm_gain", "mla_w_up", "w_out",
       "norm1_gain_2", "w_in_2", "b_gates_2", "q_norm_gain_2", "k_norm_gain_2", "lambda_q1_2", "lambda_k1_2",
       "lambda_q2_2", "lambda_k2_2", "attn_subln_gain_2", "w_attn_o_2", "conv_w_2", "conv_b_2", "lru_wa_2",
       "lru_ba_2", "lru_wi_2", "lru_bi_2", "lru_lambda_2", "w_lru_o_2", "w_out_2", "norm2_gain_2",
       "w_group_router_2", "b_group_router_2", "w_expert_router_2", "b_expert_router_2", "w_expert_gate_2",
       "w_expert_up_2", "w_expert_down_2")


def build(nc, shapes, known):
    a = {name: nc.dram_tensor("in_" + name, shape, dt, kind="ExternalInput").ap()
         for name, (shape, dt) in shapes.items()}
    out = nc.dram_tensor("out", (1, SEQ, D), F32, kind="ExternalOutput").ap()
    return program(nc, a, out, known)


def kernel(**inputs):
    import concourse.bacc as _bacc
    from concourse.bass_utils import run_bass_kernel_spmd as _run

    arrays = {name: np.ascontiguousarray(inputs[name]) for name in _IN}
    arrays["const"] = constants()
    arrays["rotary"] = rotary_table()
    shapes = {name: (x.shape, mybir.dt.from_np(x.dtype)) for name, x in arrays.items()}
    known = build(_bacc.Bacc("TRN2", target_bir_lowering=False, num_devices=1), shapes, None)
    nc = _bacc.Bacc("TRN2", target_bir_lowering=False, num_devices=1)
    build(nc, shapes, known)
    result = _run(nc, [{"in_" + name: x for name, x in arrays.items()}], core_ids=[0])
    return result.results[0]["out"]
```

```python
import math
from contextlib import ExitStack

import numpy as np

import concourse.bass as bass
from concourse import mybir
from concourse.alu_op_type import AluOpType as ALU

F32 = mybir.dt.float32
I32 = mybir.dt.int32
F32R = mybir.dt.float32r
U32 = mybir.dt.uint32
ACT = mybir.ActivationFunctionType
AX = mybir.AxisListType

P = 128
D = 1024
DC = D // P
SEQ = 512
META = 16
T = META + SEQ
HALF = T // 2
LAYERS = 2
HEADS = 8
NOPE, ROPE, VD = 64, 32, 64
QK = NOPE + ROPE
QR, KVR = 768, 256
QC, KC = QR // P, KVR // P
POOLW = 512
PG = POOLW // P
EPS = 1e-6
SCALE1 = 1.0 / math.sqrt(QK)
TILES = [(0, META)] + [(META + P * i, P) for i in range(SEQ // P)]
NT = len(TILES)
PAD = 16
LV = 22

C_U, C_Z, C_Q, C_ROPE, C_ZM, C_GP, C_GM = 0, 512, 1024, 2048, 2080, 2592, 3616

R_L, R_A, R_B, R_R, R_S, R_X, R_M, R_W, R_P, R_Q, R_WT, R_END = (
    0, 80, 400, 720, 800, 824, 904, 968, 1032, 1112, 1176, 1184)
R_V = 1200

SLOTS = 3
SLOT_F = 4096
ACCS = 4

K_IDENT, K_MASK, K_ROT2, K_ROT1, K_FREQ, K_META, K_CNT = 0, 128, 256, 384, 416, 417, 433
K_BD = K_CNT + PG * PAD
K_TIE = K_BD + P
K_LT = K_TIE + 16
K_IOTA = K_LT + P
K_TOKEN = K_IOTA + P
K_FIRST = K_TOKEN + 4
K_ONES = K_FIRST + 16
OVER = 7
K_NTH = K_ONES + 48
K_OE = K_NTH + OVER
K_OT = K_OE + 48
K_END = K_OT + 48

S = SEQ
QT = S // P
SUB = 64
SCALE2 = SUB ** -0.5
LAM_INIT = 0.8 - 0.6 * math.exp(-0.3 * 0)
G2 = 14
DIRS = 2
TAPS = 4
GROUPS, EPG = 4, 4
EXPERTS = GROUPS * EPG
HID = 512
V_N1, V_N2, V_BG, V_SUB, V_CW, V_CB, V_BA, V_BI, V_LM, V_QN, V_KN, V_END = (
    0, 8, 16, 32, 33, 65, 73, 89, 105, 121, 122, 123)


def constants():
    t = np.zeros((P, K_END), np.float32)
    t[:, K_IDENT:K_IDENT + P] = np.eye(P)
    t[:, K_MASK:K_MASK + P] = np.where(np.arange(P)[None, :] > np.arange(P)[:, None], -1e30, 0.0)
    for sub in range(2):
        for m in range(64):
            k = m + 32 if m < 32 else m - 32
            t[64 * sub + k, K_ROT2 + 64 * sub + m] = -1.0 if m < 32 else 1.0
    for m in range(ROPE):
        k = m + 16 if m < 16 else m - 16
        t[NOPE + k, K_ROT1 + m] = -1.0 if m < 16 else 1.0
    freq = (10000.0 ** (-(np.arange(16, dtype=np.float32) / np.float32(16)).astype(np.float64))).astype(np.float32)
    t[NOPE:QK, K_FREQ] = np.tile(freq, 2)
    t[:, K_META:K_META + META] = np.arange(META)
    for g in range(PG):
        t[:, K_CNT + g * PAD:K_CNT + (g + 1) * PAD] = 1.0 / np.minimum(np.arange(1, PAD + 1), 2 ** (g + 1))
    for sub in range(2):
        t[64 * sub:64 * sub + 64, K_BD + 64 * sub:K_BD + 64 * sub + 64] = 1.0
    for i in range(4):
        t[:, K_TIE + 4 * i:K_TIE + 4 * i + i] = 1.0
    t[:, K_IOTA:K_IOTA + P] = np.arange(P)
    t[:, K_TOKEN:K_TOKEN + 4] = np.arange(P)[:, None] + P * np.arange(4)
    t[:, K_FIRST:K_FIRST + 16] = P * np.arange(16) + 1
    t[:, K_ONES:K_ONES + 48] = 1.0
    t[:, K_NTH:K_NTH + OVER] = np.arange(1, OVER + 1)
    t[:, K_OE:K_OE + 48] = np.tile(np.arange(16), 3)
    t[:, K_OT:K_OT + 48] = np.repeat(128 * np.arange(1, 4), 16)
    t[:, K_LT:K_LT + P] = np.arange(P)[:, None] < np.arange(P)[None, :]
    return t


def rotary_table():
    inv = (10000.0 ** (-(np.arange(0, SUB, 2, dtype=np.float32) / np.float32(SUB)).astype(np.float64)))
    ang = (np.arange(S, dtype=np.float32)[:, None] * inv.astype(np.float32)[None, :]).astype(np.float32)
    ang = np.tile(ang.T.astype(np.float64), (P // 32, 1))
    return np.stack([np.cos(ang), np.sin(ang)], axis=1).astype(np.float32)


class Counts:

    def __init__(self, known=None):
        self.known = known
        self.value, self.marks, self.start, self.per, self.trips = {}, {}, {}, {}, {}
        self.slots = {}
        self.inside = None

    def mark(self, sem, label=None, by=1):
        self.value[sem.name] = self.value.get(sem.name, 0) + by
        if label is not None:
            assert (sem.name, label) not in self.marks, label
            self.marks[sem.name, label] = (self.inside and self.inside[0], self.value[sem.name])

    def enter(self, loop, index, trips):
        self.inside = (loop, index)
        self.trips[loop] = trips
        self.begun = dict(self.value)

    def leave(self):
        loop = self.inside[0]
        for name, v in self.value.items():
            start = self.begun.get(name, 0)
            if v > start:
                self.start[loop, name], self.per[loop, name] = start, v - start
                self.value[name] = start + (v - start) * self.trips[loop]
        self.inside = None

    def _value(self, name, loop, v, back):
        if loop is None:
            return v
        per = self.known.per[loop, name]
        if self.inside and self.inside[0] == loop:
            return self.inside[1] * per + (v - back * per)
        return v + (self.known.trips[loop] - 1) * per

    def at(self, sem, label, back=0):
        if self.known is None:
            return 1
        loop, v = self.known.marks[sem.name, label]
        return self._value(sem.name, loop, v, back)

    def in_pass(self, sem, label, index):
        if self.known is None:
            return 1
        loop, v = self.known.marks[sem.name, label]
        return index * self.known.per[loop, sem.name] + v

    def now(self, sem):
        if self.known is None:
            return 1
        return self._value(sem.name, self.inside and self.inside[0], self.value[sem.name], 0)


def program(nc, a, out, known=None):
    n = Counts(known)
    mark, at, now, in_pass = n.mark, n.at, n.now, n.in_pass
    with ExitStack() as ctx:
        def sb(name, shape, dt=F32):
            return ctx.enter_context(nc.sbuf_tensor(name, shape, dt))

        def sb_split(name, shape):
            with nc.sbuf_tensor(name + "_split", shape, F32R) as split:
                pass
            return sb(name, shape), split

        def sem(name):
            return ctx.enter_context(nc.semaphore(name))

        ring, ring_split = sb_split("ring", [P, SLOTS, SLOT_F])
        hres = sb("hres", [P, DC, T])
        h = sb("h", [P, DC, T])
        upad, upad_split = sb_split("upad", [P, PG, PAD + T])
        zp, zp_split = sb_split("zp", [P, PG, T])
        latent = sb("latent", [P, QC + KC, T])
        krope = sb("krope", [P, 2, T])
        qk, qk_split = sb_split("qk", [P, 2 * HEADS, T])
        v, v_split = sb_split("v", [P, NT, HEADS * VD])
        work, work_split = sb_split("work", [P, DC, T])
        gate = sb("gate", [P, 2, T])
        o = sb("o", [P, PG, T])
        trig = sb("trig", [P, 2, T])
        const = sb("const", [P, K_END])
        ones = sb("ones", [P, P])
        vecs = sb("vecs", [P, LAYERS * LV])
        lv = sb("lv", [P, LV])
        small = sb("small", [P, 16])
        vec2 = sb("vec2", [P, V_END])
        half_bias = sb("half_bias", [P, V_LM - V_BG])
        lamt = sb("lamt", [P, 4 * SUB])
        decay = sb("decay", [P, 6, 16])
        router = sb("router", [P, DC, GROUPS + EXPERTS])
        router_bias = sb("router_bias", [P, GROUPS + EXPERTS])
        logits = sb("logits", [P, QT, GROUPS + EXPERTS])
        rt = sb("rt", [P, 1, 8])
        rows_of = sb("rows_of", [P, EXPERTS + 1], U32)
        back_rows = sb("back_rows", [P, 8], U32)
        over_i = sb("over_i", [P, 1 + OVER], I32)
        over_t = sb("over_t", [P, OVER])
        h_rows = nc.dram_tensor("h_rows", (S, D), F32, kind="Internal").ap()
        y_rows = nc.dram_tensor("y_rows", ((EXPERTS + OVER) * P, D), F32, kind="Internal").ap()

        qT, kT = qk[:, 0:HEADS, :], qk[:, HEADS:, :]
        cq, ckv = latent[:, 0:QC, :], latent[:, QC:, :]
        flat = latent[:, :, :].rearrange("p c t -> p (c t)")
        probs = [flat[:, i * T:(i + 1) * T] for i in range(3)]
        probsT = [flat[:, 3 * T + i * NT * P:3 * T + (i + 1) * NT * P].rearrange("p (j q) -> p j q", j=NT)
                  for i in range(2)]
        cosT, sinT = trig[NOPE:QK, 0, :], trig[NOPE:QK, 1, :]
        winA, winB = (zp[:, :, :].rearrange("p c t -> p (c t)")[:, i * (PAD + T):(i + 1) * (PAD + T)]
                      for i in range(2))
        qkf = qk[:, :, :].rearrange("p c t -> p (c t)")
        xin = qkf[:, 0:4 * D].rearrange("p (i d) -> p i d", i=4)
        metain = qkf[:, 4 * D:5 * D]
        vrows = qkf[:, 5 * D:5 * D + P]
        vrows2 = qkf[:, 5 * D + P:5 * D + 2 * P]
        h_up = [qk_split[:, c, :] for c in range(DC)]
        h_low = [qk_split[:, DC + c, :] for c in range(DC)]
        m_up = [zp_split[:, c, :] if c < PG else upad_split[:, c - PG, PAD:] for c in range(DC)]
        m_low = [work_split[:, c, :] for c in range(DC)]
        vflat = v_split[:, :, :].rearrange("p c t -> p (c t)")
        w_up = [vflat[:, i * D:(i + 1) * D].rearrange("p (k m) -> p k m", k=DC) for i in range(2)]
        ident, mask = const[:, K_IDENT:K_IDENT + P], const[:, K_MASK:K_MASK + P]
        rot1 = const[NOPE:QK, K_ROT1:K_ROT1 + ROPE]

        xr = hres[:, :, META:T]
        h2 = h[:, :, 0:S]
        q2, k2 = qk[:, 0:DC, 0:S], qk[:, DC:, 0:S]
        workf = work[:, :, :].rearrange("p c t -> p (c t)")
        v2 = workf[:, 0:QT * D].rearrange("p (j n) -> p j n", j=QT)
        merged = work[:, :, 0:S]
        lru_x = latent
        gelu = [zp[:, c, 0:S] if c < PG else o[:, c - PG, 0:S] for c in range(DC)]
        tmp = [v[:, i, :] for i in range(NT)]
        probs2 = [[gate[:, c, 0:S] for c in range(2)], [krope[:, c, 0:S] for c in range(2)],
                  [v[:, c, :] for c in range(2)]]
        padf = upad[:, :, :].rearrange("p c t -> p (c t)")
        probsT2 = [padf[:, i * S:(i + 1) * S].rearrange("p (j q) -> p j q", j=QT) for i in range(4)]
        cos2, sin2 = trig[:, 0, 0:S], trig[:, 1, 0:S]
        x_tok = workf[:, 0:QT * D].rearrange("p (i d) -> p i d", i=QT)
        h_tok = qkf[:, 0:QT * D].rearrange("p (i d) -> p i d", i=QT)
        returned = qkf[:, 0:8 * D].rearrange("p (i d) -> p i d", i=8)
        x_gath = flat[:, 0:D]
        x_exp = flat[:, D:2 * D].rearrange("p (k s) -> p k s", k=DC)
        hid = flat[:, 2 * D:2 * D + HID]
        hid_t = flat[:, 2 * D + HID:3 * D].rearrange("p (k s) -> p k s", k=HID // P)
        y_out = flat[:, 3 * D:4 * D]
        zpf = zp[:, :, :].rearrange("p c t -> p (c t)")
        picks = [zpf[:, i * 512:(i + 1) * 512].rearrange("p (i s) -> p i s", i=QT) for i in range(2)]
        R = o[:, :, :].rearrange("p c t -> p (c t)")
        rot2 = const[:, K_ROT2:K_ROT2 + P]
        blocks = const[:, K_BD:K_BD + P]

        acc = ctx.enter_context(nc.psum_tensor("acc", [P, ACCS, 2, 512], F32))

        psum_filled = sem("psum_filled")
        act_evacuated = sem("act_evacuated")
        dve_evacuated = sem("dve_evacuated")
        act_made = sem("act_made")
        dve_made = sem("dve_made")
        pool_made = sem("pool_made")
        dve_step = sem("dve_step")
        pool_step = sem("pool_step")
        w_loaded = [sem(f"w_loaded{i}") for i in range(SLOTS)]
        w_free = [sem(f"w_free{i}") for i in range(SLOTS)]
        const_loaded = sem("const_loaded")
        x_loaded = sem("x_loaded")
        vec_loaded = sem("vec_loaded")
        stored = sem("stored")
        squared = sem("squared")
        y_zeroed = sem("y_zeroed")
        summed = sem("summed")
        turned_x = sem("turned_x")
        column = sb("column", [P, 1], U32)
        picked = sem("picked")
        combined = sem("combined")
        h_stored = sem("h_stored")
        x_gathered = sem("x_gathered")
        y_stored = sem("y_stored")
        all_stored = sem("all_stored")
        rows_back = [sem(f"rows_back{i}") for i in range(QT)]

        held = sem("held")

        def rows(w, c0, c1):
            return w[:, c0:c1].rearrange("(k p) n -> p k n", p=P)

        def layer_granules(layer):
            w = a["w_in"][layer]
            return [
                ("cq0", rows(w, C_Q, C_Q + 512)), ("cq1", rows(w, C_Q + 512, C_Q + 1024)),
                ("u", rows(w, C_U, C_U + 512)),
                ("kvb", rows(a["w_kv_b"][layer], 0, HEADS * (NOPE + VD))),
                ("qb0", rows(a["w_q_b"][layer], 0, 4 * QK)), ("qb1", rows(a["w_q_b"][layer], 4 * QK, 8 * QK)),
                ("z", rows(w, C_Z, C_Z + 512)),
                ("pg", a["pool_w_group"][layer].rearrange("g c d -> c g d")),
                ("pup", rows(a["pool_w_up"][layer], 0, D)),
                ("gp0", rows(w, C_GP, C_GP + 512)), ("gp1", rows(w, C_GP + 512, C_GP + 1024)),
                ("zm", rows(w, C_ZM, C_ZM + 512)),
                ("mup", rows(a["mla_w_up"][layer], 0, D)),
                ("gm0", rows(w, C_GM, C_GM + 512)), ("gm1", rows(w, C_GM + 512, C_GM + 1024)),
                ("wo0", rows(a["w_out"][layer], 0, 512)), ("wo1", rows(a["w_out"][layer], 512, 1024)),
            ]

        PLACE1 = [0, 1, 2, 0, 1, 2, 0, 1, 2, 0, 1, 0, 2, 1, 0, 1, 2]
        shapes1 = {name: (place, ap.shape[1], ap.shape[2])
                   for place, (name, ap) in zip(PLACE1, layer_granules(0))}
        LAST1 = list(shapes1)
        shapes1["rope"] = (shapes1["kvb"][0], DC, ROPE)
        START = {"rope": KC * HEADS * (NOPE + VD)}

        def weight(name):
            slot, k, m = shapes1[name]
            at_ = START.get(name, 0)
            return ring[:, slot, at_:at_ + k * m].rearrange("p (k m) -> p k m", k=k)

        GRANULES2 = (["q0", "q1", "k0", "k1", "v0", "v1", "lx0", "lx1", "lg0", "lg1", "lru",
                      "ga0", "ao0", "ga1", "ao1", "gl0", "lo0", "gl1", "lo1", "xo0", "xo1"])
        COLS2 = {x: 512 * i for i, x in enumerate(
            ["q0", "q1", "k0", "k1", "v0", "v1", "lx0", "lx1", "lg0", "lg1", "ga0", "ga1", "gl0", "gl1"])}
        PLACE2 = [0, 1, 2, 0, 1, 2, 0, 1, 2, 0, 1, 2, 0, 2, 0, 1, 2, 0, 1, 2, 0]
        for name, place in zip(GRANULES2, PLACE2):
            shapes1[name] = (place, 32, P) if name == "lru" else (place, DC, 512)
        for over in "", "+":
            shapes1["gate" + over], shapes1["up" + over] = (0, DC, HID), (1, DC, HID)
            shapes1["down" + over] = (2, HID // P, D)

        background = ([("z", i) for i in range(PG)] + [("pg", i) for i in range(PG)]
                      + [x for m in range(DC) for x in (("gp", m), ("yp", m))])
        items = [(hd, i) for hd in range(HEADS) for i in range(NT)]
        STEPS = len(items) + 3

        def background_at(step):
            lo, hi = -(-step * len(background) // STEPS), -(-(step + 1) * len(background) // STEPS)
            return background[lo:hi]

        def gate_uses():
            order = []
            for x in background:
                if x[0] in ("z", "gp"):
                    order.append(x)
            order += [("zm", c) for c in range(PG)] + [("gm", m) for m in range(DC)]
            return {x: i for i, x in enumerate(order)}, order

        gate_no, gate_order = gate_uses()

        def gate_reader(x):
            return {"z": ("z", x[1]), "gp": ("yp", x[1]), "zm": ("og", x[1]), "gm": ("mg", x[1])}[x[0]]

        LAG = 4
        items2 = [(hd, i) for hd in range(HEADS) for i in range(QT)]
        STEPS2 = len(items2) + 3

        def background2_at(step):
            return range((step * DC) // STEPS2, ((step + 1) * DC) // STEPS2)

        lru_units = [(d, c) for c0 in range(0, DC, 2) for d in range(DIRS) for c in (c0, c0 + 1)]

        def unit_tiles(u):
            tiles = [k2[:, i, :] for i in range(DC)] + [padf[:, i * S:(i + 1) * S] for i in range(4)]
            return tiles[3 * (u % 4):3 * (u % 4) + 3]

        JOBS_A = ([(("c", j), f"cq{j // 4}", j % 4) for j in range(2, QC + KC)]
                  + [(("u", j), "u", j) for j in range(PG)])
        JOBS_C = ([(("zm", j), "zm", j) for j in range(2, PG)] + [(("gm", m), f"gm{m // 4}", m % 4) for m in range(DC)]
                  + [(("out", m), f"wo{m // 4}", m % 4) for m in range(DC)])
        job_no = {x[0]: i for jobs_ in (JOBS_A, JOBS_C) for i, x in enumerate(jobs_)}

        def columns(name, j, of=ring):
            slot, k, m = shapes1[name]
            return of[:, slot, 0:k * m].rearrange("p (k m) -> p k m", k=k)[:, :, j * P:(j + 1) * P]

        block = ctx.enter_context(nc.Block())

        @block.sync
        def _(sp):
            sp.dma_start(const[:, :], a["const"]).then_inc(const_loaded, 16)
            sp.dma_start(krope[NOPE:QK, 0, META:T].bitcast(I32),
                         a["positions"].to_broadcast([ROPE, SEQ])).then_inc(const_loaded, 16)
            sp.wait_ge(pool_made, at(pool_made, "vrows"))
            for l in range(LAYERS):
                r = LV * l
                for name, r0, k, m in (("norm_gain", 0, DC, P), ("q_a_norm_gain", 8, QC, P),
                                       ("kv_a_norm_gain", 14, KC, P), ("pool_scale", 16, PG, P),
                                       ("q_norm_gain", 20, 1, QK), ("k_norm_gain", 21, 1, QK)):
                    sp.dma_start(vrows[r + r0:r + r0 + k, 0:m],
                                 a[name][l].rearrange("(k m) -> k m", k=k)).then_inc(vec_loaded, 16)
                    mark(vec_loaded, None, 16)
            for name, r0, k in (("norm1_gain_2", V_N1, DC), ("norm2_gain_2", V_N2, DC), ("b_gates_2", V_BG, 16),
                                ("attn_subln_gain_2", V_SUB, 1), ("conv_w_2", V_CW, TAPS * DC),
                                ("conv_b_2", V_CB, DC), ("lru_ba_2", V_BA, 16), ("lru_bi_2", V_BI, 16),
                                ("lru_lambda_2", V_LM, 16)):
                src = a[name][0]
                src = src.rearrange("j (c m) -> (j c) m", m=P) if len(src.shape) == 2 else \
                    src.rearrange("(k m) -> k m", k=k)
                sp.dma_start(vrows2[r0:r0 + k, :], src).then_inc(vec_loaded, 16)
                mark(vec_loaded, None, 16)
            for name, r0 in (("q_norm_gain_2", V_QN), ("k_norm_gain_2", V_KN)):
                for sub in range(2):
                    sp.dma_start(vrows2[r0:r0 + 1, SUB * sub:SUB * sub + SUB], a[name]).then_inc(vec_loaded, 16)
                    mark(vec_loaded, None, 16)
            for i, name in enumerate(("lambda_q1_2", "lambda_k1_2", "lambda_q2_2", "lambda_k2_2")):
                sp.dma_start(lamt[:, i * SUB:(i + 1) * SUB], a[name].to_broadcast([P, SUB])).then_inc(vec_loaded, 16)
                mark(vec_loaded, None, 16)
            with nc.allow_non_contiguous_dma(reason="narrow router weights"):
                sp.dma_start(router[:, :, 0:GROUPS], a["w_group_router_2"][0].rearrange("(k p) n -> p k n", p=P))\
                    .then_inc(vec_loaded, 16)
                sp.dma_start(router[:, :, GROUPS:], a["w_expert_router_2"][0].rearrange("(k p) n -> p k n", p=P))\
                    .then_inc(vec_loaded, 16)
            sp.dma_start(router_bias[:, 0:GROUPS], a["b_group_router_2"].to_broadcast([P, GROUPS]))\
                .then_inc(vec_loaded, 16)
            sp.dma_start(router_bias[:, GROUPS:], a["b_expert_router_2"].to_broadcast([P, EXPERTS]))\
                .then_inc(vec_loaded, 16)
            mark(vec_loaded, "vectors", 64)

            with sp.Fori(0, LAYERS) as layer:
                n.enter("layer", layer, LAYERS)
                for i, (name, src) in enumerate(layer_granules(layer)):
                    slot = PLACE1[i]
                    before = [x for x, place in zip(LAST1[:i], PLACE1) if place == slot]
                    last = before[-1] if before else [x for x, place in zip(LAST1, PLACE1) if place == slot][-1]
                    sp.wait_ge(w_free[slot], at(w_free[slot], ("used", last), back=not before))
                    sp.sem_inc(held, 1)
                    sp.dma_start(weight(name), src).then_inc(w_loaded[slot], 16)
                    if name == "kvb":
                        sp.dma_start(weight("rope"), rows(a["w_in"][layer], C_ROPE, C_ROPE + ROPE))\
                            .then_inc(w_loaded[slot], 16)
                        mark(w_loaded[slot], None, 16)
                    mark(w_loaded[slot], name, 16)
                n.leave()
            w2 = {x: rows(a["w_in_2"][0], c, c + 512) for x, c in COLS2.items()}
            for x, name in (("ao", "w_attn_o_2"), ("lo", "w_lru_o_2"), ("xo", "w_out_2")):
                for i in range(2):
                    w2[f"{x}{i}"] = rows(a[name][0], 512 * i, 512 * i + 512)
            in_slot = {shapes1[x][0]: x for x in LAST1}
            for name in GRANULES2:
                slot = shapes1[name][0]
                last, in_slot[slot] = in_slot[slot], name
                sp.wait_ge(w_free[slot], at(w_free[slot], ("used", last)))
                if name == "lru":
                    for kind, x in enumerate(("lru_wa_2", "lru_wi_2")):
                        for d in range(DIRS):
                            at_ = 16 * kind + 8 * d
                            sp.dma_start(weight(name)[:, at_:at_ + 8, :],
                                         a[x][0, d].rearrange("b d e -> d b e")).then_inc(w_loaded[slot], 16)
                    mark(w_loaded[slot], name, 64)
                else:
                    sp.dma_start(weight(name), w2[name]).then_inc(w_loaded[slot], 16)
                    mark(w_loaded[slot], name, 16)
                if name == "q0":
                    sp.wait_ge(dve_made, at(dve_made, ("qr", HEADS - 1)))
                    sp.dma_start(trig[:, :, 0:S], a["rotary"]).then_inc(const_loaded, 16)
                    mark(const_loaded, "rotary", 48)
            for i in range(QT):
                sp.wait_ge(act_evacuated, at(act_evacuated, ("h_tok", i)))
                sp.dma_start(h_rows[i * P:(i + 1) * P, :], h_tok[:, i, :]).then_inc(h_stored, 16)

            def expert_weights(expert, over, kinds=("gate", "up", "down")):
                for x in kinds:
                    name = x + over
                    slot = shapes1[name][0]
                    sp.wait_ge(w_free[slot], at(w_free[slot], ("used", name), back=1) if over else
                               expert + at(w_free[slot], ("used", in_slot[slot])))
                    sp.sem_inc(held, 1)
                    sp.dma_start(weight(name), a[f"w_expert_{x}_2"][0, expert].rearrange("(k p) n -> p k n", p=P))\
                        .then_inc(w_loaded[slot], 16)
                    mark(w_loaded[slot], (name, "alone") if isinstance(expert, int) else name, 16)

            expert_weights(0, "", ("gate", "up"))
            with sp.Fori(0, EXPERTS - 1) as e:
                n.enter("expert weights", e, EXPERTS - 1)
                expert_weights(e + 1, "", ("gate", "up"))
                expert_weights(e, "", ("down",))
                n.leave()
            expert_weights(EXPERTS - 1, "", ("down",))
            sp.wait_ge(dve_made, at(dve_made, "over"))
            tiles = sp.value_load(over_i[0:1, 0:1], min_val=0, max_val=OVER)
            with sp.If(tiles > 0):
                with sp.Fori(0, tiles) as k:
                    n.enter("over", k, 1)
                    expert_weights(sp.value_load(over_i[0:1, bass.ds(k + 1, 1)], min_val=0, max_val=EXPERTS - 1), "+")
                    n.leave()
            for i in range(QT):
                sp.wait_ge(combined, i + 1)
                sp.dma_start(out[0, i * P:(i + 1) * P, :], x_tok[:, i, :]).then_inc(stored, 16)
            sp.wait_ge(stored, 16 * QT)

        @block.tensor
        def _(pe):
            jobs = []

            def accumulator(label, reader):
                slot = len(jobs) % ACCS
                if len(jobs) >= ACCS:
                    before, by = jobs[-ACCS]
                    pe.wait_ge(by, at(by, before))
                    pe.sem_inc(held, 1)
                jobs.append((label, reader))
                n.slots[label] = slot
                return acc[:, slot, :, :]

            def done(ins, label):
                ins.then_inc(psum_filled, 1)
                mark(psum_filled, label)

            def drained():
                last = {by.name: (before, by) for before, by in jobs[-ACCS:]}
                for before, by in last.values():
                    pe.wait_ge(by, at(by, before))
                jobs.clear()

            def loaded(name):
                slot = shapes1[name][0]
                pe.wait_ge(w_loaded[slot], at(w_loaded[slot], name))

            def used(ins, name):
                slot = shapes1[name][0]
                ins.then_inc(w_free[slot], 1)
                mark(w_free[slot], ("used", name))

            def free(name):
                slot = shapes1[name][0]
                pe.drain().then_inc(w_free[slot], 1)
                mark(w_free[slot], ("used", name))

            def product(label, reader, lhs, rhs, rows_=P, at_row=0, before=None):
                dst = accumulator(label, reader)
                for k, w in enumerate(lhs):
                    if before:
                        before(k)
                    for half in range(2):
                        ins = nc.tensor.matmul(dst[at_row:at_row + rows_, half, 0:HALF], w,
                                               rhs(k)[:, half * HALF:(half + 1) * HALF],
                                               start=(k == 0), stop=(k == len(lhs) - 1),
                                               skip_group_check=True)
                done(ins, label)

            def product_split(label, reader, name, j, up, low, before=None):
                dst = accumulator(label, reader)
                pe.wait_ge(dve_made, at(dve_made, ("wlow",) + label))
                pe.sem_inc(held, 1)
                w1, w0 = w_up[job_no[label] % 2], columns(name, j, ring_split)
                for k in range(DC):
                    if before:
                        before(k)
                    for half in range(2):
                        c = slice(half * HALF, (half + 1) * HALF)
                        for i, (w, x) in enumerate(((w1, up[k]), (w1, low[k]), (w0, up[k]))):
                            ins = nc.tensor.matmul(dst[:, half, 0:HALF], w[:, k, :], x[:, c],
                                                   start=(k == 0 and i == 0), stop=(k == DC - 1 and i == 2),
                                                   skip_group_check=True)
                done(ins, label)

            for slot in range(SLOTS):
                pe.sem_inc(w_free[slot], LAYERS * 3)
                mark(w_free[slot], None, LAYERS * 3)

            pe.wait_ge(const_loaded, 32)
            pe.wait_ge(x_loaded, 80)
            for c in range(DC):
                dst = accumulator(("x", c), dve_evacuated)
                for i in range(4):
                    nc.tensor.transpose(dst[:, 0, i * P:(i + 1) * P], xin[:, i, c * P:(c + 1) * P], ident)
                done(nc.tensor.transpose(dst[:, 1, 0:META], metain[0:META, c * P:(c + 1) * P],
                                         ident[0:META, 0:META]), ("x", c))
            pe.wait_ge(vec_loaded, at(vec_loaded, "vectors"))
            pe.wait_ge(pool_made, at(pool_made, "vrows"))
            dst = accumulator("vecs", dve_evacuated)
            done(nc.tensor.transpose(dst[:, 0, 0:LAYERS * LV], vrows[0:LAYERS * LV, :],
                                     ident[0:LAYERS * LV, 0:LAYERS * LV]), "vecs")
            dst = accumulator("vec2", dve_evacuated)
            done(nc.tensor.transpose(dst[:, 0, 0:V_END], vrows2[0:V_END, :], ident[0:V_END, 0:V_END]), "vec2")
            drained()
            pe.wait_ge(pool_made, at(pool_made, "ones"))

            with pe.Fori(0, LAYERS) as layer:
                n.enter("layer", layer, LAYERS)
                chunk = lambda x: (lambda k: x[:, k, :])

                product("ss_h", act_evacuated, [ones[:, :]] * DC, chunk(latent),
                        before=lambda k: pe.wait_ge(squared, at(squared, ("sq", k), back=1)))

                def h_ready(k):
                    pe.wait_ge(dve_made, at(dve_made, ("h", k)))

                def h_split(k):
                    pe.wait_ge(dve_made, at(dve_made, ("hlow", k)))

                for name, c0, kinds in (("cq0", 0, 4), ("cq1", 4, 4)):
                    loaded(name)
                    for j in range(kinds):
                        c = c0 + j
                        if c < 2:
                            product(("c", c), act_evacuated,
                                    [weight(name)[:, k, j * P:(j + 1) * P] for k in range(DC)], chunk(h),
                                    before=h_ready if c == 0 else None)
                        else:
                            product_split(("c", c), act_evacuated, name, j, h_up, h_low,
                                          before=h_split if c == 2 else None)
                    free(name)
                loaded("u")
                for j in range(PG):
                    product_split(("u", j), dve_evacuated, "u", j, h_up, h_low)
                    if j == 0:
                        pe.wait_ge(act_evacuated, at(act_evacuated, ("c", QC + KC - 1)))
                        product("ss_cq", act_evacuated, [ones[:, :]] * QC, chunk(work))
                        product("ss_ckv", act_evacuated, [ones[:, :]] * KC, lambda k: work[:, QC + k, :])
                free("u")
                loaded("kvb")
                product("rope", dve_evacuated, [weight("rope")[:, k, :] for k in range(DC)], chunk(h),
                        rows_=ROPE, at_row=NOPE)
                pe.wait_ge(dve_evacuated, at(dve_evacuated, "rope"))
                product("rotk", dve_evacuated, [rot1], lambda k: krope[NOPE:QK, 0, :],
                        rows_=ROPE, at_row=NOPE)
                wkv = weight("kvb").rearrange("p k (h c) -> p k h c", h=HEADS)
                pe.wait_ge(dve_made, at(dve_made, ("cn", QC + KC - 1)))
                for i, (t0, nt) in enumerate(TILES):
                    dst = accumulator(("v", i), act_evacuated)
                    for k in range(KC):
                        ins = nc.tensor.matmul(dst[0:nt, 0, :], ckv[:, k, t0:t0 + nt], wkv[:, k, :, NOPE:],
                                               start=(k == 0), stop=(k == KC - 1))
                    done(ins, ("v", i))
                def k_head(hd):
                    product(("k", hd), act_evacuated, [wkv[:, k, hd, 0:NOPE] for k in range(KC)],
                            chunk(ckv), rows_=NOPE)

                def kss(hd):
                    pe.wait_ge(act_evacuated, at(act_evacuated, ("k", hd)))
                    if hd == 0:
                        pe.wait_ge(act_made, at(act_made, "sq_rope"))
                    product(("kss", hd), act_evacuated, [ones[0:QK, 0:QK]],
                            lambda k: work[0:QK, 2 + hd % 2, :], rows_=QK)

                def q_head(hd):
                    w = weight(f"qb{hd // 4}")
                    m = (hd % 4) * QK
                    product(("q", hd), act_evacuated, [w[:, k, m:m + QK] for k in range(QC)],
                            chunk(cq), rows_=QK)

                def qss(hd):
                    pe.wait_ge(act_evacuated, at(act_evacuated, ("q", hd)))
                    product(("qss", hd), act_evacuated, [ones[0:QK, 0:QK]],
                            lambda k: work[0:QK, 4 + hd % 2, :], rows_=QK)

                def rotq(hd):
                    pe.wait_ge(dve_made, at(dve_made, ("qn", hd)))
                    product(("rotq", hd), dve_evacuated, [rot1], lambda k: qT[NOPE:QK, hd, :],
                            rows_=ROPE, at_row=NOPE)

                for hd in range(HEADS + 2):
                    if hd < HEADS:
                        if hd % 4 == 0:
                            loaded(f"qb{hd // 4}")
                        k_head(hd)
                        if hd == HEADS - 1:
                            free("kvb")
                        q_head(hd)
                        if hd % 4 == 3:
                            free(f"qb{hd // 4}")
                    if 1 <= hd <= HEADS:
                        kss(hd - 1)
                        qss(hd - 1)
                    if 2 <= hd < HEADS:
                        rotq(hd - 2)

                def scores(s):
                    hd, i = items[s]
                    t0, nt = TILES[i]
                    if i == 0:
                        pe.wait_ge(dve_made, at(dve_made, ("qr", hd)))
                    dst = accumulator(("s", s), act_evacuated).rearrange("p a b -> p (a b)")
                    for c0 in range(0, t0 + nt, 512):
                        c1 = min(c0 + 512, t0 + nt)
                        ins = nc.tensor.matmul(dst[0:nt, c0:c1], qT[0:QK, hd, t0:t0 + nt],
                                               kT[0:QK, hd, c0:c1], start=True, stop=True)
                    done(ins, ("s", s))

                def turn(s):
                    hd, i = items[s]
                    nt = TILES[i][1]
                    pe.wait_ge(dve_made, at(dve_made, ("p", s)))
                    dst = accumulator(("t", s), act_evacuated).rearrange("p a (b q) -> p (a b) q", q=P)
                    for j in range(i + 1):
                        k0, nk = TILES[j]
                        ins = nc.tensor.transpose(dst[0:nk, j, 0:nt], probs[s % 3][0:nt, k0:k0 + nk],
                                                  ident[0:nt, 0:nt])
                    done(ins, ("t", s))

                def values(s):
                    hd, i = items[s]
                    nt = TILES[i][1]
                    pe.wait_ge(act_evacuated, at(act_evacuated, ("t", s)))
                    dst = accumulator(("o", s), act_evacuated)
                    r = VD * (hd % 2)
                    for j in range(i + 1):
                        nk = TILES[j][1]
                        ins = nc.tensor.matmul(dst[r:r + VD, 0, 0:nt], v[0:nk, j, hd * VD:(hd + 1) * VD],
                                               probsT[s % 2][0:nk, j, 0:nt], start=(j == 0), stop=(j == i),
                                               skip_group_check=True)
                    done(ins, ("o", s))

                def back(x):
                    kind, m = x
                    if kind == "z":
                        if m == 0:
                            loaded("z")
                        product(x, dve_evacuated, [weight("z")[:, k, m * P:(m + 1) * P] for k in range(DC)],
                                chunk(h))
                        if m == PG - 1:
                            free("z")
                    elif kind == "pg":
                        if m == 0:
                            loaded("pg")
                        pe.wait_ge(dve_made, at(dve_made, ("mixed", m)))
                        product(x, dve_evacuated, [weight("pg")[:, m, :]], lambda k: upad[:, m, PAD:])
                        if m == PG - 1:
                            free("pg")
                    elif kind == "gp":
                        g = f"gp{m // 4}"
                        if m % 4 == 0:
                            loaded(g)
                        product(x, act_evacuated,
                                [weight(g)[:, k, (m % 4) * P:(m % 4 + 1) * P] for k in range(DC)], chunk(h))
                        if m == 3:
                            free(g)
                    else:
                        if m == 0:
                            loaded("pup")
                            pe.wait_ge(dve_evacuated, at(dve_evacuated, ("pg", PG - 1)))
                        product(x, dve_evacuated, [weight("pup")[:, k, m * P:(m + 1) * P] for k in range(PG)],
                                chunk(zp))
                        if m == DC - 1:
                            free("pup")
                            free("gp1")

                for s in range(STEPS):
                    if s < len(items):
                        scores(s)
                    for x in background_at(s):
                        back(x)
                    if s < 2:
                        rotq(HEADS - 2 + s)
                    if 2 <= s < len(items) + 2:
                        turn(s - 2)
                    if s >= 3:
                        values(s - 3)

                loaded("zm")
                for c in range(PG):
                    if c < 2:
                        product(("zm", c), dve_evacuated,
                                [weight("zm")[:, k, c * P:(c + 1) * P] for k in range(DC)], chunk(h))
                    else:
                        product_split(("zm", c), dve_evacuated, "zm", c, h_up, h_low,
                                      before=(lambda k: pe.wait_ge(dve_made, at(dve_made, ("hlow2", k))))
                                      if c == 2 else None)
                free("zm")
                loaded("mup")
                for m in range(DC):
                    g = f"gm{m // 4}"
                    if m % 4 == 0:
                        loaded(g)
                    product_split(("gm", m), act_evacuated, g, m % 4, h_up, h_low)
                    if m == 3:
                        free(g)
                    if m == 0:
                        pe.wait_ge(dve_made, at(dve_made, ("og", PG - 1)))
                    product(("ym", m), dve_evacuated,
                            [weight("mup")[:, k, m * P:(m + 1) * P] for k in range(PG)], chunk(o))
                free("mup")
                free("gm1")
                for m in range(DC):
                    g = f"wo{m // 4}"
                    if m % 4 == 0:
                        loaded(g)
                    product_split(("out", m), dve_evacuated, g, m % 4, m_up, m_low,
                                  before=(lambda k: pe.wait_ge(dve_made, at(dve_made, ("mlow", k))))
                                  if m == 0 else None)
                    if m % 4 == 3:
                        free(g)
                drained()
                n.leave()

            def product2(label, reader, lhs, rhs, before=None):
                dst = accumulator(label, reader)
                for k, w in enumerate(lhs):
                    if before:
                        before(k)
                    ins = nc.tensor.matmul(dst[:, 0, :], w, rhs(k), start=(k == 0), stop=(k == len(lhs) - 1))
                done(ins, label)

            def projection(label, reader, name, j, rhs, before=None):
                if j == 0:
                    loaded(name)
                product2(label, reader, [weight(name)[:, k, j * P:(j + 1) * P] for k in range(DC)], rhs, before)
                if j == 3:
                    free(name)

            on_h2, on = (lambda k: h2[:, k, :]), (lambda x: (lambda k: x))
            product2("ss_1", act_evacuated, [ones[:, :]] * DC, lambda k: latent[:, k, META:T],
                     before=lambda k: pe.wait_ge(squared, at(squared, ("sq", k))))

            def qk_sum(c):
                pe.wait_ge(act_evacuated, at(act_evacuated, ("qk", c)))
                product2(("qkss", c), act_evacuated, [blocks], on(tmp[c % 2]))

            def qk_turn(c):
                pe.wait_ge(dve_made, at(dve_made, ("qkn", c)))
                product2(("qkrot", c), dve_evacuated, [rot2], on(qk[:, c, 0:S]))

            for c in range(2 * DC + 2):
                if c < 2 * DC:
                    name = ("q0", "q1", "k0", "k1")[c // 4]
                    projection(("qk", c), act_evacuated, name, c % 4, on_h2,
                               before=(lambda k: pe.wait_ge(dve_made, at(dve_made, ("h1", k)))) if c == 0 else None)
                if 1 <= c <= 2 * DC:
                    qk_sum(c - 1)
                if c >= 2:
                    qk_turn(c - 2)
            for g in range(2):
                name = f"v{g}"
                loaded(name)
                for j in range(QT):
                    dst = accumulator(("v2", g, j), act_evacuated)
                    for k in range(DC):
                        ins = nc.tensor.matmul(dst[:, 0, :], h2[:, k, j * P:(j + 1) * P], weight(name)[:, k, :],
                                               start=(k == 0), stop=(k == DC - 1))
                    done(ins, ("v2", g, j))
                free(name)

            def scores2(s):
                hd, i = items2[s]
                if s == 0:
                    pe.wait_ge(dve_made, at(dve_made, ("qkr", 2 * DC - 1)))
                dst = accumulator(("s2", s), act_evacuated)
                for c in range(2):
                    r = slice(SUB * c, SUB * c + SUB)
                    ins = nc.tensor.matmul(dst[:, c, :], q2[r, hd, i * P:(i + 1) * P], k2[r, hd, :],
                                           start=True, stop=True)
                done(ins, ("s2", s))

            def turn2(s):
                pe.wait_ge(dve_made, at(dve_made, ("p2", s)))
                dst = accumulator(("t2", s), act_evacuated)
                for j in range(QT):
                    ins = nc.tensor.transpose(dst[:, 0, j * P:(j + 1) * P], probs2[s % 3][0][:, j * P:(j + 1) * P],
                                              ident)
                done(ins, ("t2", s))

            def values2(s):
                hd, i = items2[s]
                pe.wait_ge(act_evacuated, at(act_evacuated, ("t2", s)))
                dst = accumulator(("o2", s), act_evacuated)
                for j in range(QT):
                    ins = nc.tensor.matmul(dst[:, 0, 0:P], v2[:, j, hd * P:(hd + 1) * P], probsT2[s % 4][:, j, :],
                                           start=(j == 0), stop=(j == QT - 1))
                done(ins, ("o2", s))

            for s in range(STEPS2):
                if s < len(items2):
                    scores2(s)
                for c in background2_at(s):
                    projection(("lx", c), act_evacuated, f"lx{c // 4}", c % 4, on_h2)
                if 2 <= s < len(items2) + 2:
                    turn2(s - 2)
                if s >= 3:
                    values2(s - 3)
            for c in range(DC + LAG):
                if c < DC:
                    projection(("lg", c), act_evacuated, f"lg{c // 4}", c % 4, on_h2)
                if c >= LAG:
                    pe.wait_ge(act_made, at(act_made, ("sqo", c - LAG)))
                    product2(("oss", c - LAG), act_evacuated, [ones[:, :]], on(tmp[(c - LAG) % 2]))

            def lru(u):
                d, c = lru_units[u]
                if d == 0:
                    pe.wait_ge(pool_made, at(pool_made, ("conv", c)))
                dst = accumulator(("lru", u), act_evacuated)
                for kind in range(2):
                    ins = nc.tensor.matmul(dst[:, kind, :], weight("lru")[:, 16 * kind + 8 * d + c, :],
                                           lru_x[:, c, 0:S], start=True, stop=True)
                done(ins, ("lru", u))

            loaded("lru")
            for m in range(DC):
                if m:
                    lru(2 * m)
                    lru(2 * m + 1)
                if m == DC - 1:
                    free("lru")
                projection(("ga", m), act_evacuated, f"ga{m // 4}", m % 4, on_h2)
                projection(("ya", m), dve_evacuated, f"ao{m // 4}", m % 4, lambda k: q2[:, k, :],
                           before=(lambda k: pe.wait_ge(dve_made, at(dve_made, ("on", k)))) if m == 0 else None)
                if m == 0:
                    lru(0)
                    lru(1)
            for m in range(DC):
                projection(("gl", m), act_evacuated, f"gl{m // 4}", m % 4, on_h2)
                projection(("yl", m), dve_evacuated, f"lo{m // 4}", m % 4, lambda k: gelu[k],
                           before=(lambda k: pe.wait_ge(dve_made, at(dve_made, ("lru_y", k)))) if m == 0 else None)
            for m in range(DC):
                projection(("out2", m), dve_evacuated, f"xo{m // 4}", m % 4, lambda k: merged[:, k, :],
                           before=(lambda k: pe.wait_ge(dve_made, at(dve_made, ("mg2", k)))) if m == 0 else None)
            product2("ss_2", act_evacuated, [ones[:, :]] * DC, lambda k: merged[:, k, :],
                     before=lambda k: pe.wait_ge(act_made, at(act_made, ("sq2", k))))
            for i in range(QT):
                dst = accumulator(("x_tok", i), act_evacuated).rearrange("p a b -> p (a b)")
                for c in range(DC):
                    ins = nc.tensor.transpose(dst[:, c * P:(c + 1) * P], xr[:, c, i * P:(i + 1) * P], ident)
                done(ins, ("x_tok", i))
            dst = accumulator("logits", dve_evacuated)
            for i in range(QT):
                for k in range(DC):
                    if i == 0:
                        pe.wait_ge(dve_made, at(dve_made, ("h3", k)))
                    ins = nc.tensor.matmul(dst[:, 0, 20 * i:20 * i + 20], h2[:, k, i * P:(i + 1) * P],
                                           router[:, k, :], start=(k == 0), stop=(k == DC - 1))
            done(ins, "logits")
            for i in range(QT):
                dst = accumulator(("h_tok", i), act_evacuated).rearrange("p a b -> p (a b)")
                for c in range(DC):
                    ins = nc.tensor.transpose(dst[:, c * P:(c + 1) * P], h2[:, c, i * P:(i + 1) * P], ident)
                done(ins, ("h_tok", i))
            pe.wait_ge(dve_made, at(dve_made, "chosen"))
            dst = accumulator("places", dve_evacuated)
            chosen = R[:, R_M:R_M + 64]
            for i in range(QT):
                for j in range(i + 1):
                    lhs = const[:, K_LT:K_LT + P] if j == i else ones[:, :]
                    nc.tensor.matmul(dst[:, 0, 16 * i:16 * i + 16], lhs, chosen[:, 16 * j:16 * j + 16],
                                     start=(j == 0), stop=(j == i))
            for j in range(QT):
                ins = nc.tensor.matmul(dst[:, 0, 64:80], ones[:, :], chosen[:, 16 * j:16 * j + 16],
                                       start=(j == 0), stop=(j == QT - 1))
            done(ins, "places")
            dst = accumulator("rows_of", dve_evacuated)
            for e in range(EXPERTS):
                pe.wait_ge(dve_made, at(dve_made, ("pick", e)))
                for i in range(QT):
                    ins = nc.tensor.matmul(dst[:, 0, e:e + 1], picks[e % 2][:, i, :],
                                           const[:, K_TOKEN + i:K_TOKEN + i + 1], start=(i == 0), stop=(i == QT - 1))
                ins.then_inc(picked, 1)
                mark(picked, ("pick", e))
            pe.wait_ge(picked, at(picked, ("pick", EXPERTS - 1)))
            done(pe.drain(), "rows_of")
            drained()

            BANK = {"g": acc[:, 0, 0, :], "u": acc[:, 0, 1, :], "ht": acc[:, 3, 0, :], "pick": acc[:, 3, 1, :]}
            TWO = {"xt": acc[:, 1, :, :], "y": acc[:, 2, :, :]}

            def turn_tokens(label, arrived):
                pe.wait_ge(x_gathered, arrived)
                for c in range(DC):
                    ins = nc.tensor.transpose(TWO["xt"].rearrange("p a b -> p (a b)")[:, c * P:(c + 1) * P],
                                              x_gath[:, c * P:(c + 1) * P], ident)
                done(ins, label)

            def weights_of(name, expert):
                slot = shapes1[name][0]
                pe.wait_ge(w_loaded[slot], at(w_loaded[slot], name) if expert is None else
                           in_pass(w_loaded[slot], name, expert - (name != "down")))

            def into_hidden(x, tag, over="", expert=None):
                name = {"g": "gate", "u": "up"}[x] + over
                weights_of(name, expert)
                for k in range(DC):
                    ins = nc.tensor.matmul(BANK[x], x_exp[:, k, :], weight(name)[:, k, :], start=(k == 0),
                                           stop=(k == DC - 1))
                done(ins, (x, tag))
                slot = shapes1[name][0]
                pe.drain().then_inc(w_free[slot], 1)
                mark(w_free[slot], ("used", name) if tag == over else None)

            def turn_hidden(tag):
                for k in range(HID // P):
                    ins = nc.tensor.transpose(BANK["ht"][:, k * P:(k + 1) * P], hid[:, k * P:(k + 1) * P], ident)
                done(ins, ("ht", tag))

            def out_of_hidden(tag, over="", expert=None):
                weights_of("down" + over, expert)
                for half in range(2):
                    for k in range(HID // P):
                        ins = nc.tensor.matmul(TWO["y"][:, half, :], hid_t[:, k, :],
                                               weight("down" + over)[:, k, half * 512:(half + 1) * 512],
                                               start=(k == 0), stop=(k == HID // P - 1))
                done(ins, ("y", tag))
                slot = shapes1["down"][0]
                pe.drain().then_inc(w_free[slot], 1)
                mark(w_free[slot], ("used", "down" + over) if tag == over else None)

            turn_tokens("xt0", at(x_gathered, "x0"))
            pe.wait_ge(act_evacuated, at(act_evacuated, "xt0"))
            into_hidden("g", "first", expert=0)
            into_hidden("u", "first", expert=0)
            turn_tokens("xt1", in_pass(x_gathered, ("x", ""), 0))
            pe.wait_ge(act_evacuated, at(act_evacuated, "xt1"))
            pe.wait_ge(dve_evacuated, at(dve_evacuated, ("u", "first")))
            with pe.Fori(0, EXPERTS - 1) as e:
                n.enter("experts", e, EXPERTS - 1)
                pe.wait_ge(act_evacuated, at(act_evacuated, ("xt", ""), back=1))
                into_hidden("g", "", expert=e + 1)
                pe.wait_ge(dve_evacuated, at(dve_evacuated, ("u", ""), back=1))
                turn_hidden("")
                into_hidden("u", "", expert=e + 1)
                turn_tokens(("xt", ""), in_pass(x_gathered, ("x", ""), e + 1))
                pe.wait_ge(dve_evacuated, at(dve_evacuated, ("ht", "")))
                pe.wait_ge(act_evacuated, at(act_evacuated, ("y", ""), back=1))
                out_of_hidden("", expert=e)
                n.leave()
            pe.wait_ge(dve_evacuated, at(dve_evacuated, ("u", "")))
            turn_hidden("last")
            pe.wait_ge(dve_evacuated, at(dve_evacuated, ("ht", "last")))
            pe.wait_ge(act_evacuated, at(act_evacuated, ("y", "")))
            out_of_hidden("last", expert=EXPERTS - 1)
            pe.wait_ge(dve_made, at(dve_made, "over"))
            pe.wait_ge(act_evacuated, at(act_evacuated, ("y", "last")))
            tiles = pe.value_load(over_i[0:1, 0:1], min_val=0, max_val=OVER)
            with pe.If(tiles > 0):
                with pe.Fori(0, tiles) as k:
                    n.enter("over", k, 1)
                    pe.wait_ge(dve_made, at(dve_made, ("pick", "+")))
                    pe.sem_inc(held, 1)
                    for i in range(QT):
                        ins = nc.tensor.matmul(BANK["pick"][:, 0:1], picks[0][:, i, :],
                                               const[:, K_TOKEN + i:K_TOKEN + i + 1], start=(i == 0), stop=(i == QT - 1))
                    done(ins, ("pick", "+"))
                    turn_tokens(("xt", "+"), at(x_gathered, ("x", "+")))
                    pe.wait_ge(act_evacuated, at(act_evacuated, ("xt", "+")))
                    into_hidden("g", "+", "+")
                    into_hidden("u", "+", "+")
                    pe.wait_ge(dve_evacuated, at(dve_evacuated, ("u", "+")))
                    turn_hidden("+")
                    pe.wait_ge(dve_evacuated, at(dve_evacuated, ("ht", "+")))
                    pe.wait_ge(act_evacuated, at(act_evacuated, ("y", "+"), back=1))
                    out_of_hidden("+", "+")
                    n.leave()

        @block.scalar
        def _(act):
            def result(label):
                act.wait_ge(psum_filled, at(psum_filled, label))
                slot = known.slots[label] if known else 0
                return acc[:, slot, :, 0:HALF]

            def flat2(x):
                return x.rearrange("p (a t) -> p a t", a=2)

            for i in range(4):
                act.dma_start(xin[:, i, :], a["x"][0, i * P:(i + 1) * P, :]).then_inc(x_loaded, 16)
            act.dma_start(metain[0:META, :], a["meta_tokens"]).then_inc(x_loaded, 16)
            act.wait_ge(dve_made, at(dve_made, "angles"))
            nc.scalar.activation(sinT, krope[NOPE:QK, 0, :], ACT.Sin).then_inc(act_made, 1)
            mark(act_made)
            nc.scalar.activation(cosT, krope[NOPE:QK, 1, :], ACT.Sin, scale=-1.0,
                                 bias=small[NOPE:QK, 0:1]).then_inc(act_made, 1)
            mark(act_made, "trig")

            def squares(c, of, label):
                act.wait_ge(dve_evacuated, at(dve_evacuated, of))
                nc.scalar.activation(latent[:, c, :], hres[:, c, :], ACT.Square).then_inc(squared, 1)
                mark(squared, label)

            def upper(dst, src, label):
                nc.scalar.activation(dst, src, ACT.Copy).then_inc(act_made, 1)
                mark(act_made, label)

            def weights_upper(jobs_, i):
                if i < len(jobs_):
                    label, name, j = jobs_[i]
                    slot = shapes1[name][0]
                    act.wait_ge(w_loaded[slot], at(w_loaded[slot], name))
                    if i >= 2:
                        act.wait_ge(psum_filled, at(psum_filled, jobs_[i - 2][0]))
                        act.sem_inc(held, 1)
                    upper(w_up[i % 2], columns(name, j), ("wup",) + label)

            for c in range(DC):
                squares(c, ("x", c), ("sq0", c))
            with act.Fori(0, LAYERS) as layer:
                n.enter("layer", layer, LAYERS)

                def root(label, dst, width, rows_=P):
                    src = result(label)
                    nc.scalar.activation(flat2(dst), src[0:rows_], ACT.Sqrt, scale=1.0 / width,
                                         bias=small[0:rows_, 1:2]).then_inc(act_evacuated, 1)
                    mark(act_evacuated, label)

                root("ss_h", work[:, 0, :], D)
                for i in range(2):
                    weights_upper(JOBS_A, i)
                for c in range(DC):
                    act.wait_ge(dve_made, at(dve_made, ("h", c)))
                    upper(h_up[c], h[:, c, :], ("hup", c))
                for c in range(QC + KC):
                    src = result(("c", c))
                    if c == 0:
                        act.wait_ge(dve_made, at(dve_made, ("h", DC - 1)))
                    nc.scalar.activation(flat2(work[:, c, :]), src, ACT.Square)
                    nc.scalar.activation(flat2(latent[:, c, :]), src, ACT.Copy).then_inc(act_evacuated, 1)
                    mark(act_evacuated, ("c", c))
                    if c >= 2:
                        weights_upper(JOBS_A, c)
                weights_upper(JOBS_A, DC)
                root("ss_cq", work[:, 0, :], QR)
                root("ss_ckv", work[:, 1, :], KVR)
                weights_upper(JOBS_A, DC + 1)
                src = result("rope")
                for i in range(2):
                    ins = nc.scalar.activation(flat2(work[NOPE:QK, 2 + i, :]), src[NOPE:QK], ACT.Square)
                ins.then_inc(act_made, 1)
                mark(act_made, "sq_rope")
                for i, (t0, nt) in enumerate(TILES):
                    result(("v", i))
                    slot = known.slots["v", i] if known else 0
                    nc.scalar.activation(v[0:nt, i, :], acc[0:nt, slot, 0, :], ACT.Copy).then_inc(act_evacuated, 1)
                    mark(act_evacuated, ("v", i))

                def head(kind, hd, rows_, dst, sq):
                    src = result((kind, hd))
                    if hd >= 2:
                        act.wait_ge(psum_filled, at(psum_filled, (kind + "ss", hd - 2)))
                    nc.scalar.activation(flat2(sq), src[0:rows_], ACT.Square)
                    nc.scalar.activation(flat2(dst), src[0:rows_], ACT.Copy).then_inc(act_evacuated, 1)
                    mark(act_evacuated, (kind, hd))

                def head_root(kind, hd, tile):
                    if hd >= 1:
                        act.wait_ge(dve_made, at(dve_made, (kind + "n", hd - 1)))
                    elif kind == "k":
                        act.wait_ge(dve_made, at(dve_made, ("cn", QC + KC - 1)))
                    root((kind + "ss", hd), work[0:QK, tile, :], QK, QK)

                for hd in range(HEADS + 1):
                    if hd < HEADS:
                        if hd == 0:
                            act.wait_ge(pool_made, at(pool_made, ("krep", 0)))
                        head("k", hd, NOPE, kT[0:NOPE, hd, :], work[0:NOPE, 2 + hd % 2, :])
                        head("q", hd, QK, qT[0:QK, hd, :], work[0:QK, 4 + hd % 2, :])
                    if hd >= 1:
                        head_root("k", hd - 1, 0)
                        head_root("q", hd - 1, 1)

                def gate_free(x):
                    i = gate_no[x]
                    if i >= 2:
                        y = gate_reader(gate_order[i - 2])
                        s_ = dve_evacuated if y[0] in ("z", "yp") else dve_made
                        act.wait_ge(s_, at(s_, y))
                    return gate[:, i % 2, :]

                def back(x):
                    if x[0] in ("z", "gp"):
                        src = result(x)
                        dst = gate_free(x)
                        ins = nc.scalar.activation(flat2(dst), src, ACT.Tanh, scale=0.5)
                        if x[0] == "z":
                            ins.then_inc(act_made, 1)
                            mark(act_made, ("tanh",) + x)
                        else:
                            ins.then_inc(act_evacuated, 1)
                            mark(act_evacuated, x)

                for s in range(STEPS):
                    if s < len(items):
                        hd, i = items[s]
                        t0, nt = TILES[i]
                        result(("s", s))
                        slot = known.slots["s", s] if known else 0
                        act.wait_ge(dve_made, at(dve_made, ("max", s)))
                        if s >= 3:
                            act.wait_ge(psum_filled, at(psum_filled, ("t", s - 3)))
                        nc.scalar.activation(
                            probs[s % 3][0:nt, 0:t0 + nt],
                            acc[0:nt, slot, :, :].rearrange("p a b -> p (a b)")[:, 0:t0 + nt],
                            ACT.Exp, scale=SCALE1, bias=small[0:nt, 2 + s % 3:3 + s % 3],
                            accum_out=small[0:nt, 5 + s % 3:6 + s % 3]).then_inc(act_evacuated, 1)
                        mark(act_evacuated, ("s", s))
                    for x in background_at(s):
                        back(x)
                    if 2 <= s < len(items) + 2:
                        hd, i = items[s - 2]
                        nt = TILES[i][1]
                        result(("t", s - 2))
                        slot = known.slots["t", s - 2] if known else 0
                        src = acc[:, slot, :, :].rearrange("p a (b q) -> p (a b) q", q=P)
                        if s >= 4:
                            act.wait_ge(psum_filled, at(psum_filled, ("o", s - 4)))
                        ins = nc.scalar.activation(probsT[s % 2][0:META, 0, 0:nt], src[0:META, 0, 0:nt], ACT.Copy)
                        if i:
                            ins = nc.scalar.activation(probsT[s % 2][:, 1:i + 1, 0:nt], src[:, 1:i + 1, 0:nt], ACT.Copy)
                        ins.then_inc(act_evacuated, 1)
                        mark(act_evacuated, ("t", s - 2))
                    if s >= 3:
                        hd, i = items[s - 3]
                        t0, nt = TILES[i]
                        result(("o", s - 3))
                        slot = known.slots["o", s - 3] if known else 0
                        r = VD * (hd % 2)
                        nc.scalar.activation(o[r:r + VD, hd // 2, t0:t0 + nt], acc[r:r + VD, slot, 0, 0:nt],
                                             ACT.Copy).then_inc(act_evacuated, 1)
                        mark(act_evacuated, ("o", s - 3))

                for c in range(DC):
                    upper(h_up[c], h[:, c, :], ("hup2", c))
                for i in range(2):
                    weights_upper(JOBS_C, i)
                for c in range(PG):
                    src = result(("zm", c))
                    nc.scalar.activation(flat2(gate_free(("zm", c))), src, ACT.Tanh, scale=0.5).then_inc(act_made, 1)
                    mark(act_made, ("tanh", "zm", c))
                    if c >= 2:
                        weights_upper(JOBS_C, c)

                def merged_upper(m):
                    act.wait_ge(dve_made, at(dve_made, ("mg", m)))
                    upper(m_up[m], work[:, m, :], ("mup", m))

                for m in range(DC):
                    src = result(("gm", m))
                    nc.scalar.activation(flat2(gate_free(("gm", m))), src, ACT.Tanh, scale=0.5)\
                        .then_inc(act_evacuated, 1)
                    mark(act_evacuated, ("gm", m))
                    weights_upper(JOBS_C, m + 4)
                    if m:
                        merged_upper(m - 1)
                merged_upper(DC - 1)
                for m in range(DC):
                    weights_upper(JOBS_C, m + 12)
                    squares(m, ("out", m), ("sq", m))
                n.leave()

            def result2(label):
                act.wait_ge(psum_filled, at(psum_filled, label))
                return acc[:, known.slots[label] if known else 0, 0, :]

            def evacuated(ins, label):
                ins.then_inc(act_evacuated, 1)
                mark(act_evacuated, label)

            def made(ins, label):
                ins.then_inc(act_made, 1)
                mark(act_made, label)

            def root2(label, dst, width):
                evacuated(nc.scalar.activation(dst, result2(label), ACT.Sqrt, scale=1.0 / width,
                                               bias=small[:, 1:2]), label)

            root2("ss_1", tmp[2], D)
            for c in range(2 * DC + 1):
                if c < 2 * DC:
                    src = result2(("qk", c))
                    if c >= 2:
                        act.wait_ge(psum_filled, at(psum_filled, ("qkss", c - 2)))
                    nc.scalar.activation(tmp[c % 2], src, ACT.Square)
                    evacuated(nc.scalar.activation(qk[:, c, 0:S], src, ACT.Copy), ("qk", c))
                if c >= 1:
                    i = c - 1
                    if i < 2:
                        act.wait_ge(dve_made, at(dve_made, ("h1", DC - 1)))
                    else:
                        act.wait_ge(dve_made, at(dve_made, ("qkn", i - 2)))
                    root2(("qkss", i), tmp[2 + i % 2], SUB)
            for g in range(2):
                for j in range(QT):
                    evacuated(nc.scalar.activation(v2[:, j, g * S:(g + 1) * S], result2(("v2", g, j)), ACT.Copy),
                              ("v2", g, j))
            act.wait_ge(dve_made, at(dve_made, "lam_sums"))
            made(nc.scalar.activation(small[:, 10:12], small[:, 8:10], ACT.Exp), "lam_exp")
            for s in range(STEPS2):
                if s < len(items2):
                    act.wait_ge(psum_filled, at(psum_filled, ("s2", s)))
                    act.wait_ge(dve_made, at(dve_made, ("max2", s)))
                    if s >= 3:
                        act.wait_ge(psum_filled, at(psum_filled, ("t2", s - 3)))
                    slot = known.slots["s2", s] if known else 0
                    for c in range(2):
                        b = 2 * (s % 2) + c
                        ins = nc.scalar.activation(probs2[s % 3][c], acc[:, slot, c, :], ACT.Exp, scale=SCALE2,
                                                   bias=rt[:, 0, b:b + 1], accum_out=rt[:, 0, 4 + b:5 + b])
                    evacuated(ins, ("s2", s))
                for c in background2_at(s):
                    evacuated(nc.scalar.activation(lru_x[:, c, 1:1 + S], result2(("lx", c)), ACT.Copy), ("lx", c))
                if 2 <= s < len(items2) + 2:
                    src = result2(("t2", s - 2)).rearrange("p (j q) -> p j q", j=QT)
                    if s >= 6:
                        act.wait_ge(psum_filled, at(psum_filled, ("o2", s - 6)))
                    evacuated(nc.scalar.activation(probsT2[(s - 2) % 4], src, ACT.Copy), ("t2", s - 2))
                if s >= 3:
                    hd, i = items2[s - 3]
                    evacuated(nc.scalar.activation(q2[:, hd, i * P:(i + 1) * P], result2(("o2", s - 3))[:, 0:P],
                                                   ACT.Copy), ("o2", s - 3))
            act.wait_ge(dve_made, at(dve_made, "neg_abs"))
            made(nc.scalar.activation(decay[:, 1, :], decay[:, 1, :], ACT.Exp), "lam_e")
            def output_squares(c):
                if c >= 2:
                    act.wait_ge(psum_filled, at(psum_filled, ("oss", c - 2)))
                act.wait_ge(act_evacuated, at(act_evacuated, ("o2", len(items2) - 1)))
                made(nc.scalar.activation(tmp[c % 2], q2[:, c, :], ACT.Square), ("sqo", c))

            for c in range(2):
                output_squares(c)
            for c in range(DC + LAG):
                if c < DC:
                    evacuated(nc.scalar.activation(gelu[c], result2(("lg", c)), ACT.Copy), ("lg", c))
                if c >= LAG:
                    i = c - LAG
                    if i >= 2:
                        act.wait_ge(dve_made, at(dve_made, ("on", i - 2)))
                    elif i == 0:
                        act.wait_ge(pool_made, at(pool_made, ("conv", DC - 1)))
                    root2(("oss", i), tmp[2 + i % 2], P)
                    if i + 2 < DC:
                        output_squares(i + 2)
            act.wait_ge(act_evacuated, at(act_evacuated, ("lg", DC - 1)))
            for c in range(DC):
                made(nc.scalar.activation(gelu[c], gelu[c], ACT.Gelu_apprx_tanh), ("gelu", c))

            def lru_gates(u):
                d, c = lru_units[u]
                act.wait_ge(psum_filled, at(psum_filled, ("lru", u)))
                slot = known.slots["lru", u] if known else 0
                if u:
                    act.wait_ge(dve_made, at(dve_made, ("lru_in", u - 1)))
                else:
                    act.wait_ge(dve_made, at(dve_made, ("on", DC - 1)))
                b = V_BA - V_BG + 8 * d + c
                nc.scalar.activation(tmp[0], acc[:, slot, 0, :], ACT.Tanh, scale=0.5, bias=half_bias[:, b:b + 1])
                b += V_BI - V_BA
                evacuated(nc.scalar.activation(tmp[1], acc[:, slot, 1, :], ACT.Tanh, scale=0.5,
                                               bias=half_bias[:, b:b + 1]), ("lru", u))
                act.wait_ge(dve_made, at(dve_made, ("lru_z", u)))
                if u >= 4:
                    act.wait_ge(dve_made, at(dve_made, ("scan", u - 4)))
                made(nc.scalar.activation(unit_tiles(u)[0], tmp[2], ACT.Exp, scale=-1.0), ("lru_a", u))
                made(nc.scalar.activation(tmp[3], tmp[2], ACT.Tanh), ("lru_t", u))

            def gate2(label, col, i):
                src = result2(label)
                if i < 2:
                    act.wait_ge(psum_filled, at(psum_filled, ("t2", len(items2) - 1)))
                if label[0] == "ga" and i >= 2:
                    act.wait_ge(dve_evacuated, at(dve_evacuated, ("ya", i - 2)))
                elif label[0] == "gl":
                    j = i - DC
                    if j < 2:
                        act.wait_ge(dve_evacuated, at(dve_evacuated, ("ya", DC - 2 + j)))
                    else:
                        act.wait_ge(dve_made, at(dve_made, ("mg2", j - 2)))
                evacuated(nc.scalar.activation(gate[:, i % 2, 0:S], src, ACT.Tanh, scale=0.5,
                                               bias=half_bias[:, col:col + 1]), label)

            for m in range(DC):
                if m:
                    lru_gates(2 * m)
                    lru_gates(2 * m + 1)
                gate2(("ga", m), m, m)
                if m == 0:
                    lru_gates(0)
                    lru_gates(1)
                if m % 2 == 1:
                    for u in range(4 * (m // 2), 4 * (m // 2) + 4):
                        act.wait_ge(dve_made, at(dve_made, ("lru_f", u)))
                        made(nc.scalar.activation(unit_tiles(u)[2], unit_tiles(u)[2], ACT.Sqrt, scale=0.5),
                             ("lru_m", u))
            for m in range(DC):
                gate2(("gl", m), DC + m, DC + m)
            act.wait_ge(dve_evacuated, at(dve_evacuated, ("out2", DC - 1)))
            for c in range(DC):
                made(nc.scalar.activation(merged[:, c, :], xr[:, c, :], ACT.Square), ("sq2", c))
            root2("ss_2", tmp[2], D)

            def both(label):
                act.wait_ge(psum_filled, at(psum_filled, label))
                return acc[:, known.slots[label] if known else 0, :, :].rearrange("p a b -> p (a b)")

            for i in range(QT):
                evacuated(nc.scalar.activation(x_tok[:, i, :], both(("x_tok", i)), ACT.Copy), ("x_tok", i))
            act.wait_ge(dve_made, at(dve_made, "shifted"))
            made(nc.scalar.activation(R[:, R_X:R_X + 80], R[:, R_X:R_X + 80], ACT.Exp), "shares")
            for i in range(QT):
                evacuated(nc.scalar.activation(h_tok[:, i, :], both(("h_tok", i)), ACT.Copy), ("h_tok", i))

            def turned(label):
                act.wait_ge(psum_filled, at(psum_filled, label))
                evacuated(nc.scalar.activation(x_exp, acc[:, 1, :, :].rearrange("p a (k s) -> p (a k) s", s=P),
                                               ACT.Copy), label)

            def gated(tag, back=0):
                act.wait_ge(psum_filled, at(psum_filled, ("g", tag)))
                if tag != "first":
                    act.wait_ge(dve_evacuated, at(dve_evacuated, ("ht", tag), back=back))
                evacuated(nc.scalar.activation(hid, acc[:, 0, 0, :], ACT.Silu), ("g", tag))

            def results(over, row):
                act.wait_ge(psum_filled, at(psum_filled, ("y", over)))
                act.wait_ge(y_stored, at(y_stored, ("y", ""), back=0) if over == "last" else
                            at(y_stored, ("y", over), back=1))
                evacuated(nc.scalar.activation(y_out, acc[:, 2, :, :].rearrange("p a b -> p (a b)"), ACT.Copy),
                          ("y", over))
                act.wait_ge(act_evacuated, at(act_evacuated, ("y", over)))
                act.sem_inc(held, 1)
                act.dma_start(y_rows[bass.ds(row, P), :], y_out).then_inc(y_stored, 16)
                mark(y_stored, ("y", over), 16)

            act.sem_inc(y_stored, 1)
            mark(y_stored)
            turned("xt0")
            act.wait_ge(act_evacuated, at(act_evacuated, "xt0"))
            act.sem_inc(turned_x, 1)
            gated("first")
            turned("xt1")
            act.wait_ge(act_evacuated, at(act_evacuated, "xt1"))
            act.sem_inc(turned_x, 1)
            with act.Fori(0, EXPERTS - 1) as e:
                n.enter("experts", e, EXPERTS - 1)
                gated("")
                turned(("xt", ""))
                act.wait_ge(act_evacuated, at(act_evacuated, ("xt", "")))
                act.sem_inc(turned_x, 1)
                results("", e * P)
                n.leave()
            results("last", (EXPERTS - 1) * P)
            act.wait_ge(y_zeroed, 16 * OVER)
            act.wait_ge(dve_made, at(dve_made, "over"))
            tiles = act.value_load(over_i[0:1, 0:1], min_val=0, max_val=OVER)
            with act.If(tiles > 0):
                with act.Fori(0, tiles) as k:
                    n.enter("over", k, 1)
                    turned(("xt", "+"))
                    gated("+", back=1)
                    results("+", k * P + EXPERTS * P)
                    n.leave()
            act.wait_ge(y_stored, tiles * 16 + (1 + 16 * EXPERTS))
            act.sem_inc(all_stored, 1)

        @block.vector
        def _(dve):
            def result(label):
                dve.wait_ge(psum_filled, at(psum_filled, label))
                slot = known.slots[label] if known else 0
                return acc[:, slot, :, 0:HALF]

            def flat2(x):
                return x.rearrange("p (a t) -> p a t", a=2)

            def chain(ins):
                ins.then_inc(dve_step, 1)
                mark(dve_step)
                dve.wait_ge(dve_step, now(dve_step))

            def made(ins, label):
                ins.then_inc(dve_made, 1)
                mark(dve_made, label)

            def evacuated(ins, label):
                ins.then_inc(dve_evacuated, 1)
                mark(dve_evacuated, label)

            stt, ts = nc.vector.scalar_tensor_tensor, nc.vector.tensor_scalar
            nc.vector.memset(small[:, 0:1], math.pi / 2)
            nc.vector.memset(small[:, 1:2], EPS)
            nc.vector.memset(upad[:, :, 0:PAD], 0.0)
            dve.wait_ge(const_loaded, 32)
            ang, turns = trig[NOPE:QK, 0, :], trig[NOPE:QK, 1, :]
            nc.vector.tensor_copy(ang[:, 0:META], const[NOPE:QK, K_META:K_META + META])
            chain(nc.vector.tensor_copy(ang[:, META:T], krope[NOPE:QK, 0, META:T].bitcast(I32)))
            chain(ts(ang[:, META:T], ang[:, META:T], float(META), None, ALU.add))
            chain(ts(ang, ang, const[NOPE:QK, K_FREQ:K_FREQ + 1], None, ALU.mult))
            big = 1.5 * 2 ** 23
            chain(ts(turns, ang, 1.0 / (2 * math.pi), big, ALU.mult, ALU.add))
            chain(ts(turns, turns, -big, None, ALU.add))
            rest, parts = 2 * math.pi, []
            for bits in (8, 12, 24):
                e = 2.0 ** (bits - 1 - math.floor(math.log2(abs(rest))))
                parts.append(math.trunc(rest * e) / e if bits < 24 else rest)
                rest -= parts[-1]
            for part in parts:
                chain(stt(out=ang, in0=turns, scalar=-part, in1=ang, op0=ALU.mult, op1=ALU.add))
            chain(ts(krope[NOPE:QK, 0, :], ang, 3.1415925, -3.1415925, ALU.min, ALU.max))
            dve.wait_ge(dve_step, now(dve_step))
            made(stt(out=krope[NOPE:QK, 1, :], in0=krope[NOPE:QK, 0, :], scalar=-1.0,
                     in1=krope[NOPE:QK, 0, :], op0=ALU.mult, op1=ALU.max), "angles")

            for c in range(DC):
                result(("x", c))
                slot = known.slots["x", c] if known else 0
                nc.vector.tensor_copy(hres[:, c, 0:META], acc[:, slot, 1, 0:META])
                evacuated(nc.vector.tensor_copy(hres[:, c, META:T], acc[:, slot, 0, :]), ("x", c))
            result("vecs")
            slot = known.slots["vecs"] if known else 0
            evacuated(nc.vector.tensor_copy(vecs[:, :], acc[:, slot, 0, 0:LAYERS * LV]), "vecs")
            result("vec2")
            slot = known.slots["vec2"] if known else 0
            evacuated(nc.vector.tensor_copy(vec2[:, :], acc[:, slot, 0, 0:V_END]), "vec2")
            dve.wait_ge(dve_evacuated, at(dve_evacuated, "vec2"))
            made(ts(half_bias[:, :], vec2[:, V_BG:V_LM], 0.5, None, ALU.mult), "half_bias")
            dve.wait_ge(dve_evacuated, at(dve_evacuated, ("x", DC - 1)))
            with dve.Fori(0, LAYERS) as layer:
                n.enter("layer", layer, LAYERS)
                chain(nc.vector.tensor_copy(lv[:, :], vecs[:, bass.ds(layer * LV, LV)]))
                chain(nc.vector.tensor_copy(small[:, 8:9], lv[:, 21:22]))
                chain(nc.vector.memset(small[NOPE:QK, 8:9], 1.0))

                def inverse(label, tile, rows_=P):
                    dve.wait_ge(act_evacuated, at(act_evacuated, label))
                    chain(nc.vector.reciprocal(work[0:rows_, tile, :], work[0:rows_, tile, :]))

                inverse("ss_h", 0)
                for c in range(DC):
                    made(stt(out=h[:, c, :], in0=hres[:, c, :], scalar=lv[:, c:c + 1], in1=work[:, 0, :],
                             op0=ALU.mult, op1=ALU.mult), ("h", c))
                def lower(dst, src, up, label, of):
                    dve.wait_ge(act_made, at(act_made, of))
                    made(nc.vector.tensor_tensor(dst, src, up.bitcast(F32), ALU.subtract), label)

                def weights_lower(jobs_, i):
                    if i < len(jobs_):
                        label, name, j = jobs_[i]
                        lower(columns(name, j, ring_split), columns(name, j), w_up[i % 2],
                              ("wlow",) + label, ("wup",) + label)

                for c in range(DC):
                    if c == 0:
                        dve.wait_ge(dve_made, at(dve_made, ("h", DC - 1)))
                    lower(h_low[c], h[:, c, :], h_up[c], ("hlow", c), ("hup", c))
                for i in range(DC):
                    weights_lower(JOBS_A, i)

                def pool_in(g):
                    evacuated(nc.vector.tensor_copy(flat2(upad[:, g, PAD:]), result(("u", g))), ("u", g))

                pool_in(0)
                weights_lower(JOBS_A, DC)
                for label, tile, c0, c1 in (("ss_cq", 0, 0, QC), ("ss_ckv", 1, QC, QC + KC)):
                    inverse(label, tile)
                    for c in range(c0, c1):
                        made(stt(out=latent[:, c, :], in0=latent[:, c, :], scalar=lv[:, 8 + c:9 + c],
                                 in1=work[:, tile, :], op0=ALU.mult, op1=ALU.mult), ("cn", c))
                    pool_in(1 + tile)
                    if tile == 0:
                        weights_lower(JOBS_A, DC + 1)
                pool_in(3)
                src = result("rope")
                dve.wait_ge(act_made, at(act_made, "sq_rope"))
                dve.wait_ge(act_made, at(act_made, "trig"))
                evacuated(ts(flat2(krope[NOPE:QK, 0, :]), src[NOPE:QK], lv[NOPE:QK, 21:22], None, ALU.mult), "rope")
                src = result("rotk")
                evacuated(nc.vector.tensor_tensor(flat2(krope[NOPE:QK, 1, :]), src[NOPE:QK], flat2(sinT), ALU.mult),
                          "rotk")
                chain(nc.vector.tensor_tensor(krope[NOPE:QK, 0, :], krope[NOPE:QK, 0, :], cosT, ALU.mult))
                dve.wait_ge(dve_evacuated, at(dve_evacuated, "rotk"))
                made(nc.vector.tensor_tensor(krope[NOPE:QK, 0, :], krope[NOPE:QK, 0, :], krope[NOPE:QK, 1, :],
                                             ALU.add), "kR")
                for g in range(PG):
                    w = 2 ** (g + 1)
                    dve.wait_ge(pool_made, at(pool_made, ("window", g)))
                    win_ = winA if g % 2 == 0 else winB
                    first = const[:, K_CNT + g * PAD:K_CNT + (g + 1) * PAD]
                    chain(nc.vector.tensor_tensor(win_[:, PAD:2 * PAD], win_[:, PAD:2 * PAD], first, ALU.mult))
                    nc.vector.tensor_tensor(upad[:, g, PAD:2 * PAD], win_[:, PAD:2 * PAD],
                                            upad[:, g, PAD:2 * PAD], ALU.subtract)
                    made(stt(out=upad[:, g, 2 * PAD:], in0=win_[:, 2 * PAD:], scalar=1.0 / w,
                             in1=upad[:, g, 2 * PAD:], op0=ALU.mult, op1=ALU.subtract), ("mixed", g))

                def k_norm(hd):
                    inverse(("kss", hd), 0, QK)
                    dve.wait_ge(pool_made, at(pool_made, ("krep", hd)))
                    made(stt(out=kT[0:QK, hd, :], in0=kT[0:QK, hd, :], scalar=small[0:QK, 8:9],
                             in1=work[0:QK, 0, :], op0=ALU.mult, op1=ALU.mult), ("kn", hd))

                def q_norm(hd):
                    inverse(("qss", hd), 1, QK)
                    made(stt(out=qT[0:QK, hd, :], in0=qT[0:QK, hd, :], scalar=lv[0:QK, 20:21],
                             in1=work[0:QK, 1, :], op0=ALU.mult, op1=ALU.mult), ("qn", hd))

                def q_rope(hd):
                    src = result(("rotq", hd))
                    turned = work[NOPE:QK, 6, :]
                    if hd:
                        dve.wait_ge(dve_made, at(dve_made, ("qr", hd - 1)))
                    evacuated(nc.vector.tensor_tensor(flat2(turned), src[NOPE:QK], flat2(sinT), ALU.mult),
                              ("rotq", hd))
                    chain(nc.vector.tensor_tensor(qT[NOPE:QK, hd, :], qT[NOPE:QK, hd, :], cosT, ALU.mult))
                    dve.wait_ge(dve_evacuated, at(dve_evacuated, ("rotq", hd)))
                    made(nc.vector.tensor_tensor(qT[NOPE:QK, hd, :], qT[NOPE:QK, hd, :], turned, ALU.add),
                         ("qr", hd))

                for hd in range(HEADS + 1):
                    if hd < HEADS:
                        k_norm(hd)
                        q_norm(hd)
                    if 1 <= hd < HEADS - 1:
                        q_rope(hd - 1)

                def back(x):
                    kind, m = x
                    src = result(x) if kind != "gp" else None
                    if kind == "z":
                        dve.wait_ge(act_made, at(act_made, ("tanh",) + x))
                        evacuated(stt(out=flat2(zp[:, m, :]), in0=flat2(gate[:, gate_no[x] % 2, :]), scalar=1.0,
                                      in1=src, op0=ALU.add, op1=ALU.mult), x)
                    elif kind == "pg":
                        dve.wait_ge(dve_evacuated, at(dve_evacuated, ("z", m)))
                        evacuated(stt(out=flat2(zp[:, m, :]), in0=src, scalar=lv[:, 16 + m:17 + m],
                                      in1=flat2(zp[:, m, :]), op0=ALU.mult, op1=ALU.mult), x)
                    elif kind == "yp":
                        dve.wait_ge(act_evacuated, at(act_evacuated, ("gp", m)))
                        if m == 0:
                            dve.wait_ge(dve_made, at(dve_made, ("qr", HEADS - 1)))
                        g = gate[:, gate_no["gp", m] % 2, :]
                        evacuated(stt(out=flat2(work[:, m, :]), in0=flat2(g), scalar=1.0, in1=src,
                                      op0=ALU.add, op1=ALU.mult), x)

                def normalise(s):
                    hd, i = items[s]
                    t0, nt = TILES[i]
                    r = small[0:nt, 5 + s % 3:6 + s % 3]
                    dve.wait_ge(act_evacuated, at(act_evacuated, ("s", s)))
                    chain(nc.vector.reciprocal(r, r))
                    made(ts(probs[s % 3][0:nt, 0:t0 + nt], probs[s % 3][0:nt, 0:t0 + nt], r, None, ALU.mult),
                         ("p", s))

                for s in range(STEPS):
                    if s < len(items):
                        hd, i = items[s]
                        t0, nt = TILES[i]
                        result(("s", s))
                        slot = known.slots["s", s] if known else 0
                        src = acc[0:nt, slot, :, :].rearrange("p a b -> p (a b)")
                        top = small[0:nt, 2 + s % 3:3 + s % 3]
                        chain(nc.vector.tensor_tensor(src[:, t0:t0 + nt], src[:, t0:t0 + nt], mask[0:nt, 0:nt],
                                                      ALU.add))
                        chain(nc.vector.tensor_reduce(top, src[:, 0:t0 + nt], AX.X, ALU.max))
                        made(ts(top, top, -SCALE1, None, ALU.mult), ("max", s))
                    if 1 <= s <= len(items):
                        normalise(s - 1)
                    for x in background_at(s):
                        back(x)
                    if s < 2:
                        q_rope(HEADS - 2 + s)

                for c in range(DC):
                    lower(h_low[c], h[:, c, :], h_up[c], ("hlow2", c), ("hup2", c))
                for i in range(2):
                    weights_lower(JOBS_C, i)
                for c in range(PG):
                    src = result(("zm", c))
                    dve.wait_ge(act_made, at(act_made, ("tanh", "zm", c)))
                    g = gate[:, gate_no["zm", c] % 2, :]
                    evacuated(stt(out=flat2(g), in0=flat2(g), scalar=1.0, in1=src, op0=ALU.add, op1=ALU.mult),
                              ("zm", c))
                    dve.wait_ge(dve_evacuated, at(dve_evacuated, ("zm", c)))
                    if c == 0:
                        dve.wait_ge(act_evacuated, at(act_evacuated, ("o", len(items) - 1)))
                    made(nc.vector.tensor_tensor(o[:, c, :], o[:, c, :], g, ALU.mult), ("og", c))
                    if c >= 2:
                        weights_lower(JOBS_C, c)

                def merged_lower(m):
                    lower(m_low[m], work[:, m, :], m_up[m], ("mlow", m), ("mup", m))

                for m in range(DC):
                    weights_lower(JOBS_C, m + 4)
                    if m:
                        merged_lower(m - 1)
                    src = result(("ym", m))
                    dve.wait_ge(act_evacuated, at(act_evacuated, ("gm", m)))
                    g = gate[:, gate_no["gm", m] % 2, :]
                    evacuated(stt(out=flat2(g), in0=flat2(g), scalar=1.0, in1=src, op0=ALU.add, op1=ALU.mult),
                              ("ym", m))
                    dve.wait_ge(dve_evacuated, at(dve_evacuated, ("ym", m)))
                    made(nc.vector.tensor_tensor(work[:, m, :], work[:, m, :], g, ALU.add), ("mg", m))
                merged_lower(DC - 1)
                for m in range(DC):
                    weights_lower(JOBS_C, m + 12)
                    src = result(("out", m))
                    evacuated(stt(out=flat2(hres[:, m, :]), in0=src, scalar=0.25, in1=flat2(hres[:, m, :]),
                                  op0=ALU.mult, op1=ALU.add), ("out", m))
                dve.wait_ge(dve_evacuated, at(dve_evacuated, ("out", DC - 1)))
                n.leave()

            def result2(label):
                dve.wait_ge(psum_filled, at(psum_filled, label))
                return acc[:, known.slots[label] if known else 0, 0, :]

            tt = nc.vector.tensor_tensor

            def inverse2(label, tile):
                dve.wait_ge(act_evacuated, at(act_evacuated, label))
                chain(nc.vector.reciprocal(tmp[tile], tmp[tile]))

            inverse2("ss_1", 2)
            for c in range(DC):
                made(stt(out=h2[:, c, :], in0=xr[:, c, :], scalar=vec2[:, V_N1 + c:V_N1 + c + 1], in1=tmp[2],
                         op0=ALU.mult, op1=ALU.mult), ("h1", c))
            dve.wait_ge(const_loaded, at(const_loaded, "rotary"))

            def qk_turned(c):
                src = result2(("qkrot", c))
                x = qk[:, c, 0:S]
                if c:
                    dve.wait_ge(dve_made, at(dve_made, ("qkr", c - 1)))
                evacuated(tt(tmp[4], src, sin2, ALU.mult), ("qkrot", c))
                chain(tt(x, x, cos2, ALU.mult))
                dve.wait_ge(dve_evacuated, at(dve_evacuated, ("qkrot", c)))
                made(tt(x, x, tmp[4], ALU.add), ("qkr", c))

            for c in range(2 * DC + 1):
                if c < 2 * DC:
                    x = qk[:, c, 0:S]
                    g = V_QN if c < DC else V_KN
                    inverse2(("qkss", c), 2 + c % 2)
                    made(stt(out=x, in0=x, scalar=vec2[:, g:g + 1], in1=tmp[2 + c % 2], op0=ALU.mult,
                             op1=ALU.mult), ("qkn", c))
                if c >= 1:
                    qk_turned(c - 1)
            for i in range(2):
                x, y = lamt[:, 2 * i * SUB:(2 * i + 1) * SUB], lamt[:, (2 * i + 1) * SUB:(2 * i + 2) * SUB]
                chain(tt(x, x, y, ALU.mult))
                ins = nc.vector.tensor_reduce(small[:, 8 + i:9 + i], x, AX.X, ALU.add)
            made(ins, "lam_sums")
            dve.wait_ge(act_made, at(act_made, "lam_exp"))
            chain(tt(small[:, 12:13], small[:, 11:12], small[:, 10:11], ALU.subtract))
            chain(ts(small[:, 12:13], small[:, 12:13], -LAM_INIT, None, ALU.add))
            nc.vector.memset(lru_x[:, :, 0:1], 0.0)
            made(nc.vector.memset(lru_x[:, :, 1 + S:3 + S], 0.0), "lru_pad")

            def weigh(s):
                dve.wait_ge(act_evacuated, at(act_evacuated, ("s2", s)))
                b = 4 + 2 * (s % 2)
                chain(nc.vector.reciprocal(rt[:, 0, b:b + 2], rt[:, 0, b:b + 2]))
                chain(ts(rt[:, 0, b + 1:b + 2], rt[:, 0, b + 1:b + 2], small[:, 12:13], None, ALU.mult))
                p0, p1 = probs2[s % 3]
                chain(ts(p1, p1, rt[:, 0, b + 1:b + 2], None, ALU.mult))
                made(stt(out=p0, in0=p0, scalar=rt[:, 0, b:b + 1], in1=p1, op0=ALU.mult, op1=ALU.add), ("p2", s))

            for s in range(STEPS2):
                if s < len(items2):
                    dve.wait_ge(psum_filled, at(psum_filled, ("s2", s)))
                    slot = known.slots["s2", s] if known else 0
                    b = 2 * (s % 2)
                    chain(nc.vector.tensor_reduce(rt[:, 0, b:b + 2], acc[:, slot, :, :], AX.X, ALU.max))
                    made(ts(rt[:, 0, b:b + 2], rt[:, 0, b:b + 2], -SCALE2, None, ALU.mult), ("max2", s))
                if 1 <= s <= len(items2):
                    weigh(s - 1)

            lam = vec2[:, V_LM:V_LM + 16]
            d_ = [decay[:, i, :] for i in range(6)]
            chain(ts(d_[0], lam, -1.0, None, ALU.mult))
            made(tt(d_[1], d_[0], lam, ALU.min), "neg_abs")
            dve.wait_ge(act_made, at(act_made, "lam_e"))
            chain(ts(d_[2], d_[1], 2.0, None, ALU.add))
            chain(nc.vector.reciprocal(d_[2], d_[2]))
            chain(tt(d_[2], d_[2], d_[1], ALU.mult))
            chain(tt(d_[3], d_[2], d_[2], ALU.mult))
            chain(ts(d_[4], d_[3], 1.0 / 17, 1.0 / 15, ALU.mult, ALU.add))
            for i in range(13, 0, -2):
                chain(tt(d_[4], d_[4], d_[3], ALU.mult))
                chain(ts(d_[4], d_[4], 1.0 / i, None, ALU.add))
            chain(tt(d_[4], d_[4], d_[2], ALU.mult))
            chain(ts(d_[0], d_[0], 0.0, 4.0, ALU.max, ALU.mult))
            chain(stt(out=d_[5], in0=d_[4], scalar=8.0, in1=d_[0], op0=ALU.mult, op1=ALU.add))

            for c in range(DC):
                if c >= 2:
                    dve.wait_ge(pool_made, at(pool_made, ("conv", c - 2)))
                elif c == 0:
                    dve.wait_ge(act_evacuated, at(act_evacuated, ("lx", DC - 1)))
                y = tmp[2 + c % 2]
                for j in range(TAPS):
                    x, w = lru_x[:, c, j:j + S], vec2[:, V_CW + 8 * j + c:V_CW + 8 * j + c + 1]
                    if j == 0:
                        chain(ts(y, x, w, vec2[:, V_CB + c:V_CB + c + 1], ALU.mult, ALU.add))
                    elif j < TAPS - 1:
                        chain(stt(out=y, in0=x, scalar=w, in1=y, op0=ALU.mult, op1=ALU.add))
                    else:
                        made(stt(out=y, in0=x, scalar=w, in1=y, op0=ALU.mult, op1=ALU.add), ("conv", c))
            for c in range(DC):
                inverse2(("oss", c), 2 + c % 2)
                if c == 0:
                    chain(ts(small[:, 13:14], vec2[:, V_SUB:V_SUB + 1], 1.0 - LAM_INIT, None, ALU.mult))
                made(stt(out=q2[:, c, :], in0=q2[:, c, :], scalar=small[:, 13:14], in1=tmp[2 + c % 2],
                         op0=ALU.mult, op1=ALU.mult), ("on", c))

            def lru_unit(u):
                d, c = lru_units[u]
                dve.wait_ge(act_evacuated, at(act_evacuated, ("lru", u)))
                if u:
                    dve.wait_ge(act_made, at(act_made, ("lru_t", u - 1)))
                made(ts(tmp[2], tmp[0], 1.0, decay[:, 5, 8 * d + c:8 * d + c + 1], ALU.add, ALU.mult), ("lru_z", u))
                made(stt(out=unit_tiles(u)[1], in0=tmp[1], scalar=1.0, in1=lru_x[:, c, 0:S], op0=ALU.add,
                         op1=ALU.mult), ("lru_in", u))
                dve.wait_ge(act_made, at(act_made, ("lru_t", u)))
                f = unit_tiles(u)[2]
                chain(ts(f, tmp[3], 1.0, None, ALU.add))
                chain(nc.vector.reciprocal(f, f))
                made(tt(f, f, tmp[3], ALU.mult), ("lru_f", u))

            def lru_scan(u):
                d, c = lru_units[u]
                a_, x_, m_ = unit_tiles(u)
                dve.wait_ge(act_made, at(act_made, ("lru_m", u)))
                chain(tt(x_, x_, m_, ALU.mult))
                back_ = slice(None, None, -1 if d else 1)
                made(nc.vector.tensor_tensor_scan(m_[:, back_], a_[:, back_], x_[:, back_], 0.0, ALU.mult,
                                                  ALU.add), ("scan", u))
                if d:
                    f_ = unit_tiles(u - 2)[2]
                    dve.wait_ge(dve_made, at(dve_made, ("scan", u)))
                    chain(tt(m_, m_, f_, ALU.add))
                    made(tt(gelu[c], gelu[c], m_, ALU.mult), ("lru_y", c))

            def weighed(label, gate_label, i, dst):
                src = result2(label)
                dve.wait_ge(act_evacuated, at(act_evacuated, gate_label))
                evacuated(stt(out=dst, in0=gate[:, i % 2, 0:S], scalar=1.0, in1=src, op0=ALU.add, op1=ALU.mult),
                          label)

            for m in range(DC):
                if m == 0:
                    dve.wait_ge(act_evacuated, at(act_evacuated, ("o2", len(items2) - 1)))
                if m:
                    lru_unit(2 * m)
                    lru_unit(2 * m + 1)
                weighed(("ya", m), ("ga", m), m, merged[:, m, :])
                if m == 0:
                    lru_unit(0)
                    lru_unit(1)
                if m % 2 == 1:
                    for u in range(4 * (m // 2), 4 * (m // 2) + 4):
                        lru_scan(u)
            for m in range(DC):
                weighed(("yl", m), ("gl", m), m, gate[:, m % 2, 0:S])
                dve.wait_ge(dve_evacuated, at(dve_evacuated, ("yl", m)))
                made(tt(merged[:, m, :], merged[:, m, :], gate[:, m % 2, 0:S], ALU.add), ("mg2", m))
            for m in range(DC):
                evacuated(stt(out=xr[:, m, :], in0=result2(("out2", m)), scalar=0.5, in1=xr[:, m, :],
                              op0=ALU.mult, op1=ALU.add), ("out2", m))
            inverse2("ss_2", 2)
            for c in range(DC):
                made(stt(out=h2[:, c, :], in0=xr[:, c, :], scalar=vec2[:, V_N2 + c:V_N2 + c + 1], in1=tmp[2],
                         op0=ALU.mult, op1=ALU.mult), ("h3", c))

            def r(at_, *dims):
                x = R[:, at_:at_ + math.prod(dims)]
                return x if len(dims) == 1 else x.rearrange("p (a b) -> p a b", a=dims[0])

            def spread(x, count):
                return x.unsqueeze(2).to_broadcast([P, x.shape[1], count])

            src = result2("logits")[:, 0:80].rearrange("p (i n) -> p i n", i=QT)
            evacuated(tt(logits[:, :, :], src, router_bias[:, :].unsqueeze(1).to_broadcast([P, QT, 20]), ALU.add),
                      "logits")
            dve.wait_ge(dve_evacuated, at(dve_evacuated, "logits"))
            nc.vector.tensor_copy(r(R_L, QT, 4), logits[:, :, 0:GROUPS])
            chain(nc.vector.tensor_copy(r(R_L + 16, QT, 16), logits[:, :, GROUPS:]))
            four = r(R_L, 20, 4)
            shape = [P, 20, 4, 4]
            other, own = four.unsqueeze(2).to_broadcast(shape), four.unsqueeze(3).to_broadcast(shape)
            tie = const[:, K_TIE:K_TIE + 16].rearrange("p (x j) -> p x j", x=4).unsqueeze(1).to_broadcast(shape)
            pa, pb_ = (R[:, x:x + 320].rearrange("p (m x j) -> p m x j", m=20, x=4) for x in (R_A, R_B))
            chain(tt(pb_, other, own, ALU.is_equal))
            chain(tt(pb_, pb_, tie, ALU.mult))
            chain(tt(pa, other, own, ALU.is_gt))
            chain(tt(pa, pa, pb_, ALU.add))
            chain(nc.vector.tensor_reduce(R[:, R_R:R_R + 80], R[:, R_A:R_A + 320].rearrange("p (m j) -> p m j", j=4),
                                          AX.X, ALU.add))
            chain(nc.vector.tensor_reduce(R[:, R_S:R_S + 20], four, AX.X, ALU.max))
            made(tt(r(R_X, 20, 4), four, spread(R[:, R_S:R_S + 20], 4), ALU.subtract), "shifted")
            chain(ts(R[:, R_R:R_R + 16], R[:, R_R:R_R + 16], 0.5, None, ALU.is_lt))
            chain(ts(R[:, R_R + 16:R_R + 80], R[:, R_R + 16:R_R + 80], 1.5, None, ALU.is_lt))
            made(tt(r(R_M, 16, 4), r(R_R + 16, 16, 4), spread(R[:, R_R:R_R + 16], 4), ALU.mult), "chosen")
            dve.wait_ge(act_made, at(act_made, "shares"))
            chain(tt(R[:, R_X + 16:R_X + 80], R[:, R_X + 16:R_X + 80], R[:, R_R + 16:R_R + 80], ALU.mult))
            chain(nc.vector.tensor_reduce(R[:, R_S:R_S + 20], r(R_X, 20, 4), AX.X, ALU.add))
            chain(nc.vector.reciprocal(R[:, R_S:R_S + 20], R[:, R_S:R_S + 20]))
            chain(tt(r(R_S + 4, 4, 4), r(R_S + 4, 4, 4), spread(R[:, R_S:R_S + 4], 4), ALU.mult))
            chain(tt(r(R_W, 16, 4), r(R_X + 16, 16, 4), spread(R[:, R_S + 4:R_S + 20], 4), ALU.mult))
            chain(tt(R[:, R_W:R_W + 64], R[:, R_W:R_W + 64], R[:, R_M:R_M + 64], ALU.mult))
            src = result2("places")
            evacuated(nc.vector.tensor_copy(R[:, R_P:R_P + 80], src[:, 0:80]), "places")
            dve.wait_ge(dve_evacuated, at(dve_evacuated, "places"))
            chain(stt(out=R[:, R_Q:R_Q + 64], in0=R[:, R_P:R_P + 64], scalar=1.0, in1=R[:, R_M:R_M + 64],
                      op0=ALU.add, op1=ALU.mult))
            chain(ts(R[:, R_Q:R_Q + 64], R[:, R_Q:R_Q + 64], -1.0, None, ALU.add))
            places = r(R_Q, QT, 16)

            def pick(dst, place):
                iota = const[:, K_IOTA:K_IOTA + P].unsqueeze(1).to_broadcast([P, QT, P])
                return tt(dst, iota, place.to_broadcast([P, QT, P]), ALU.is_equal)

            dve.wait_ge(psum_filled, at(psum_filled, ("out2", 0)))
            for e in range(EXPERTS):
                if e >= 2:
                    dve.wait_ge(picked, at(picked, ("pick", e - 2)))
                made(pick(picks[e % 2], places[:, :, e:e + 1]), ("pick", e))
            nc.vector.memset(R[:, R_A:R_A + 17], 0.0)
            evacuated(nc.vector.tensor_copy(R[:, R_B:R_B + 16], result2("rows_of")[:, 0:16]), "rows_of")
            dve.wait_ge(dve_evacuated, at(dve_evacuated, "rows_of"))
            chain(nc.vector.tensor_copy(rows_of[:, 0:EXPERTS], R[:, R_B:R_B + 16]))
            made(nc.vector.tensor_copy(rows_of[:, EXPERTS:], R[:, R_A:R_A + 1]), "rows_of")
            dve.wait_ge(dve_made, at(dve_made, "rows_of"))
            counts = R[:, R_P + 64:R_P + 80].unsqueeze(1).to_broadcast([P, 3, 16])
            edges = const[:, K_OT:K_OT + 48].rearrange("p (t e) -> p t e", t=3)
            chain(tt(r(R_A, 3, 16), counts, edges, ALU.is_gt))
            flags = R[:, R_A:R_A + 48]
            chain(nc.vector.tensor_tensor_scan(R[:, R_A + 48:R_A + 96], const[:, K_ONES:K_ONES + 48], flags, 0.0,
                                               ALU.mult, ALU.add))
            shape = [P, OVER, 48]
            lst, lst2 = r(R_V, OVER, 48), r(R_V + OVER * 48, OVER, 48)
            chain(tt(lst, R[:, R_A + 48:R_A + 96].unsqueeze(1).to_broadcast(shape),
                     spread(const[:, K_NTH:K_NTH + OVER], 48), ALU.is_equal))
            chain(tt(lst, lst, flags.unsqueeze(1).to_broadcast(shape), ALU.mult))
            chain(tt(lst2, lst, const[:, K_OT:K_OT + 48].unsqueeze(1).to_broadcast(shape), ALU.mult))
            chain(nc.vector.tensor_reduce(over_t[:, :], lst2, AX.X, ALU.add))
            chain(tt(lst, lst, const[:, K_OE:K_OE + 48].unsqueeze(1).to_broadcast(shape), ALU.mult))
            chain(nc.vector.tensor_reduce(R[:, R_B + 1:R_B + 1 + OVER], lst, AX.X, ALU.add))
            chain(nc.vector.tensor_copy(R[:, R_B:R_B + 1], R[:, R_A + 95:R_A + 96]))
            made(nc.vector.tensor_copy(over_i[:, :], R[:, R_B:R_B + 1 + OVER]), "over")

            first = const[:, K_FIRST:K_FIRST + 16].unsqueeze(1).to_broadcast([P, QT, 16])
            chain(tt(r(R_V, QT, 16), r(R_P, QT, 16), first, ALU.add))
            base = R[:, R_A + 48:R_A + 96]
            step = R[:, R_A + 96:R_A + 144]
            chain(ts(base, base, float(P), float((EXPERTS - 1) * P + 1), ALU.mult, ALU.add))
            chain(tt(base, base, const[:, K_OT:K_OT + 48], ALU.subtract))
            chain(tt(step[:, 16:48], base[:, 16:48], base[:, 0:32], ALU.subtract))
            chain(tt(step[:, 0:16], base[:, 0:16], const[:, K_FIRST:K_FIRST + 16], ALU.subtract))
            for t in range(3):
                beyond = r(R_A + 144, QT, 16)
                chain(ts(beyond, r(R_P, QT, 16), float(P * (t + 1)), None, ALU.is_ge))
                chain(tt(beyond, beyond, step[:, 16 * t:16 * t + 16].unsqueeze(1).to_broadcast([P, QT, 16]),
                         ALU.mult))
                chain(tt(r(R_V, QT, 16), r(R_V, QT, 16), beyond, ALU.add))
            chain(tt(R[:, R_V:R_V + 64], R[:, R_V:R_V + 64], R[:, R_M:R_M + 64], ALU.mult))
            chain(nc.vector.tensor_reduce(R[:, R_S:R_S + 4], r(R_V, QT, 16), AX.X, ALU.max))
            chain(nc.vector.tensor_reduce(R[:, R_S + 4:R_S + 8], r(R_V, QT, 16), AX.X, ALU.add))
            chain(tt(r(R_A, QT, 16), r(R_V, QT, 16), spread(R[:, R_S:R_S + 4], 16), ALU.is_equal))
            chain(tt(R[:, R_A:R_A + 64], R[:, R_A:R_A + 64], R[:, R_W:R_W + 64], ALU.mult))
            chain(nc.vector.tensor_reduce(R[:, R_WT:R_WT + 4], r(R_A, QT, 16), AX.X, ALU.add))
            chain(tt(R[:, R_A:R_A + 64], R[:, R_W:R_W + 64], R[:, R_A:R_A + 64], ALU.subtract))
            chain(nc.vector.tensor_reduce(R[:, R_WT + 4:R_WT + 8], r(R_A, QT, 16), AX.X, ALU.add))
            chain(tt(R[:, R_S + 4:R_S + 8], R[:, R_S + 4:R_S + 8], R[:, R_S:R_S + 4], ALU.subtract))
            chain(ts(R[:, R_S:R_S + 8], R[:, R_S:R_S + 8], -1.0, None, ALU.add))
            made(nc.vector.tensor_copy(back_rows[:, :], R[:, R_S:R_S + 8]), "back_rows")
            def hidden(tag):
                dve.wait_ge(psum_filled, at(psum_filled, ("u", tag)))
                dve.wait_ge(act_evacuated, at(act_evacuated, ("g", tag)))
                evacuated(tt(hid, hid, acc[:, 0, 1, :], ALU.mult), ("u", tag))

            def hidden_turned(tag):
                dve.wait_ge(psum_filled, at(psum_filled, ("ht", tag)))
                evacuated(nc.vector.tensor_copy(hid_t, acc[:, 3, 0, :].rearrange("p (k s) -> p k s", s=P)),
                          ("ht", tag))

            hidden("first")
            with dve.Fori(0, EXPERTS - 1) as e:
                n.enter("experts", e, EXPERTS - 1)
                hidden_turned("")
                hidden("")
                n.leave()
            hidden_turned("last")
            dve.wait_ge(dve_made, at(dve_made, "over"))
            tiles = dve.value_load(over_i[0:1, 0:1], min_val=0, max_val=OVER)
            with dve.If(tiles > 0):
                with dve.Fori(0, tiles) as k:
                    n.enter("over", k, 1)
                    expert = dve.value_load(over_i[0:1, bass.ds(k + 1, 1)], min_val=0, max_val=EXPERTS - 1)
                    mine = R[:, R_A:R_A + 4]
                    chain(nc.vector.tensor_copy(mine.unsqueeze(2), places[:, :, bass.ds(expert, 1)]))
                    chain(ts(mine, mine, over_t[:, bass.ds(k, 1)], None, ALU.subtract))
                    made(pick(picks[0], mine.unsqueeze(2)), ("pick", "+"))
                    dve.wait_ge(psum_filled, at(psum_filled, ("pick", "+")))
                    made(nc.vector.tensor_copy(rows_of[:, 0:1], acc[:, 3, 1, 0:1]), ("rows_of", "+"))
                    hidden("+")
                    hidden_turned("+")
                    n.leave()
            for i in range(QT):
                dve.wait_ge(rows_back[i], 32)
                for j in range(2):
                    ins = stt(out=x_tok[:, i, :], in0=returned[:, 2 * i + j, :],
                              scalar=R[:, R_WT + 4 * j + i:R_WT + 4 * j + i + 1], in1=x_tok[:, i, :],
                              op0=ALU.mult, op1=ALU.add)
                    if j == 0:
                        ins.then_inc(summed, 1)
                        dve.wait_ge(summed, i + 1)
                ins.then_inc(combined, 1)

        @block.gpsimd
        def _(pool):
            nc.gpsimd.memset(vrows2, 0.0).then_inc(pool_step, 1)
            mark(pool_step)
            nc.gpsimd.memset(vrows, 0.0).then_inc(pool_made, 1)
            mark(pool_made, "vrows")
            nc.gpsimd.memset(ones[:, :], 1.0).then_inc(pool_made, 1)
            mark(pool_made, "ones")

            def chain(ins):
                ins.then_inc(pool_step, 1)
                mark(pool_step)
                pool.wait_ge(pool_step, now(pool_step))

            with pool.Fori(0, LAYERS) as layer:
                n.enter("layer", layer, LAYERS)
                for g in range(PG):
                    pool.wait_ge(dve_evacuated, at(dve_evacuated, ("u", g)))
                    if g >= 2:
                        pool.wait_ge(dve_made, at(dve_made, ("mixed", g - 1)))
                    src = upad[:, g, :]
                    bufs = [winA, winB] if g % 2 == 0 else [winB, winA]
                    lo = 0
                    order = [bufs[(g - j) % 2] for j in range(g + 1)]
                    for j, dst in enumerate(order):
                        sh = 2 ** j
                        lo += sh
                        if g == 1 and j == 0:
                            pool.wait_ge(dve_made, at(dve_made, ("mixed", 0)))
                        ins = nc.gpsimd.tensor_tensor(dst[:, lo:], src[:, lo:], src[:, lo - sh:PAD + T - sh], ALU.add)
                        src = dst
                        if j < g:
                            chain(ins)
                    ins.then_inc(pool_made, 1)
                    mark(pool_made, ("window", g))
                pool.wait_ge(dve_made, at(dve_made, ("mixed", PG - 1)))
                pool.sem_inc(held, 1)
                for hd in range(HEADS):
                    nc.gpsimd.tensor_copy(kT[NOPE:QK, hd, :], krope[NOPE:QK, 0, :]).then_inc(pool_made, 1)
                    mark(pool_made, ("krep", hd))
                n.leave()
            for c in range(DC):
                pool.wait_ge(dve_made, at(dve_made, ("conv", c)))
                nc.gpsimd.tensor_copy(lru_x[:, c, 0:S], tmp[2 + c % 2]).then_inc(pool_made, 1)
                mark(pool_made, ("conv", c))
            def gather(label, column):
                nc.gpsimd.indirect_dma_start(x_gath, None, h_rows,
                                             bass.IndirectOffsetOnAxis(column, 0)).then_inc(x_gathered, 16)
                mark(x_gathered, label, 16)

            pool.wait_ge(dve_made, at(dve_made, ("lru_y", DC - 1)))
            chain(nc.gpsimd.memset(padf[:, 0:D], 0.0))
            for k in range(OVER):
                pool.dma_start(y_rows[(EXPERTS + k) * P:(EXPERTS + k + 1) * P, :], padf[:, 0:D])\
                    .then_inc(y_zeroed, 16)
            pool.wait_ge(h_stored, 16 * QT)
            pool.wait_ge(dve_made, at(dve_made, "rows_of"))
            gather("x0", rows_of[:, 0:1])
            with pool.Fori(0, EXPERTS) as e:
                n.enter("gathers", e, EXPERTS)
                pool.wait_ge(turned_x, e + 1)
                pool.sem_inc(held, 1)
                nc.gpsimd.tensor_copy(column[:, :], rows_of[:, bass.ds(e + 1, 1)]).then_inc(pool_step, 1)
                mark(pool_step)
                pool.wait_ge(pool_step, now(pool_step))
                pool.sem_inc(held, 1)
                gather(("x", ""), column[:, :])
                n.leave()
            pool.wait_ge(dve_made, at(dve_made, "over"))
            tiles = pool.value_load(over_i[0:1, 0:1], min_val=0, max_val=OVER)
            with pool.If(tiles > 0):
                with pool.Fori(0, tiles) as k:
                    n.enter("over", k, 1)
                    pool.wait_ge(dve_made, at(dve_made, ("rows_of", "+")))
                    pool.sem_inc(held, 1)
                    gather(("x", "+"), rows_of[:, 0:1])
                    n.leave()
            pool.wait_ge(dve_made, at(dve_made, "back_rows"))
            pool.wait_ge(all_stored, 1)
            for i in range(QT):
                for j in range(2):
                    nc.gpsimd.indirect_dma_start(returned[:, 2 * i + j, :], None, y_rows,
                                                 bass.IndirectOffsetOnAxis(back_rows[:, 4 * j + i:4 * j + i + 1], 0))\
                        .then_inc(rows_back[i], 16)
    return n


_IN = ("x", "positions", "meta_tokens", "norm_gain", "w_in", "pool_w_group", "pool_scale", "pool_w_up",
       "q_a_norm_gain", "kv_a_norm_gain", "w_q_b", "w_kv_b", "q_norm_gain", "k_norm_gain", "mla_w_up", "w_out",
       "norm1_gain_2", "w_in_2", "b_gates_2", "q_norm_gain_2", "k_norm_gain_2", "lambda_q1_2", "lambda_k1_2",
       "lambda_q2_2", "lambda_k2_2", "attn_subln_gain_2", "w_attn_o_2", "conv_w_2", "conv_b_2", "lru_wa_2",
       "lru_ba_2", "lru_wi_2", "lru_bi_2", "lru_lambda_2", "w_lru_o_2", "w_out_2", "norm2_gain_2",
       "w_group_router_2", "b_group_router_2", "w_expert_router_2", "b_expert_router_2", "w_expert_gate_2",
       "w_expert_up_2", "w_expert_down_2")


def build(nc, shapes, known):
    a = {name: nc.dram_tensor("in_" + name, shape, dt, kind="ExternalInput").ap()
         for name, (shape, dt) in shapes.items()}
    out = nc.dram_tensor("out", (1, SEQ, D), F32, kind="ExternalOutput").ap()
    return program(nc, a, out, known)


def kernel(**inputs):
    import concourse.bacc as _bacc
    from concourse.bass_utils import run_bass_kernel_spmd as _run

    arrays = {name: np.ascontiguousarray(inputs[name]) for name in _IN}
    arrays["const"] = constants()
    arrays["rotary"] = rotary_table()
    shapes = {name: (x.shape, mybir.dt.from_np(x.dtype)) for name, x in arrays.items()}
    known = build(_bacc.Bacc("TRN2", target_bir_lowering=False, num_devices=1), shapes, None)
    nc = _bacc.Bacc("TRN2", target_bir_lowering=False, num_devices=1)
    build(nc, shapes, known)
    result = _run(nc, [{"in_" + name: x for name, x in arrays.items()}], core_ids=[0])
    return result.results[0]["out"]
```
